# Optimizing a Trainium2 kernel written in Bass

```python
import jax, jax.numpy as jnp
from jax import lax
import numpy as np

D_MODEL = 1024
BATCH = 1
SEQ = 256
DEPTH = 2

HEAD_DIM = 64
BLOCK = 128
N_MEM = 256
BRANCH_WIDTH = 256
N_BRANCH = 4
POOL_WINDOWS = (2, 4, 8, 16)
POOL_GROUPS = 4
POOL_GDIM = BRANCH_WIDTH // POOL_GROUPS
DSA_HEADS = 4
DSA_LATENT = 128
IDX_HEADS = 8
IDX_DIM = 32
DSA_TOPK_MAX = 256
SB_HEADS = 4
SWA_HEADS = 4
SWA_KV_HEADS = 2
SWA_WINDOW = 128
MEM_HEADS = 4
D_FF = ((8 * D_MODEL // 3 + 255) // 256) * 256
RMS_EPS = 1e-6

SPLIT_SIZES = (
    BRANCH_WIDTH,
    DSA_HEADS * HEAD_DIM,
    DSA_LATENT,
    IDX_HEADS * IDX_DIM,
    IDX_DIM,
    IDX_HEADS,
    SB_HEADS * HEAD_DIM,
    SB_HEADS * HEAD_DIM,
    SB_HEADS * HEAD_DIM,
    SWA_HEADS * HEAD_DIM,
    SWA_KV_HEADS * HEAD_DIM,
    SWA_KV_HEADS * HEAD_DIM,
    N_BRANCH * D_MODEL,
)
D_IN = sum(SPLIT_SIZES)

kernel_name = "hybrid_gated_pool_dsa_stickbreak_swa"

def _split_points():
    pts, acc = [], 0
    for s in SPLIT_SIZES[:-1]:
        acc += s
        pts.append(acc)
    return pts

def rmsnorm(x, g):
    x32 = x.astype(jnp.float32)
    y = x32 * lax.rsqrt(jnp.mean(x32 * x32, axis=-1, keepdims=True) + RMS_EPS)
    return (y * g).astype(x.dtype)

def swiglu(h, w_up, w_down):
    gate, up = jnp.split(h @ w_up, 2, axis=-1)
    return (jax.nn.silu(gate) * up) @ w_down

def _blocks(a, nb):
    return a.reshape(a.shape[0], nb, BLOCK, *a.shape[2:]).swapaxes(0, 1)

def _unblocks(a):
    a = a.swapaxes(0, 1)
    return a.reshape(a.shape[0], a.shape[1] * a.shape[2], *a.shape[3:])

def _trailing_mean_minus_self(u, w):
    S = u.shape[1]
    c = jnp.cumsum(u, axis=1)
    c_prev = jnp.pad(c, ((0, 0), (w, 0), (0, 0)))[:, :S]
    cnt = jnp.minimum(jnp.arange(1, S + 1), w).astype(u.dtype)[None, :, None]
    return (c - c_prev) / cnt - u

def pool_mixer(u, pool_w, pool_scale):
    B, S, _ = u.shape
    ug = u.astype(jnp.float32).reshape(B, S, POOL_GROUPS, POOL_GDIM)
    pooled = jnp.stack([_trailing_mean_minus_self(ug[:, :, g], w)
                        for g, w in enumerate(POOL_WINDOWS)], axis=2)
    mixed = jnp.einsum('bsgc,gcd->bsgd', pooled.astype(u.dtype), pool_w)
    return mixed.reshape(B, S, BRANCH_WIDTH) * pool_scale

def dsa_mixer(q, c_kv, idx_q, idx_k, idx_w, kv_norm, w_uk, w_uv):
    B, S = q.shape[:2]
    nb = S // BLOCK
    topk = min(DSA_TOPK_MAX, S // 4)
    c = rmsnorm(c_kv, kv_norm)
    q_lat = jnp.einsum('bshd,rhd->bshr', q, w_uk)
    ik = idx_k.astype(jnp.float32)
    key_pos = jnp.arange(S)

    def one_block(args):
        n, qb, iqb, iwb = args
        qpos = n * BLOCK + jnp.arange(BLOCK)
        causal = key_pos[None, :] <= qpos[:, None]
        logits = jnp.einsum('bqhd,bsd->bqhs', iqb.astype(jnp.float32), ik) * IDX_DIM ** -0.5
        score = jnp.einsum('bqh,bqhs->bqs', iwb.astype(jnp.float32), jax.nn.relu(logits))
        score = jnp.where(causal[None], score, -jnp.inf)
        _, idx = lax.top_k(score, topk)
        valid = idx <= qpos[None, :, None]
        c_sel = jax.vmap(lambda cb, ib: cb[ib])(c, idx)
        s = jnp.einsum('bqhr,bqkr->bqhk', qb.astype(jnp.float32),
                       c_sel.astype(jnp.float32)) * HEAD_DIM ** -0.5
        s = jnp.where(valid[:, :, None, :], s, -jnp.inf)
        p = jax.nn.softmax(s, axis=-1)
        return jnp.einsum('bqhk,bqkr->bqhr', p.astype(c.dtype), c_sel)

    o_lat = lax.map(one_block, (jnp.arange(nb), _blocks(q_lat, nb),
                                _blocks(idx_q, nb), _blocks(idx_w, nb)))
    o = jnp.einsum('bshr,rhd->bshd', _unblocks(o_lat), w_uv)
    return o.reshape(B, S, DSA_HEADS * HEAD_DIM)

def stick_breaking_mixer(q, k, v):
    B, S, H, dh = q.shape
    nb = S // BLOCK
    kf = k.astype(jnp.float32)
    key_pos = jnp.arange(S)

    def one_block(args):
        n, qb = args
        qpos = n * BLOCK + jnp.arange(BLOCK)
        strict = (key_pos[None, :] < qpos[:, None])[None, None]
        z = jnp.einsum('bqhd,bshd->bhqs', qb.astype(jnp.float32), kf) * dh ** -0.5
        log_1m_beta = jnp.where(strict, jax.nn.log_sigmoid(-z), 0.0)
        between = lax.cumsum(log_1m_beta, axis=3, reverse=True) - log_1m_beta
        a = jnp.where(strict, jnp.exp(jax.nn.log_sigmoid(z) + between), 0.0)
        return jnp.einsum('bhqs,bshd->bqhd', a.astype(v.dtype), v)

    o = lax.map(one_block, (jnp.arange(nb), _blocks(q, nb)))
    return _unblocks(o).reshape(B, S, H * dh)

def swa_sink_mixer(q, k, v, sinks):
    B, S, HQ, dh = q.shape
    HKV = k.shape[2]
    G = HQ // HKV
    nb = S // BLOCK
    qb = q.reshape(B, nb, BLOCK, HKV, G, dh)

    def band(a):
        ab = a.reshape(B, nb, BLOCK, HKV, dh)
        prev = jnp.pad(ab, ((0, 0), (1, 0), (0, 0), (0, 0), (0, 0)))[:, :nb]
        return jnp.concatenate([prev, ab], axis=2)

    kb, vb = band(k), band(v)
    s = jnp.einsum('bnqkgd,bnjkd->bnkgqj', qb.astype(jnp.float32),
                   kb.astype(jnp.float32)) * dh ** -0.5
    kj = jnp.arange(2 * BLOCK)[None, :]
    rel = (jnp.arange(BLOCK)[:, None] + BLOCK) - kj
    in_window = (rel >= 0) & (rel < SWA_WINDOW)
    key_ok = (jnp.arange(nb)[:, None] * BLOCK - BLOCK + kj) >= 0
    mask = in_window[None] & key_ok[:, None, :]
    s = jnp.where(mask[None, :, None, None], s, -jnp.inf)
    sink = jnp.broadcast_to(sinks.astype(jnp.float32).reshape(HKV, G)[None, None, :, :, None, None],
                            s.shape[:-1] + (1,))
    p = jax.nn.softmax(jnp.concatenate([s, sink], axis=-1), axis=-1)[..., :-1]
    o = jnp.einsum('bnkgqj,bnjkd->bnqkgd', p.astype(v.dtype), vb)
    return o.reshape(B, S, HQ * dh)

def hybrid_mixer(h, w_in, pool_w, pool_scale, dsa_kv_norm, dsa_w_uk, dsa_w_uv,
                 swa_sinks, w_branch, w_out):
    B, S, _ = h.shape
    (u_pool, dsa_q, dsa_ckv, idx_q, idx_k, idx_w, sb_q, sb_k, sb_v,
     swa_q, swa_k, swa_v, gate_logits) = jnp.split(h @ w_in, _split_points(), axis=-1)
    o_a = pool_mixer(u_pool, pool_w, pool_scale)
    o_b = dsa_mixer(dsa_q.reshape(B, S, DSA_HEADS, HEAD_DIM), dsa_ckv,
                    idx_q.reshape(B, S, IDX_HEADS, IDX_DIM), idx_k,
                    idx_w * IDX_HEADS ** -0.5, dsa_kv_norm, dsa_w_uk, dsa_w_uv)
    o_c = stick_breaking_mixer(sb_q.reshape(B, S, SB_HEADS, HEAD_DIM),
                               sb_k.reshape(B, S, SB_HEADS, HEAD_DIM),
                               sb_v.reshape(B, S, SB_HEADS, HEAD_DIM))
    o_d = swa_sink_mixer(swa_q.reshape(B, S, SWA_HEADS, HEAD_DIM),
                         swa_k.reshape(B, S, SWA_KV_HEADS, HEAD_DIM),
                         swa_v.reshape(B, S, SWA_KV_HEADS, HEAD_DIM), swa_sinks)
    branches = jnp.stack([o_a, o_b, o_c, o_d], axis=2)
    y = jnp.einsum('bsic,icd->bsid', branches, w_branch)
    gates = jax.nn.sigmoid(gate_logits.reshape(B, S, N_BRANCH, D_MODEL))
    merged = jnp.sum(gates * y, axis=2)
    return merged @ w_out

def memory_cross_attention(h, mem_n, w_q, w_kv, w_o):
    B, S, _ = h.shape
    M = mem_n.shape[1]
    q = (h @ w_q).reshape(B, S, MEM_HEADS, HEAD_DIM)
    k, v = jnp.split(mem_n @ w_kv, 2, axis=-1)
    k = k.reshape(B, M, MEM_HEADS, HEAD_DIM)
    v = v.reshape(B, M, MEM_HEADS, HEAD_DIM)
    s = jnp.einsum('bshd,bmhd->bhsm', q.astype(jnp.float32), k.astype(jnp.float32)) * HEAD_DIM ** -0.5
    p = jax.nn.softmax(s, axis=-1)
    o = jnp.einsum('bhsm,bmhd->bshd', p.astype(v.dtype), v)
    return o.reshape(B, S, MEM_HEADS * HEAD_DIM) @ w_o

def setup_inputs(seed: int = 0) -> dict:
    key = jax.random.key(seed)
    ks = iter(jax.random.split(key, 40))

    def nrm(shape, scale):
        return jax.random.normal(next(ks), shape, jnp.float32) * scale

    def gain(shape):
        return 1.0 + nrm(shape, 0.05)

    L, D, F = DEPTH, D_MODEL, D_FF
    return {
        "x": nrm((BATCH, SEQ, D), 1.0),
        "mem": nrm((BATCH, N_MEM, D), 1.0),
        "ffn1_pre": gain((L, D)),
        "ffn1_w_up": nrm((L, D, 2 * F), D ** -0.5),
        "ffn1_w_down": nrm((L, F, D), F ** -0.5),
        "ffn1_post": gain((L, D)),
        "mix_pre": gain((L, D)),
        "w_in": nrm((L, D, D_IN), D ** -0.5),
        "pool_w": nrm((L, POOL_GROUPS, POOL_GDIM, POOL_GDIM), POOL_GDIM ** -0.5),
        "pool_scale": 1.0 + nrm((L, BRANCH_WIDTH), 0.1),
        "dsa_kv_norm": gain((L, DSA_LATENT)),
        "dsa_w_uk": nrm((L, DSA_LATENT, DSA_HEADS, HEAD_DIM), HEAD_DIM ** -0.5),
        "dsa_w_uv": nrm((L, DSA_LATENT, DSA_HEADS, HEAD_DIM), DSA_LATENT ** -0.5),
        "swa_sinks": nrm((L, SWA_HEADS), 0.5),
        "w_branch": nrm((L, N_BRANCH, BRANCH_WIDTH, D), BRANCH_WIDTH ** -0.5),
        "w_out": nrm((L, D, D), D ** -0.5),
        "mix_post": gain((L, D)),
        "xattn_pre": gain((L, D)),
        "mem_norm": gain((L, D)),
        "xattn_w_q": nrm((L, D, MEM_HEADS * HEAD_DIM), D ** -0.5),
        "xattn_w_kv": nrm((L, D, 2 * MEM_HEADS * HEAD_DIM), D ** -0.5),
        "xattn_w_o": nrm((L, MEM_HEADS * HEAD_DIM, D), (MEM_HEADS * HEAD_DIM) ** -0.5),
        "xattn_post": gain((L, D)),
        "ffn2_pre": gain((L, D)),
        "ffn2_w_up": nrm((L, D, 2 * F), D ** -0.5),
        "ffn2_w_down": nrm((L, F, D), F ** -0.5),
        "ffn2_post": gain((L, D)),
    }

def reference(x, mem, ffn1_pre, ffn1_w_up, ffn1_w_down, ffn1_post,
              mix_pre, w_in, pool_w, pool_scale, dsa_kv_norm, dsa_w_uk, dsa_w_uv,
              swa_sinks, w_branch, w_out, mix_post,
              xattn_pre, mem_norm, xattn_w_q, xattn_w_kv, xattn_w_o, xattn_post,
              ffn2_pre, ffn2_w_up, ffn2_w_down, ffn2_post):
    for l in range(DEPTH):
        x = x + 0.5 * rmsnorm(swiglu(rmsnorm(x, ffn1_pre[l]), ffn1_w_up[l], ffn1_w_down[l]),
                              ffn1_post[l])
        m = hybrid_mixer(rmsnorm(x, mix_pre[l]), w_in[l], pool_w[l], pool_scale[l],
                         dsa_kv_norm[l], dsa_w_uk[l], dsa_w_uv[l], swa_sinks[l],
                         w_branch[l], w_out[l])
        x = x + rmsnorm(m, mix_post[l])
        c = memory_cross_attention(rmsnorm(x, xattn_pre[l]), rmsnorm(mem, mem_norm[l]),
                                   xattn_w_q[l], xattn_w_kv[l], xattn_w_o[l])
        x = x + rmsnorm(c, xattn_post[l])
        x = x + 0.5 * rmsnorm(swiglu(rmsnorm(x, ffn2_pre[l]), ffn2_w_up[l], ffn2_w_down[l]),
                              ffn2_post[l])
    return x


_drawn_inputs = setup_inputs


def setup_inputs(seed=0):
    import zlib

    import numpy as np

    out = dict(_drawn_inputs(seed))
    spreads = {}
    factors = {'swa_sinks': 8.0, 'ffn2_post': 2.792}
    for name, (base, spread) in spreads.items():
        noise = np.random.default_rng([zlib.crc32(name.encode()), seed]).standard_normal(out[name].shape)
        drawn = base * np.exp(spread * noise) if base else spread * noise
        out[name] = __import__('jax').numpy.asarray(drawn.astype(out[name].dtype))
    for name, factor in factors.items():
        out[name] = (out[name] * factor).astype(out[name].dtype)
    return out
```

```python
from contextlib import ExitStack

import concourse.bass as bass
from concourse import mybir
import numpy as np

P = 128
F32 = mybir.dt.float32
F32R = mybir.dt.float32r
ALU = mybir.AluOpType
ACT = mybir.ActivationFunctionType
AX = mybir.AxisListType.X

DEPTH = 2
TOK = 256
NB = TOK // P
D = 1024
KC = D // P
F = 2816
FG = 256
NG = F // FG
FC = F // P
BW = 256
EPS = 1e-6
NEG = -1e30
TAKEN = -3e38
TOPK = 64
WINDOWS = (2, 4, 8, 16)

H_FFN1 = 0
H_MIX = H_FFN1 + 4 * NG + FC
MIX_COLS = ((0, 512), (512, 424), (936, 512), (1448, 512), (1960, 256)) + tuple(
    (2216 + 512 * g, 512) for g in range(8))
NMG = len(MIX_COLS)
M_BRANCH = 4 * NMG
M_OUT = M_BRANCH + 8
H_X = H_MIX + M_OUT + 8
H_FFN2 = H_X + 8
NH = H_FFN2 + 4 * NG + FC
NU = NH // 2
RAW = 4
SPL = 4
AHEAD = 3
assert NU % RAW == 0 and NH % SPL == 0

HALF = [1024] * NH
for _g, (_c, _n) in enumerate(MIX_COLS):
    for _i in range(4):
        HALF[H_MIX + 4 * _g + _i] = 2 * _n

RQ = {n: i for i, n in enumerate([
    "pre0_0", "pre0_1", "post0_0", "post0_1", "pre1_0", "pre1_1", "c_0", "c_1", "post1_0", "post1_1",
    "mem_0", "mem_1", "pre2_0", "pre2_1", "post2_0", "post2_1", "pre3_0", "pre3_1", "post3_0", "post3_1"])}
NRQ = len(RQ)

AT_T = {0: 5, 1: 9, 2: 9, 3: 10, 4: 14, 5: 14, 6: 19, 7: 21}
AT_POOLED, AT_POOLMIX = 6, 7
AT_DKV = 11
AT_IDX = (12, 15)
AT_SB = (22, 25, 27)
AT_ATT = (29, 33, 37, 41)
AT_MERGE = tuple(M_BRANCH + 2 + 2 * i for i in range(4))
AT_MEM = M_OUT + 5

C_ID, C_TRI, C_ONES, C_STRICT, C_CAUS, C_WIN, C_BAND, C_SC = 0, 128, 256, 384, 512, 640, 768, 768 + 12 * 128
N_CONST = C_SC + 8
K_INVD, K_INVC, K_INVD4, K_EPS, K_EPS4, K_POW = range(6)


def constants():
    c = np.zeros((P, N_CONST), np.float32)
    i, j = np.arange(P)[:, None], np.arange(P)[None, :]
    c[:, C_ID:C_ID + P] = i == j
    c[:, C_TRI:C_TRI + P] = -(i >= j).astype(np.float32)
    c[:, C_ONES:C_ONES + P] = -1.0
    c[:, C_STRICT:C_STRICT + P] = i < j
    c[:, C_CAUS:C_CAUS + P] = np.where(j <= i, 0.0, NEG)
    c[:, C_WIN:C_WIN + P] = np.where(j > i, 0.0, NEG)
    for g, w in enumerate(WINDOWS):
        for part, (si, ti) in enumerate(((0, 0), (0, P), (P, P))):
            s, t = i + si, j + ti
            band = ((s <= t) & (s > t - w)) / np.minimum(t + 1, w) - (s == t)
            at = C_BAND + (3 * g + part) * P
            c[:, at:at + P] = band
    for k, v in ((K_INVD, 1 / D), (K_INVC, 1 / P), (K_INVD4, 4 / D), (K_EPS, EPS), (K_EPS4, 4 * EPS), (K_POW, -0.5)):
        c[:, C_SC + k] = v
    return c


def trunk(nc, a, out):
    with ExitStack() as ctx:
        sem = lambda n: ctx.enter_context(nc.semaphore(n))
        base = (nc.sbuf_base + 63) // 64 * 64
        place = {}

        def put(name, shape, dt, at=None):
            size = 4 * int(np.prod(shape))
            at = place.get("end", base) if at is None else at
            place["end"] = max(place.get("end", base), at + (size + 63) // 64 * 64)
            assert place["end"] <= nc.sbuf_usable_end, (name, place["end"])
            place[name] = at
            return nc.alloc_sbuf_tensor_at(name, [P, *shape], dt, offset=at)

        raw = put("raw", (RAW, 2048), F32)
        wh = put("wh", (SPL, 1024), F32R)
        wl = put("wl", (SPL, 1024), F32R)
        x = put("x", (NB, D), F32)
        xh = put("xh", (KC, TOK), F32R)
        xl = put("xl", (KC, TOK), F32R)
        ah = put("ah", (FC, TOK), F32R)
        al = put("al", (FC, TOK), F32R)
        A = place["ah"]
        gates = put("gates", (4, NB, D), F32, A)
        brh = put("brh", (4, 2, TOK), F32R, A + 32768)
        brl = put("brl", (4, 2, TOK), F32R, A + 32768 + 8192)
        memn = put("memn", (NB, D), F32, A)
        memh = put("memh", (KC, TOK), F32R, A + 8192)
        meml = put("meml", (KC, TOK), F32R, A + 16384)
        yg = put("yg", (NB, D), F32)
        tmp = put("tmp", (D,), F32)
        W = place["yg"]
        merged = put("merged", (NB, D), F32, W)
        sb_sp = put("sb_sp", (1536,), F32, W)
        sb_a = put("sb_a", (1536,), F32, W + 6144)
        relu = put("relu", (8, TOK), F32, W)
        nat = put("nat", (2, NB, 512), F32)
        sg = put("sg", (2, NB, FG), F32, place["nat"])
        an = put("an", (2, NB, FG), F32, place["nat"] + 4096)
        sc = put("sc", (4, TOK), F32)
        junk = put("junk", (D,), F32, place["sc"])
        pT = put("pT", (4, 2, P), F32)
        cn = put("cn", (NB, P), F32, place["pT"])
        ikr = put("ikr", (NB, 4, 32), F32, place["pT"] + 1024)
        swkr = put("swkr", (NB, 2, P), F32, place["pT"] + 2048)
        u_n = put("u_n", (NB, BW), F32)
        v_sb = put("v_sb", (NB, BW), F32)
        v_sw = put("v_sw", (NB, P), F32)
        v_ds = put("v_ds", (NB, BW), F32)
        dqT = put("dqT", (2, TOK), F32)
        iqT = put("iqT", (2, TOK), F32)
        ikT = put("ikT", (TOK,), F32)
        cT = put("cT", (TOK,), F32)
        dkT = put("dkT", (2, TOK), F32)
        sbqT = put("sbqT", (2, TOK), F32)
        sbkT = put("sbkT", (2, TOK), F32)
        swqT = put("swqT", (2, TOK), F32)
        swkT = put("swkT", (2, TOK), F32)
        xqT, mkT, v_m = dqT, sbkT, v_sb
        poT = put("poT", (2, TOK), F32, place["sbqT"])
        score = put("score", (TOK,), F32)
        dmask = put("dmask", (NB, TOK), F32)
        gbc = put("gbc", (D,), F32)
        cst = put("cst", (N_CONST,), F32)
        gT = put("gT", (5, KC), F32)
        pw = put("pw", (2, 64), F32)
        psc = put("psc", (2,), F32)
        kvn = put("kvn", (1,), F32)
        uk = put("uk", (BW,), F32)
        uv = put("uv", (BW,), F32)
        snk = put("snk", (4,), F32)
        ssq = put("ssq", (NRQ,), F32)
        msq = put("msq", (NRQ,), F32)
        rms = put("rms", (NRQ,), F32)
        hrs = put("hrs", (NB,), F32)
        iw = put("iw", (NB, 8), F32)
        top8 = put("top8", (8,), F32)
        nmx = put("nmx", (4,), F32)
        den = put("den", (4,), F32)
        rcp = put("rcp", (4,), F32)
        carry = put("carry", (1,), F32)
        esk = put("esk", (4,), F32)

        ps = ctx.enter_context(nc.psum_tensor("ps", [P, 8, 512], F32))

        ident = cst[:, C_ID:C_ID + P]
        k_col = lambda k: cst[:, C_SC + k:C_SC + k + 1]

        raw_in = [sem(f"raw_in{r}") for r in range(RAW)]
        hi_done, split_done, half_done = sem("hi_done"), sem("split_done"), sem("half_done")
        params_in, const_in, x_in, gbc_in, mem_in, stored = (
            sem(n) for n in ("params_in", "const_in", "x_in", "gbc_in", "mem_in", "stored"))
        x_new, x_turned, x_hi, x_lo = sem("x_new"), sem("x_turned"), sem("x_hi"), sem("x_lo")
        squared, rms_ready, gained = sem("squared"), sem("rms_ready"), sem("gained")
        silu_done, act_done, act_turned, act_hi, act_lo = (
            sem(n) for n in ("silu_done", "act_done", "act_turned", "act_hi", "act_lo"))
        nat_done, turned, turned_out = sem("nat_done"), sem("turned"), sem("turned_out")
        mix_pe, mix_out, br_hi, br_lo = sem("mix_pe"), sem("mix_out"), sem("br_hi"), sem("br_lo")
        idx_pe, relu_done, sel_done = sem("idx_pe"), sem("relu_done"), sem("sel_done")
        sb_pe, sb_act, sb_dve = sem("sb_pe"), sem("sb_act"), sem("sb_dve")
        att_s, att_max, att_exp, att_p, att_t, att_tev, att_o = (
            sem(f"att_{n}") for n in ("s", "max", "exp", "p", "t", "tev", "o"))
        merge_done, m_turned, m_hi, m_lo = sem("merge_done"), sem("m_turned"), sem("m_hi"), sem("m_lo")
        mem_turned, mem_hi, mem_lo = sem("mem_turned"), sem("mem_hi"), sem("mem_lo")
        dve_link, act_link, pool_link = sem("dve_link"), sem("act_link"), sem("pool_link")
        half_rms = sem("half_rms")

        N_PAR = 12
        N_BR = 8
        BR = {"pool": 0, "sb": 1, "swa0": 2, "swa1": 3, "dsa0": 4, "dsa1": 5, "x0": 6, "x1": 7}
        ATT = (("swa", 0), ("swa", 1), ("dsa", 0), ("dsa", 1), ("x", 0), ("x", 1))
        N_ATT = len(ATT)
        N_ALINK, N_VLINK = 3, 86

        up = {f: a[f"ffn{f}_w_up"].rearrange("l (c p) (t n) -> l p c t n", p=P, t=2) for f in (1, 2)}
        down = {f: a[f"ffn{f}_w_down"].rearrange("l (c p) n -> l p c n", p=P) for f in (1, 2)}
        w_in = a["w_in"].rearrange("l (c p) n -> l p c n", p=P)
        w_br = a["w_branch"].rearrange("l i (c p) n -> l i p c n", p=P)
        w_out = a["w_out"].rearrange("l (c p) n -> l p c n", p=P)
        w_q = a["xattn_w_q"].rearrange("l (c p) n -> l p c n", p=P)
        w_kv = a["xattn_w_kv"].rearrange("l (c p) n -> l p c n", p=P)
        w_o = a["xattn_w_o"].rearrange("l (c p) n -> l p c n", p=P)

        block = ctx.enter_context(nc.Block())

        @block.sync
        def _(sp):
            sp.dma_start(x[:], a["x"].rearrange("o (b p) d -> p (o b) d", p=P)).then_inc(x_in, 16)
            sp.dma_start(cst[:], a["consts"]).then_inc(const_in, 16)

            def load(L, u, srcs, dims, it=0, by=0):
                c, n = dims
                dst = raw[:, u % RAW, 0:c * n].rearrange("p (c n) -> p c n", c=c)
                sp.wait_ge(split_done, L * NH + 2 * u + 2 + it * (2 * RAW))
                for i, src in enumerate(srcs):
                    part = dst[:, :, i * n // 2:(i + 1) * n // 2] if by else dst[:, i * c // 2:(i + 1) * c // 2, :]
                    sp.dma_start(part, src).then_inc(raw_in[u % RAW], 16)

            def chunks(w, k0, kn):
                return w[:, k0:k0 + kn // 2, :], w[:, k0 + kn // 2:k0 + kn, :]

            def load_gain(L, k, name):
                sp.wait_ge(gained, L * 4 + k)
                sp.dma_start(gbc[:], a[name][L].partition_broadcast(P)).then_inc(gbc_in, 16)

            def ffn(L, f, u0, k):
                def group(g, u, it=0):
                    for i in range(2):
                        load(L, u + i, [up[f][L, :, 4 * i:4 * i + 4, t, bass.ts(g, FG)] for t in range(2)], (4, 2 * FG),
                             it, by=1)
                group(0, u0)
                with sp.Fori(0, (NG - 1) // 2) as it:
                    for j in range(2):
                        group(2 * it + 1 + j, u0 + 2 + 2 * j, it)
                load_gain(L, k, f"ffn{f}_post")
                for c in range(FC // 2):
                    load(L, u0 + 2 * NG + c, chunks(down[f][L], 2 * c, 2), (2, D))

            with sp.Fori(0, DEPTH) as L:
                sp.wait_ge(x_lo, L * 16)
                def par(dst, src):
                    sp.dma_start(dst, src).then_inc(params_in, 16)
                with nc.allow_non_contiguous_dma("gains, a value per partition"):
                    for i, n in enumerate(("ffn1_pre", "mix_pre", "xattn_pre", "mem_norm", "ffn2_pre")):
                        par(gT[:, i, :], a[n][L].rearrange("(c p) -> p c", p=P))
                    par(psc[:], a["pool_scale"][L].rearrange("(c p) -> p c", p=P))
                    par(kvn[:], a["dsa_kv_norm"][L].rearrange("(c p) -> p c", p=P))
                for c in range(2):
                    par(pw[:, c, :], a["pool_w"][L, 2 * c:2 * c + 2].rearrange("g c d -> (g c) d"))
                par(uk[:], a["dsa_w_uk"][L].rearrange("r h d -> r (h d)"))
                par(uv[:], a["dsa_w_uv"][L].rearrange("r h d -> r (h d)"))
                par(snk[:], a["swa_sinks"][L].partition_broadcast(P))
                ffn(L, 1, H_FFN1 // 2, 0)
                u = H_MIX // 2
                for g, (c0, n) in enumerate(MIX_COLS):
                    for i in range(2):
                        load(L, u, chunks(w_in[L, :, :, c0:c0 + n], 4 * i, 4), (4, n))
                        u += 1
                    if g == 6:
                        load_gain(L, 1, "mix_post")
                for i in range(4):
                    load(L, u, chunks(w_br[L, i], 0, 2), (2, D))
                    u += 1
                for i in range(4):
                    load(L, u, chunks(w_out[L], 2 * i, 2), (2, D))
                    u += 1
                sp.wait_ge(merge_done, L * 4 + 4)
                sp.dma_start(memn[:], a["mem"].rearrange("o (b p) d -> p (o b) d", p=P)).then_inc(mem_in, 16)
                for i in range(2):
                    load(L, u, chunks(w_kv[L], 4 * i, 4), (4, 512))
                    u += 1
                load(L, u, chunks(w_q[L], 0, KC), (KC, BW))
                load_gain(L, 2, "xattn_post")
                load(L, u + 1, chunks(w_o[L], 0, 2), (2, D))
                ffn(L, 2, H_FFN2 // 2, 3)
            sp.wait_ge(x_new, 2 + 8 * DEPTH)
            sp.dma_start(out.rearrange("o (b p) d -> p (o b) d", p=P), x[:]).then_inc(stored, 16)
            sp.wait_ge(stored, 16)

        @block.gpsimd
        def _(pool):
            pool.wait_ge(const_in, 16)
            with pool.Fori(0, DEPTH) as L:
                for name, q in RQ.items():
                    half = name in ("post0_0", "post0_1", "post3_0", "post3_1")
                    inv = K_INVC if name[0] == "c" else K_INVD4 if half else K_INVD
                    pool.wait_ge(squared, L * NRQ + q + 1)
                    nc.gpsimd.tensor_tensor(msq[:, q:q + 1], ssq[:, q:q + 1], k_col(inv), ALU.mult).then_inc(pool_link, 1)
                    pool.wait_ge(pool_link, L * 2 * NRQ + 2 * q + 1)
                    nc.gpsimd.tensor_tensor(msq[:, q:q + 1], msq[:, q:q + 1], k_col(K_EPS4 if half else K_EPS),
                                            ALU.add).then_inc(pool_link, 1)
                    pool.wait_ge(pool_link, L * 2 * NRQ + 2 * q + 2)
                    nc.gpsimd.tensor_tensor(rms[:, q:q + 1], msq[:, q:q + 1], k_col(K_POW), ALU.pow).then_inc(rms_ready, 1)

        def rs(name):
            return rms[:, RQ[name]:RQ[name] + 1]

        def wide(bank, n=1024, at=0):
            return ps[:].rearrange("p b n -> p (b n)")[:, bank * 512 + at:bank * 512 + at + n]

        @block.tensor
        def _(pe):
            pe.sem_inc(half_done, SPL)
            pe.wait_ge(const_in, 16)
            mm = nc.tensor.matmul

            def turn(dst, src):
                return nc.tensor.transpose(dst, src, ident)

            def mm3(dst, sh, sl, mh, ml, start, stop):
                mm(dst, sh, mh, start=start, stop=False)
                mm(dst, sh, ml, start=False, stop=False)
                return mm(dst, sl, mh, start=False, stop=stop)

            def half(L, h, k0, kn, n, dst, sh, sl, K, it=0):
                pe.wait_ge(split_done, L * NH + h + 1 + 2 * RAW + it * 8)
                q = h % SPL
                for b in range(NB):
                    for k in range(kn):
                        tok = slice(b * P, b * P + P)
                        for c in range(0, n, 512):
                            w = min(512, n - c)
                            mv = slice(k * n + c, k * n + c + w)
                            last = mm3(dst(b, c, w), sh[:, k0 + k, tok], sl[:, k0 + k, tok],
                                       wh[:, q, mv], wl[:, q, mv], k0 + k == 0, k0 + k == K - 1)
                last.then_inc(half_done, 1)

            def turn_x(L, b, bank):
                for blk in range(NB):
                    pe.wait_ge(x_new, L * 8 + 2 * b + blk + 1)
                    for hf in range(2):
                        for c in range(4):
                            k = 4 * hf + c
                            t = turn(ps[:, bank + 2 * blk + hf, c * P:c * P + P], x[:, blk, k * P:k * P + P])
                        t.then_inc(x_turned, 1)

            def ffn(L, f, h0, b):
                E = (L * 2 + f) * NG
                turn_x(L, b, 4 if b == 0 else 0)

                def act_turn(g, it, bank):
                    pe.wait_ge(act_done, E + g + 1 + it * 2)
                    for c in range(2):
                        for blk in range(NB):
                            t = turn(ps[:, bank, c * TOK + blk * P:c * TOK + blk * P + P],
                                     an[:, g % 2, blk, c * P:c * P + P])
                    t.then_inc(act_turned, 1)

                def group(g, it=0):
                    s = 2 * (g % 2)
                    if g == 0:
                        pe.wait_ge(x_lo, L * 16 + b * 4 + 4)
                    if g >= 2 or not isinstance(it, int):
                        pe.wait_ge(act_done, E + g - 1 + it * 2)
                    for i in range(4):
                        half(L, h0 + 4 * g + i, 2 * i, 2, 512, lambda blk, c, w: ps[:, s + blk, :], xh, xl, KC, it)
                        if i == 0 and (g > 0 or not isinstance(it, int)):
                            if g > 2 or not isinstance(it, int):
                                pe.wait_ge(act_lo, E + g - 2 + it * 2)
                            act_turn(g - 1, it, 4 + (g - 1) % 2)
                group(0)
                group(1)
                group(2)
                with pe.Fori(0, (NG - 3) // 2) as it:
                    for j in range(2):
                        s = 2 * ((3 + j) % 2)
                        g = 3 + j
                        pe.wait_ge(act_done, E + g - 1 + it * 2)
                        for i in range(4):
                            half(L, h0 + 4 * g + i, 2 * i, 2, 512, lambda blk, c, w: ps[:, s + blk, :], xh, xl, KC, it)
                            if i == 0:
                                pe.wait_ge(act_lo, E + g - 2 + it * 2)
                                act_turn(g - 1, it, 4 + (g - 1) % 2)
                for c in range(FC):
                    pe.wait_ge(act_lo, E + max(c // 2 + 1, NG - 1))
                    half(L, h0 + 4 * NG + c, c, 1, D, lambda blk, cc, w: ps[:, 4 + 2 * blk + cc // 512, :], ah, al, FC)
                    if c == 0:
                        act_turn(NG - 1, 0, 2)

            def mixer(L):
                h0 = H_MIX
                turn_x(L, 1, 4)

                def t_step(j):
                    src = (nat[:, 0, :, 256:512], nat[:, 1, :, 128:384], ikr, cn, nat[:, 0, :, 0:256],
                           nat[:, 0, :, 256:512], nat[:, 1, :, 256:512], swkr)[j]
                    bank = 4 + j % 2
                    if j >= 2:
                        pe.wait_ge(turned_out, L * 10 + j - 1)
                    for c in range(1 if j in (2, 3) else 2):
                        for blk in range(NB):
                            s = (ikr[:, blk].rearrange("p r d -> p (r d)") if j == 2 else cn[:, blk] if j == 3
                                 else swkr[:, blk, c] if j == 7 else src[:, blk, c * P:c * P + P])
                            t = turn(ps[:, bank, c * TOK + blk * P:c * TOK + blk * P + P], s)
                    t.then_inc(turned, 1)

                def pooled():
                    for g in range(4):
                        o = ps[64 * (g % 2):64 * (g % 2) + 64, 6, (g // 2) * TOK:(g // 2) * TOK + TOK]
                        band = cst[:, C_BAND + 3 * g * P:C_BAND + 3 * g * P + 3 * P]
                        mm(o, u_n[:, 0, 64 * g:64 * g + 64], band[:, 0:TOK], start=True, stop=False, skip_group_check=True)
                        t = mm(o[:, P:TOK], u_n[:, 1, 64 * g:64 * g + 64], band[:, TOK:3 * P], start=False, stop=True,
                               skip_group_check=True)
                    t.then_inc(mix_pe, 1)

                def pool_mix():
                    for g in range(4):
                        r = slice(64 * (g % 2), 64 * (g % 2) + 64)
                        t = mm(ps[r, 7, (g // 2) * TOK:(g // 2) * TOK + TOK], pw[r, g // 2, :], poT[r, g // 2, :],
                               start=True, stop=True, skip_group_check=True)
                    t.then_inc(mix_pe, 1)

                def dsa_kv():
                    pe.wait_ge(turned_out, L * 10 + 4)
                    for c in range(2):
                        mm(ps[:, 4, c * TOK:c * TOK + TOK], uk[:, c * P:c * P + P], cT[:], start=True, stop=True,
                           skip_group_check=True)
                    for blk in range(NB):
                        t = mm(ps[:, 5, blk * BW:blk * BW + BW], cT[:, blk * P:blk * P + P], uv[:], start=True, stop=True,
                               skip_group_check=True)
                    t.then_inc(mix_pe, 1)

                def index(b):
                    if b == 0:
                        pe.wait_ge(mix_out, L * 2 + 2)
                        pe.wait_ge(br_lo, L * N_BR + BR["pool"] + 1)
                    else:
                        pe.wait_ge(relu_done, L * 2 + 1)
                        pe.wait_ge(turned_out, L * 10 + 6)
                    W_ = P * (b + 1)
                    for h in range(8):
                        r = slice(32 * (h % 4), 32 * (h % 4) + 32)
                        t = mm(ps[:, 4 + h % 4, (h // 4) * TOK:(h // 4) * TOK + W_], iqT[r, h // 4, b * P:b * P + P],
                               ikT[r, 0:W_], start=True, stop=True, skip_group_check=True)
                    t.then_inc(idx_pe, 1)

                def sb_scores():
                    pe.wait_ge(turned_out, L * 10 + 8)
                    pe.wait_ge(relu_done, L * 2 + 2)
                    for h in range(4):
                        r, first = slice(64 * (h % 2), 64 * (h % 2) + 64), h < 2
                        mm(ps[:, 4 + h % 2, (h // 2) * TOK:(h // 2) * TOK + TOK], sbkT[r, h // 2, 0:P], sbqT[r, h // 2, :],
                           start=first, stop=False, skip_group_check=True)
                        t = mm(ps[:, 6 + h % 2, (h // 2) * P:(h // 2) * P + P], sbkT[r, h // 2, P:TOK],
                               sbqT[r, h // 2, P:TOK], start=first, stop=False, skip_group_check=True)
                    t.then_inc(sb_pe, 1)

                def sb_sums():
                    pe.wait_ge(sb_dve, L * 2 + 1)
                    tri, ones = cst[:, C_TRI:C_TRI + P], cst[:, C_ONES:C_ONES + P]
                    for e in range(2):
                        mm(ps[:, 4 + e, :], tri, sb_sp[:, e * 512:e * 512 + 512], start=False, stop=False, skip_group_check=True)
                        own = sb_sp[:, 1024 + e * TOK:1024 + e * TOK + TOK]
                        mm(ps[:, 4 + e, :].rearrange("p (h n) -> p h n", h=2)[:, :, P:TOK], ones,
                           own.rearrange("p (h n) -> p h n", h=2), start=False, stop=True, skip_group_check=True)
                        t = mm(ps[:, 6 + e, 0:TOK], tri, own, start=False, stop=True, skip_group_check=True)
                    t.then_inc(sb_pe, 1)

                def sb_values():
                    pe.wait_ge(sb_dve, L * 2 + 2)
                    for h in range(4):
                        o = ps[64 * (h % 2):64 * (h % 2) + 64, 4, (h // 2) * TOK:(h // 2) * TOK + TOK]
                        s = (h % 2) * 2 + h // 2
                        mm(o, v_sb[:, 0, 64 * h:64 * h + 64], sb_a[:, s * TOK:s * TOK + TOK], start=True, stop=False,
                           skip_group_check=True)
                        t = mm(o[:, P:TOK], v_sb[:, 1, 64 * h:64 * h + 64], sb_a[:, 1024 + s * P:1024 + s * P + P],
                               start=False, stop=True, skip_group_check=True)
                    t.then_inc(sb_pe, 1)

                def y_branch(i):
                    if i == 0:
                        pe.wait_ge(br_lo, L * N_BR + BR["dsa1"] + 1)
                    elif i == 1:
                        pe.wait_ge(nat_done, L * (NMG + 2) + NMG)
                    else:
                        pe.wait_ge(merge_done, L * 4 + i - 1)
                    o = 4 if i % 2 == 0 else 0
                    for k in range(2):
                        half(L, h0 + M_BRANCH + 2 * i + k, k, 1, D, lambda blk, c, w: ps[:, o + 2 * blk + c // 512, :],
                             brh[:, i], brl[:, i], 2)

                def m_turn():
                    pe.wait_ge(merge_done, L * 4 + 4)
                    for blk in range(NB):
                        for hf in range(2):
                            for c in range(4):
                                k = 4 * hf + c
                                t = turn(ps[:, 4 + 2 * blk + hf, c * P:c * P + P], merged[:, blk, k * P:k * P + P])
                            t.then_inc(m_turned, 1)

                def mem_turn():
                    pe.wait_ge(mem_in, 16 * (L + 1))
                    pe.wait_ge(m_lo, L * 4 + 4)
                    for blk in range(NB):
                        for hf in range(2):
                            for c in range(4):
                                k = 4 * hf + c
                                t = turn(ps[:, 4 + 2 * blk + hf, c * P:c * P + P], memn[:, blk, k * P:k * P + P])
                            t.then_inc(mem_turned, 1)

                for m in range(M_BRANCH):
                    for j, at in AT_T.items():
                        if m == at:
                            t_pe_wait(L, j)
                            t_step(j)
                    if m == AT_POOLED:
                        pooled()
                    if m == AT_POOLMIX:
                        pe.wait_ge(mix_out, L * 2 + 1)
                    if m == AT_DKV:
                        dsa_kv()
                    for b in range(NB):
                        if m == AT_IDX[b]:
                            index(b)
                    if m == AT_SB[0]:
                        sb_scores()
                    if m == AT_SB[1]:
                        sb_sums()
                    if m == AT_SB[2]:
                        sb_values()
                    for n, at in enumerate(AT_ATT):
                        if m == at:
                            att_scores(L, n)
                        if m == at + 2:
                            att_turn(L, n)
                        if m == at + 3:
                            att_values(L, n)
                    g, i = m // 4, m % 4
                    if m == 0:
                        pe.wait_ge(x_lo, L * 16 + 8)
                    if i == 0 and g >= 2:
                        pe.wait_ge(nat_done, L * (NMG + 2) + g - 1)
                    n = MIX_COLS[g][1]
                    half(L, h0 + m, 2 * i, 2, n, lambda blk, c, w: ps[:, 2 * (g % 2) + blk, 0:n], xh, xl, KC)
                    if m == AT_POOLMIX:
                        pool_mix()
                for i in range(4):
                    y_branch(i)
                m_turn()
                for k in range(KC):
                    pe.wait_ge(m_lo, L * 4 + 4)
                    half(L, h0 + M_OUT + k, k, 1, D, lambda blk, c, w: ps[:, 2 * blk + c // 512, :], xh, xl, KC)
                    if M_OUT + k == AT_MEM:
                        mem_turn()

            def t_pe_wait(L, j):
                pe.wait_ge(nat_done, L * (NMG + 2) + (0, 1, 1, 1, 2, 2, 3, 4)[j] + 1)
                if j == 3:
                    pe.wait_ge(act_link, L * N_ALINK + 1)
                if j in (4, 5):
                    pe.wait_ge(relu_done, L * 2 + 1)
                    pe.wait_ge(mix_out, L * 2 + 2)
                if j in (6, 7):
                    pe.wait_ge(relu_done, L * 2 + 2)

            def att_scores(L, n):
                kind, b = ATT[n]
                if n == 0:
                    pe.wait_ge(br_lo, L * N_BR + BR["sb"] + 1)
                elif n != 4:
                    pe.wait_ge(br_lo, L * N_BR + BR[kind + str(b)])
                W_ = TOK if kind == "x" else P * (b + 1)
                qT, kT = {"swa": (swqT, swkT), "dsa": (dqT, dkT), "x": (xqT, mkT)}[kind]
                for h in range(4):
                    r = slice(64 * (h % 2), 64 * (h % 2) + 64)
                    c = (0 if h % 2 == h // 2 else 1) if kind == "swa" else h // 2
                    t = mm(ps[:, 4 + h % 2, (h // 2) * TOK:(h // 2) * TOK + W_], qT[r, h // 2, b * P:b * P + P],
                           kT[r, c, 0:W_], start=True, stop=True, skip_group_check=True)
                t.then_inc(att_s, 1)

            def att_turn(L, n):
                kind, b = ATT[n]
                pe.wait_ge(att_p, L * N_ATT + n + 1)
                for h in range(4):
                    for k in range(2 if kind == "x" else b + 1):
                        t = turn(ps[:, 6 + h // 2, (h % 2) * TOK + k * P:(h % 2) * TOK + k * P + P],
                                 sc[:, h, k * P:k * P + P])
                t.then_inc(att_t, 1)

            def att_values(L, n):
                kind, b = ATT[n]
                v = {"swa": v_sw, "dsa": v_ds, "x": v_m}[kind]
                K = 2 if kind == "x" else b + 1
                pe.wait_ge(att_tev, L * N_ATT + n + 1)
                for h in range(4):
                    o = ps[64 * (h % 2):64 * (h % 2) + 64, 4, (h // 2) * P:(h // 2) * P + P]
                    hv = h // 2 if kind == "swa" else h
                    for k in range(K):
                        t = mm(o, v[:, k, 64 * hv:64 * hv + 64], pT[:, (h % 2) * 2 + h // 2, k, :], start=k == 0, stop=k == K - 1,
                               skip_group_check=True)
                t.then_inc(att_o, 1)

            def memory(L):
                h0 = H_X
                pe.wait_ge(mem_lo, L * 4 + 4)
                for i in range(4):
                    half(L, h0 + i, 2 * i, 2, 512, lambda blk, c, w: ps[:, 4 + blk, :], memh, meml, KC)
                pe.wait_ge(nat_done, L * (NMG + 2) + NMG + 1)
                for c in range(2):
                    for blk in range(NB):
                        t = turn(ps[:, 6, c * TOK + blk * P:c * TOK + blk * P + P], nat[:, 0, blk, c * P:c * P + P])
                t.then_inc(turned, 1)
                turn_x(L, 2, 0)
                pe.wait_ge(x_lo, L * 16 + 12)
                for i in range(2):
                    half(L, h0 + 4 + i, 4 * i, 4, BW, lambda blk, c, w: ps[:, 4 + blk, 0:BW], xh, xl, KC)
                pe.wait_ge(nat_done, L * (NMG + 2) + NMG + 2)
                for c in range(2):
                    for blk in range(NB):
                        t = turn(ps[:, 7, c * TOK + blk * P:c * TOK + blk * P + P], nat[:, 1, blk, c * P:c * P + P])
                t.then_inc(turned, 1)
                pe.wait_ge(turned_out, L * 10 + 10)
                for n in (4, 5):
                    if n == 5:
                        pe.wait_ge(br_lo, L * N_BR + BR["x0"] + 1)
                    att_scores(L, n)
                    att_turn(L, n)
                    att_values(L, n)
                pe.wait_ge(br_lo, L * N_BR + BR["x1"] + 1)
                for k in range(2):
                    half(L, h0 + 6 + k, k, 1, D, lambda blk, c, w: ps[:, 2 * blk + c // 512, :], brh[:, 0], brl[:, 0], 2)

            with pe.Fori(0, DEPTH) as L:
                pe.wait_ge(params_in, 16 * N_PAR * (L + 1))
                ffn(L, 0, H_FFN1, 0)
                mixer(L)
                memory(L)
                ffn(L, 1, H_FFN2, 3)

        @block.scalar
        def _(act):
            fn = nc.scalar.activation
            act.wait_ge(const_in, 16)

            def hi(L, h, it=0):
                if h >= NH:
                    return
                u, n = h // 2, HALF[h]
                if h % 2 == 0:
                    act.wait_ge(raw_in[u % RAW], 32 * (L * (NU // RAW) + u // RAW + 1 + it))
                act.wait_ge(half_done, L * NH + h + 1 + it * 8)
                fn(wh[:, h % SPL, 0:n], raw[:, u % RAW, (h % 2) * n:(h % 2) * n + n], ACT.Copy).then_inc(hi_done, 1)

            def group_done(L, h, it=0):
                act.wait_ge(half_done, L * NH + h + 1 + SPL + it * 8)

            def square(L, src, name, n=D):
                q = RQ[name]
                act.wait_ge(squared, L * NRQ + q)
                fn(junk[:, 0:n], src, ACT.Square, accum_out=ssq[:, q:q + 1]).then_inc(squared, 1)

            def pre(L, b, bank):
                gi = (0, 1, 2, 4)[b]
                for j in range(4):
                    act.wait_ge(x_turned, L * 16 + b * 4 + j + 1)
                    for c in range(4):
                        k, blk = 4 * (j % 2) + c, j // 2
                        t = fn(xh[:, k, blk * P:blk * P + P], ps[:, bank + j, c * P:c * P + P], ACT.Copy,
                               scale=gT[:, gi, k:k + 1])
                    t.then_inc(x_hi, 1)
                for blk in range(NB):
                    square(L, x[:, blk], f"pre{b}_{blk}")

            def post(L, k, h_last, bank):
                group_done(L, h_last)
                for blk in range(NB):
                    square(L, wide(bank + 2 * blk), f"post{k}_{blk}")

            def ffn(L, f, h0, b):
                E = (L * 2 + f) * NG

                def silu(g, it=0):
                    group_done(L, h0 + 4 * g + 3, it)
                    if g == 0:
                        act.wait_ge(rms_ready, L * NRQ + RQ[f"pre{b}_1"] + 1)
                    if g >= 2 or not isinstance(it, int):
                        act.wait_ge(act_done, E + g - 1 + it * 2)
                    for blk in range(NB):
                        t = fn(sg[:, g % 2, blk], ps[:, 2 * (g % 2) + blk, 0:FG], ACT.Silu, scale=rs(f"pre{b}_{blk}"))
                    t.then_inc(silu_done, 1)

                def high(g, it=0):
                    bank = 2 if g == NG - 1 else 4 + g % 2
                    act.wait_ge(act_turned, E + g + 1 + it * 2)
                    k = 2 * g + 4 * it if not isinstance(it, int) else 2 * g
                    fn(ah[:, bass.ds(k, 2), :] if not isinstance(it, int) else ah[:, k:k + 2, :],
                       ps[:, bank, :].rearrange("p (c t) -> p c t", c=2), ACT.Copy).then_inc(act_hi, 1)

                pre(L, b, 4 if b == 0 else 0)
                for i in range(4):
                    hi(L, h0 + i + AHEAD)

                def group(g, it=0):
                    silu(g - 1, it)
                    hi(L, h0 + 4 * g + AHEAD, it)
                    hi(L, h0 + 4 * g + 1 + AHEAD, it)
                    high(g - 1, it)
                    hi(L, h0 + 4 * g + 2 + AHEAD, it)
                    hi(L, h0 + 4 * g + 3 + AHEAD, it)
                group(1)
                group(2)
                with act.Fori(0, (NG - 3) // 2) as it:
                    group(3, it)
                    group(4, it)
                hd = h0 + 4 * NG
                silu(NG - 1)
                hi(L, hd + AHEAD)
                hi(L, hd + 1 + AHEAD)
                high(NG - 1)
                for c in range(2, FC):
                    hi(L, hd + c + AHEAD)
                post(L, b, hd + FC - 1, 4)

            def branch_high(L, name, dst, src, scale=1.0):
                fn(dst, src, ACT.Copy, scale=scale).then_inc(br_hi, 1)

            def att_exp_step(L, n):
                kind, b = ATT[n]
                W_ = TOK if kind == "x" else P * (b + 1)
                act.wait_ge(att_max, L * N_ATT + n + 1)
                for h in range(4):
                    t = fn(sc[:, h, 0:W_], sc[:, h, 0:W_], ACT.Exp, bias=nmx[:, h:h + 1], accum_out=den[:, h:h + 1])
                if kind == "swa":
                    for h in range(4):
                        at = (h % 2) * 2 + h // 2
                        t = fn(esk[:, at:at + 1], snk[:, h:h + 1], ACT.Exp, bias=nmx[:, at:at + 1])
                t.then_inc(att_exp, 1)

            def att_high(L, n):
                kind, b = ATT[n]
                i = {"swa": 3, "dsa": 1, "x": 0}[kind]
                act.wait_ge(att_o, L * N_ATT + n + 1)
                branch_high(L, kind + str(b), brh[:, i, :, b * P:b * P + P],
                            ps[:, 4, 0:TOK].rearrange("p (c t) -> p c t", c=2))

            def mixer(L):
                h0 = H_MIX
                pre(L, 1, 4)

                def natural(g):
                    group_done(L, h0 + 4 * g + 3)
                    s, bank = g % 2, 2 * (g % 2)
                    if g == 0:
                        act.wait_ge(rms_ready, L * NRQ + RQ["pre1_1"] + 1)
                    if g == 2:
                        act.wait_ge(turned, L * 10 + 1)
                    if g == 3:
                        act.wait_ge(turned, L * 10 + 4)
                    if g == 5:
                        act.wait_ge(half_rms, L + 1)
                    for blk in range(NB):
                        src, r = ps[:, bank + blk, :], rs(f"pre1_{blk}")
                        if g == 0:
                            t = fn(u_n[:, blk], src[:, 0:256], ACT.Copy, scale=r)
                            t = fn(nat[:, 0, blk, 256:512], src[:, 256:512], ACT.Copy, scale=r)
                        elif g == 1:
                            t = fn(nat[:, 1, blk, 0:424], src[:, 0:424], ACT.Copy, scale=r)
                            for k in range(4):
                                t = fn(ikr[:, blk, k], src[:, 384:416], ACT.Copy, scale=r)
                        elif g == 2:
                            t = fn(nat[:, 0, blk], src, ACT.Copy, scale=r)
                        elif g == 3:
                            t = fn(v_sb[:, blk], src[:, 0:256], ACT.Copy, scale=r)
                            t = fn(nat[:, 1, blk, 256:512], src[:, 256:512], ACT.Copy, scale=r)
                        elif g == 4:
                            fn(swkr[:, blk, 0], src[:, 0:128], ACT.Copy, scale=r)
                            fn(swkr[:, blk, 1, 0:64], src[:, 64:128], ACT.Copy, scale=r)
                            fn(swkr[:, blk, 1, 64:128], src[:, 0:64], ACT.Copy, scale=r)
                            t = fn(v_sw[:, blk], src[:, 128:256], ACT.Copy, scale=r)
                        else:
                            i, hf = (g - 5) // 2, (g - 5) % 2
                            t = fn(gates[:, i, blk, hf * 512:hf * 512 + 512], src, ACT.Tanh, scale=hrs[:, blk:blk + 1])
                    t.then_inc(nat_done, 1)

                def c_square():
                    act.wait_ge(nat_done, L * (NMG + 2) + 2)
                    for blk in range(NB):
                        square(L, nat[:, 1, blk, 0:P], f"c_{blk}", P)

                def c_norm():
                    act.wait_ge(rms_ready, L * NRQ + RQ["c_1"] + 1)
                    for blk in range(NB):
                        t = fn(cn[:, blk], nat[:, 1, blk, 0:P], ACT.Copy, scale=rs(f"c_{blk}"))
                    t.then_inc(act_link, 1)

                def relu_step(b):
                    W_ = P * (b + 1)
                    act.wait_ge(idx_pe, L * 2 + b + 1)
                    if b == 1:
                        act.wait_ge(sel_done, L * 2 + 1)
                    t = fn(relu[:, :, 0:W_], ps[:, 4:8, :].rearrange("p b (h n) -> p (b h) n", h=2)[:, :, 0:W_], ACT.Relu,
                           scale=32.0 ** -0.5)
                    t.then_inc(relu_done, 1)

                def sb_softplus():
                    parts = ((sb_sp[:, 0:1024], wide(4)),
                             (sb_sp[:, 1024:1536].rearrange("p (e n) -> p e n", e=2), ps[:, 6:8, 0:TOK]))
                    act.wait_ge(sb_pe, L * 3 + 1)
                    act.wait_ge(sel_done, L * 2 + 2)
                    for dst, z in parts:
                        t = fn(dst, z, ACT.Abs)
                    t.then_inc(act_link, 1)
                    act.wait_ge(act_link, L * N_ALINK + 2)
                    fn(sb_sp[:], sb_sp[:], ACT.Exp, scale=-1.0).then_inc(act_link, 1)
                    act.wait_ge(act_link, L * N_ALINK + 3)
                    fn(sb_sp[:], sb_sp[:], ACT.Ln, bias=1.0).then_inc(sb_act, 1)

                def sb_exp():
                    act.wait_ge(sb_pe, L * 3 + 2)
                    fn(sb_a[:, 0:1024], wide(4), ACT.Exp)
                    fn(sb_a[:, 1024:1536].rearrange("p (e n) -> p e n", e=2), ps[:, 6:8, 0:TOK], ACT.Exp).then_inc(sb_act, 1)

                def sb_high():
                    act.wait_ge(sb_pe, L * 3 + 3)
                    branch_high(L, "sb", brh[:, 2], ps[:, 4, :].rearrange("p (c t) -> p c t", c=2))

                def pool_high():
                    act.wait_ge(mix_pe, L * 3 + 2)
                    for c in range(2):
                        t = fn(brh[:, 0, c], ps[:, 7, c * TOK:c * TOK + TOK], ACT.Copy, scale=psc[:, c:c + 1])
                    t.then_inc(br_hi, 1)

                for m in range(M_OUT):
                    if m % 4 == 0 and 0 < m <= M_BRANCH:
                        natural(m // 4 - 1)
                        if m == 8:
                            c_square()
                    hi(L, h0 + m + AHEAD)
                    if m == 9:
                        c_norm()
                    if m == AT_POOLMIX + 1:
                        pool_high()
                    for b in range(NB):
                        if m == AT_IDX[b]:
                            relu_step(b)
                    if m == AT_SB[0]:
                        sb_softplus()
                    if m == AT_SB[1]:
                        sb_exp()
                    if m == AT_SB[2]:
                        sb_high()
                    for n, at in enumerate(AT_ATT):
                        if m == at:
                            att_exp_step(L, n)
                        if m == at + 3:
                            att_high(L, n)
                for j in range(4):
                    act.wait_ge(m_turned, L * 4 + j + 1)
                    k, blk = 4 * (j % 2), j // 2
                    fn(xh[:, k:k + 4, blk * P:blk * P + P], ps[:, 4 + j, :].rearrange("p (c t) -> p c t", c=4), ACT.Copy,
                       scale=0.5).then_inc(m_hi, 1)
                for m in range(M_OUT, M_OUT + 8):
                    hi(L, h0 + m + AHEAD)
                    if m == AT_MEM:
                        act.wait_ge(mem_in, 16 * (L + 1))
                        memory_high(L)
                post(L, 1, H_MIX + M_OUT + 7, 0)
                for blk in range(NB):
                    square(L, memn[:, blk], f"mem_{blk}")

            def memory_high(L):
                for j in range(4):
                    act.wait_ge(mem_turned, L * 4 + j + 1)
                    for c in range(4):
                        k, blk = 4 * (j % 2) + c, j // 2
                        t = fn(memh[:, k, blk * P:blk * P + P], ps[:, 4 + j, c * P:c * P + P], ACT.Copy,
                               scale=gT[:, 3, k:k + 1])
                    t.then_inc(mem_hi, 1)

            def memory(L):
                h0 = H_X
                for i in range(4):
                    hi(L, h0 + i + AHEAD)
                group_done(L, h0 + 3)
                act.wait_ge(rms_ready, L * NRQ + RQ["mem_1"] + 1)
                for blk in range(NB):
                    fn(nat[:, 0, blk, 0:256], ps[:, 4 + blk, 0:256], ACT.Copy, scale=rs(f"mem_{blk}"))
                    t = fn(v_m[:, blk], ps[:, 4 + blk, 256:512], ACT.Copy, scale=rs(f"mem_{blk}"))
                t.then_inc(nat_done, 1)
                pre(L, 2, 0)
                hi(L, h0 + 4 + AHEAD)
                hi(L, h0 + 5 + AHEAD)
                group_done(L, h0 + 5)
                act.wait_ge(rms_ready, L * NRQ + RQ["pre2_1"] + 1)
                for blk in range(NB):
                    t = fn(nat[:, 1, blk, 0:256], ps[:, 4 + blk, 0:256], ACT.Copy, scale=rs(f"pre2_{blk}"))
                t.then_inc(nat_done, 1)
                for n in (4, 5):
                    att_exp_step(L, n)
                    att_high(L, n)
                hi(L, h0 + 6 + AHEAD)
                hi(L, h0 + 7 + AHEAD)
                post(L, 2, h0 + 7, 0)

            with act.Fori(0, DEPTH) as L:
                act.wait_ge(params_in, 16 * N_PAR * (L + 1))
                for h in range(AHEAD):
                    hi(L, h)
                ffn(L, 0, H_FFN1, 0)
                mixer(L)
                memory(L)
                ffn(L, 1, H_FFN2, 3)

        @block.vector
        def _(dve):
            v = nc.vector
            dve.sem_inc(split_done, 2 * RAW)
            dve.wait_ge(const_in, 16)
            dve.wait_ge(x_in, 16)
            dve.sem_inc(x_new, NB)
            links = [0]

            def link(L, ins):
                links[0] += 1
                ins.then_inc(dve_link, 1)
                dve.wait_ge(dve_link, L * N_VLINK + links[0])

            def lo(L, h, it=0):
                if h >= NH:
                    return
                u, n = h // 2, HALF[h]
                dve.wait_ge(hi_done, L * NH + h + 1 + it * 8)
                v.tensor_tensor(wl[:, h % SPL, 0:n], raw[:, u % RAW, (h % 2) * n:(h % 2) * n + n],
                                wh[:, h % SPL, 0:n].bitcast(F32), ALU.subtract).then_inc(split_done, 1)

            def pre(L, b, bank):
                gi = (0, 1, 2, 4)[b]
                for j in range(4):
                    dve.wait_ge(x_hi, L * 16 + b * 4 + j + 1)
                    for c in range(4):
                        k, blk = 4 * (j % 2) + c, j // 2
                        s = slice(blk * P, blk * P + P)
                        t = v.scalar_tensor_tensor(xl[:, k, s], ps[:, bank + j, c * P:c * P + P], gT[:, gi, k:k + 1],
                                                   xh[:, k, s].bitcast(F32), ALU.mult, ALU.subtract)
                    t.then_inc(x_lo, 1)

            def post(L, k, h_last, bank):
                dve.wait_ge(half_done, L * NH + h_last + 1 + SPL)
                dve.wait_ge(gbc_in, 16 * (L * 4 + k + 1))
                for blk in range(NB):
                    dve.wait_ge(squared, L * NRQ + RQ[f"post{k}_{blk}"] + 1)
                    t = v.tensor_tensor(yg[:, blk], wide(bank + 2 * blk), gbc[:], ALU.mult)
                t.then_inc(gained, 1)
                for blk in range(NB):
                    dve.wait_ge(rms_ready, L * NRQ + RQ[f"post{k}_{blk}"] + 1)
                    if blk == 0:
                        dve.wait_ge(gained, L * 4 + k + 1)
                    v.scalar_tensor_tensor(x[:, blk], yg[:, blk], rs(f"post{k}_{blk}"), x[:, blk], ALU.mult,
                                           ALU.add).then_inc(x_new, 1)

            def ffn(L, f, h0, b):
                E = (L * 2 + f) * NG

                def hidden(g, it=0):
                    dve.wait_ge(silu_done, E + g + 1 + it * 2)
                    if g >= 2 or not isinstance(it, int):
                        dve.wait_ge(act_turned, E + g - 1 + it * 2)
                    for blk in range(NB):
                        t = v.scalar_tensor_tensor(an[:, g % 2, blk], ps[:, 2 * (g % 2) + blk, FG:2 * FG],
                                                   rs(f"pre{b}_{blk}"), sg[:, g % 2, blk], ALU.mult, ALU.mult)
                    t.then_inc(act_done, 1)

                def low(g, it=0):
                    bank = 2 if g == NG - 1 else 4 + g % 2
                    dve.wait_ge(act_hi, E + g + 1 + it * 2)
                    k = 2 * g + 4 * it if not isinstance(it, int) else 2 * g
                    s = bass.ds(k, 2) if not isinstance(it, int) else slice(k, k + 2)
                    v.tensor_tensor(al[:, s, :], ps[:, bank, :].rearrange("p (c t) -> p c t", c=2),
                                    ah[:, s, :].bitcast(F32), ALU.subtract).then_inc(act_lo, 1)

                pre(L, b, 4 if b == 0 else 0)
                for i in range(4):
                    lo(L, h0 + i + AHEAD)

                def group(g, it=0):
                    hidden(g - 1, it)
                    lo(L, h0 + 4 * g + AHEAD, it)
                    lo(L, h0 + 4 * g + 1 + AHEAD, it)
                    low(g - 1, it)
                    lo(L, h0 + 4 * g + 2 + AHEAD, it)
                    lo(L, h0 + 4 * g + 3 + AHEAD, it)
                group(1)
                group(2)
                with dve.Fori(0, (NG - 3) // 2) as it:
                    group(3, it)
                    group(4, it)
                hd = h0 + 4 * NG
                hidden(NG - 1)
                lo(L, hd + AHEAD)
                lo(L, hd + 1 + AHEAD)
                low(NG - 1)
                for c in range(2, FC):
                    lo(L, hd + c + AHEAD)
                post(L, b, hd + FC - 1, 4)

            def turned_copy(L, j, dst, src):
                dve.wait_ge(turned, L * 10 + j + 1)
                if j == 3:
                    v.tensor_scalar(dst, src, kvn[:, 0:1], None, ALU.mult).then_inc(turned_out, 1)
                elif j == 4:
                    v.tensor_scalar(dst, src, 0.125, None, ALU.mult).then_inc(turned_out, 1)
                else:
                    v.tensor_copy(dst, src).then_inc(turned_out, 1)

            def att_mask(L, n):
                kind, b = ATT[n]
                W_ = TOK if kind == "x" else P * (b + 1)
                dve.wait_ge(att_s, L * N_ATT + n + 1)
                if kind == "dsa":
                    dve.wait_ge(sel_done, L * 2 + 2)
                src = wide(4, 1024).rearrange("p (h n) -> p h n", h=4)
                if kind == "x":
                    link(L, v.tensor_scalar(sc[:], src, 0.125, None, ALU.mult))
                else:
                    for k in range(b + 1):
                        s = slice(k * P, k * P + P)
                        if kind == "dsa":
                            m = dmask[:, b, s]
                        else:
                            m = cst[:, C_CAUS:C_CAUS + P] if k == b else cst[:, C_WIN:C_WIN + P]
                        t = v.scalar_tensor_tensor(sc[:, :, s], src[:, :, s], 0.125,
                                                   m.unsqueeze(1).to_broadcast([P, 4, P]), ALU.mult, ALU.add)
                    link(L, t)
                link(L, v.tensor_reduce(nmx[:], sc[:, :, 0:W_], AX, ALU.max))
                if kind == "swa":
                    m = nmx[:].rearrange("p (r c) -> p r c", r=2)
                    link(L, v.tensor_tensor(m, m, snk[:].rearrange("p (c r) -> p r c", r=2), ALU.max))
                v.tensor_scalar(nmx[:], nmx[:], -1.0, None, ALU.mult).then_inc(att_max, 1)

            def att_norm(L, n):
                kind, b = ATT[n]
                W_ = TOK if kind == "x" else P * (b + 1)
                dve.wait_ge(att_exp, L * N_ATT + n + 1)
                if kind == "swa":
                    link(L, v.tensor_tensor(den[:], den[:], esk[:], ALU.add))
                link(L, v.reciprocal(rcp[:], den[:]))
                v.tensor_tensor(sc[:, :, 0:W_], sc[:, :, 0:W_], rcp[:].unsqueeze(2).to_broadcast([P, 4, W_]),
                                ALU.mult).then_inc(att_p, 1)

            def att_pT(L, n):
                kind, b = ATT[n]
                K = 2 if kind == "x" else b + 1
                dve.wait_ge(att_t, L * N_ATT + n + 1)
                v.tensor_copy(pT[:, :, 0:K, :], wide(6, 1024).rearrange("p (h k n) -> p h k n", h=4, k=2)[:, :, 0:K, :])\
                    .then_inc(att_tev, 1)

            def att_low(L, n):
                kind, b = ATT[n]
                i = {"swa": 3, "dsa": 1, "x": 0}[kind]
                dve.wait_ge(br_hi, L * N_BR + BR[kind + str(b)] + 1)
                s = slice(b * P, b * P + P)
                v.tensor_tensor(brl[:, i, :, s], ps[:, 4, 0:TOK].rearrange("p (c t) -> p c t", c=2),
                                brh[:, i, :, s].bitcast(F32), ALU.subtract).then_inc(br_lo, 1)

            def mixer(L):
                h0 = H_MIX
                pre(L, 1, 4)
                for blk in range(NB):
                    if blk == 0:
                        dve.wait_ge(rms_ready, L * NRQ + RQ["pre1_1"] + 1)
                    t = v.tensor_scalar(hrs[:, blk:blk + 1], rs(f"pre1_{blk}"), 0.5, None, ALU.mult)
                t.then_inc(half_rms, 1)

                def index(b):
                    W_ = P * (b + 1)
                    dve.wait_ge(relu_done, L * 2 + b + 1)
                    link(L, v.tensor_scalar(score[:, 0:W_], relu[:, 0, 0:W_], iw[:, b, 0:1], None, ALU.mult))
                    for s in range(1, 8):
                        h = s // 2 + 4 * (s % 2)
                        link(L, v.scalar_tensor_tensor(score[:, 0:W_], relu[:, s, 0:W_], iw[:, b, h:h + 1],
                                                       score[:, 0:W_], ALU.mult, ALU.add))
                    link(L, v.tensor_tensor(score[:, b * P:b * P + P], score[:, b * P:b * P + P],
                                            cst[:, C_CAUS:C_CAUS + P], ALU.add))

                def rounds(b, n):
                    W_ = P * (b + 1)
                    for _ in range(n):
                        v.memset(carry[:], 0.0)
                        link(L, v.max(top8[:], score[:, 0:W_]))
                        v.memset(carry[:], 0.0)
                        link(L, v.match_replace(score[:, 0:W_], top8[:], score[:, 0:W_], TAKEN))

                def chosen(b):
                    W_ = P * (b + 1)
                    link(L, v.tensor_scalar(dmask[:, b, 0:W_], score[:, 0:W_], TAKEN / 2, NEG, ALU.is_gt, ALU.mult))
                    v.tensor_tensor(dmask[:, b, b * P:b * P + P], dmask[:, b, b * P:b * P + P],
                                    cst[:, C_CAUS:C_CAUS + P], ALU.add).then_inc(sel_done, 1)

                def strict_mask(t):
                    m = cst[:, C_STRICT:C_STRICT + P].unsqueeze(1).to_broadcast([P, 4, P])
                    d0 = t[:, 0:1024].rearrange("p (h n) -> p h n", h=4)[:, :, 0:P]
                    d1 = t[:, 1024:1536].rearrange("p (h n) -> p h n", h=4)
                    v.tensor_tensor(d0, d0, m, ALU.mult)
                    return v.tensor_tensor(d1, d1, m, ALU.mult)

                for m in range(M_OUT):
                    if m == 8:
                        dve.wait_ge(nat_done, L * (NMG + 2) + 2)
                        for b in range(NB):
                            link(L, v.tensor_scalar(iw[:, b], nat[:, 1, b, 416:424], 8.0 ** -0.5, None, ALU.mult))
                    for j, at in AT_T.items():
                        if m == at:
                            dst = (dqT, iqT, ikT, cT, sbqT, sbkT, swqT, swkT)[j]
                            src = ps[:, 4 + j % 2, :]
                            if j in (2, 3):
                                turned_copy(L, j, dst[:], src[:, 0:TOK])
                            else:
                                turned_copy(L, j, dst[:], src.rearrange("p (c t) -> p c t", c=2))
                    if m == AT_POOLED:
                        dve.wait_ge(mix_pe, L * 3 + 1)
                        v.tensor_copy(poT[:], ps[:, 6, :].rearrange("p (c t) -> p c t", c=2)).then_inc(mix_out, 1)
                    if m == AT_POOLMIX + 1:
                        dve.wait_ge(br_hi, L * N_BR + BR["pool"] + 1)
                        for c in range(2):
                            t = v.scalar_tensor_tensor(brl[:, 0, c], ps[:, 7, c * TOK:c * TOK + TOK], psc[:, c:c + 1],
                                                       brh[:, 0, c].bitcast(F32), ALU.mult, ALU.subtract)
                        t.then_inc(br_lo, 1)
                    if m == AT_DKV:
                        dve.wait_ge(mix_pe, L * 3 + 3)
                        v.tensor_copy(dkT[:], ps[:, 4, :].rearrange("p (c t) -> p c t", c=2))
                        v.tensor_copy(v_ds[:], ps[:, 5, :].rearrange("p (c t) -> p c t", c=2)).then_inc(mix_out, 1)
                    for b in range(NB):
                        if m == AT_IDX[b]:
                            index(b)
                        if AT_IDX[b] < m <= AT_IDX[b] + 2:
                            rounds(b, 4)
                        if m == AT_IDX[b] + 2:
                            chosen(b)
                    if m == AT_SB[0] + 1:
                        dve.wait_ge(sb_act, L * 2 + 1)
                        v.scalar_tensor_tensor(sb_sp[:, 0:1024], wide(4), 0.0, sb_sp[:, 0:1024], ALU.max, ALU.add)
                        own = sb_sp[:, 1024:1536].rearrange("p (e n) -> p e n", e=2)
                        link(L, v.scalar_tensor_tensor(own, ps[:, 6:8, 0:TOK], 0.0, own, ALU.max, ALU.add))
                        strict_mask(sb_sp).then_inc(sb_dve, 1)
                    if m == AT_SB[1]:
                        dve.wait_ge(sb_act, L * 2 + 2)
                        strict_mask(sb_a).then_inc(sb_dve, 1)
                    if m == AT_SB[2]:
                        dve.wait_ge(br_hi, L * N_BR + BR["sb"] + 1)
                        v.tensor_tensor(brl[:, 2], ps[:, 4, :].rearrange("p (c t) -> p c t", c=2),
                                        brh[:, 2].bitcast(F32), ALU.subtract).then_inc(br_lo, 1)
                    for n, at in enumerate(AT_ATT):
                        if m == at:
                            att_mask(L, n)
                        if m == at + 2:
                            att_pT(L, n)
                        if m == at + 3:
                            att_low(L, n)
                    lo(L, h0 + m + AHEAD)
                    for n, at in enumerate(AT_ATT):
                        if m == at:
                            att_norm(L, n)
                    for i in range(3):
                        if m == AT_MERGE[i]:
                            merge(L, i)
                merge(L, 3)
                for j in range(4):
                    dve.wait_ge(m_hi, L * 4 + j + 1)
                    k, s = 4 * (j % 2), slice((j // 2) * P, (j // 2) * P + P)
                    v.scalar_tensor_tensor(xl[:, k:k + 4, s], ps[:, 4 + j, :].rearrange("p (c t) -> p c t", c=4), 0.5,
                                           xh[:, k:k + 4, s].bitcast(F32), ALU.mult, ALU.subtract).then_inc(m_lo, 1)
                for m in range(M_OUT, M_OUT + 8):
                    lo(L, h0 + m + AHEAD)
                    if m == AT_MEM:
                        for j in range(4):
                            dve.wait_ge(mem_hi, L * 4 + j + 1)
                            for c in range(4):
                                k, blk = 4 * (j % 2) + c, j // 2
                                s = slice(blk * P, blk * P + P)
                                t = v.scalar_tensor_tensor(meml[:, k, s], ps[:, 4 + j, c * P:c * P + P], gT[:, 3, k:k + 1],
                                                           memh[:, k, s].bitcast(F32), ALU.mult, ALU.subtract)
                            t.then_inc(mem_lo, 1)
                post(L, 1, H_MIX + M_OUT + 7, 0)

            def merge(L, i):
                dve.wait_ge(half_done, L * NH + H_MIX + M_BRANCH + 2 * i + 1 + 1 + SPL)
                dve.wait_ge(nat_done, L * (NMG + 2) + NMG)
                o = 4 if i % 2 == 0 else 0
                for blk in range(NB):
                    y = wide(o + 2 * blk)
                    if i == 0:
                        t = v.scalar_tensor_tensor(merged[:, blk], gates[:, i, blk], 1.0, y, ALU.add, ALU.mult)
                    else:
                        link(L, v.scalar_tensor_tensor(tmp[:], gates[:, i, blk], 1.0, y, ALU.add, ALU.mult))
                        t = v.tensor_tensor(merged[:, blk], merged[:, blk], tmp[:], ALU.add)
                        if blk == 0:
                            link(L, t)
                t.then_inc(merge_done, 1)
                dve.wait_ge(merge_done, L * 4 + i + 1)

            def memory(L):
                h0 = H_X
                for i in range(4):
                    lo(L, h0 + i + AHEAD)
                turned_copy(L, 8, mkT[:], ps[:, 6, :].rearrange("p (c t) -> p c t", c=2))
                pre(L, 2, 0)
                lo(L, h0 + 4 + AHEAD)
                lo(L, h0 + 5 + AHEAD)
                turned_copy(L, 9, xqT[:], ps[:, 7, :].rearrange("p (c t) -> p c t", c=2))
                for n in (4, 5):
                    att_mask(L, n)
                    att_norm(L, n)
                    att_pT(L, n)
                    att_low(L, n)
                lo(L, h0 + 6 + AHEAD)
                lo(L, h0 + 7 + AHEAD)
                post(L, 2, h0 + 7, 0)

            with dve.Fori(0, DEPTH) as L:
                dve.wait_ge(params_in, 16 * N_PAR * (L + 1))
                for h in range(AHEAD):
                    lo(L, h)
                ffn(L, 0, H_FFN1, 0)
                mixer(L)
                memory(L)
                ffn(L, 1, H_FFN2, 3)
            assert links[0] == N_VLINK, links[0]


_INS = ("x", "mem", "ffn1_pre", "ffn1_w_up", "ffn1_w_down", "ffn1_post", "mix_pre", "w_in", "pool_w", "pool_scale",
        "dsa_kv_norm", "dsa_w_uk", "dsa_w_uv", "swa_sinks", "w_branch", "w_out", "mix_post", "xattn_pre", "mem_norm",
        "xattn_w_q", "xattn_w_kv", "xattn_w_o", "xattn_post", "ffn2_pre", "ffn2_w_up", "ffn2_w_down", "ffn2_post")


def kernel(**inputs):
    import numpy as _np
    import concourse.bacc as _bacc
    from concourse import mybir as _mybir
    from concourse.bass_utils import run_bass_kernel_spmd as _run

    nc = _bacc.Bacc("TRN2", target_bir_lowering=False, num_devices=1)
    arrays, args = {}, {}
    for name in _INS + ("consts",):
        a = constants() if name == "consts" else _np.ascontiguousarray(inputs[name])
        arrays[f"in_{name}"] = a
        args[name] = nc.dram_tensor(f"in_{name}", a.shape, _mybir.dt.from_np(a.dtype), kind="ExternalInput").ap()
    out = nc.dram_tensor("out_x", (1, TOK, D), F32, kind="ExternalOutput").ap()
    trunk(nc, args, out)
    r = _run(nc, [arrays], core_ids=[0])
    return r.results[0]["out_x"]
```

```python
from contextlib import ExitStack

import concourse.bass as bass
from concourse import mybir
import numpy as np

P = 128
F32 = mybir.dt.float32
F32R = mybir.dt.float32r
ALU = mybir.AluOpType
ACT = mybir.ActivationFunctionType
AX = mybir.AxisListType.X

DEPTH = 2
TOK = 256
NB = TOK // P
D = 1024
KC = D // P
F = 2816
FG = 256
NG = F // FG
FC = F // P
BW = 256
EPS = 1e-6
NEG = -1e30
TAKEN = -3e38
TOPK = 64
WINDOWS = (2, 4, 8, 16)

H_FFN1 = 0
H_MIX = H_FFN1 + 4 * NG + FC
MIX_COLS = ((0, 512), (512, 424), (936, 512), (1448, 512), (1960, 256)) + tuple(
    (2216 + 512 * g, 512) for g in range(8))
NMG = len(MIX_COLS)
ORDER = (0, 2, 3, 1)
M_GATES = 20
M_OUT = M_GATES + 10 * len(ORDER)
H_X = H_MIX + M_OUT + 8
H_FFN2 = H_X + 8
NH = H_FFN2 + 4 * NG + FC
NU = NH // 2
RAW = 4
SPL = 8
AHEAD = SPL - 1
SKEW = 4
assert NU % RAW == 0 and NH % SPL == 0

HALF = [1024] * NH
for _g in range(5):
    for _i in range(4):
        HALF[H_MIX + 4 * _g + _i] = 2 * MIX_COLS[_g][1]

RQ = {n: i for i, n in enumerate([
    "pre0_0", "pre0_1", "post0_0", "post0_1", "pre1_0", "pre1_1", "c_0", "c_1", "mem_0", "mem_1",
    "post1_0", "post1_1", "pre2_0", "pre2_1", "post2_0", "post2_1", "pre3_0", "pre3_1", "post3_0", "post3_1"])}
NRQ = len(RQ)

AT_T = {0: 5, 1: 9, 2: 9, 3: 10, 4: 14, 5: 14, 6: 19, 7: 21}
AT_POOLED, AT_POOLMIX = 6, 7
AT_DKV = 11
AT_IDX = (12, 15)
AT_SB = (22, 25, 27)
AT_ATT = (29, 33, 37, 41)
AT_MEM = 52

C_ID, C_SC, C_TRI, C_ONES, C_STRICT, C_CAUS, C_WIN = 0, 128, 136, 264, 392, 520, 648
N_FIRST, N_CONST = C_TRI, 776
N_BAND = 12 * P
K_INVD, K_INVC, K_INVD4, K_EPS, K_EPS4, K_POW = range(6)


def constants():
    c = np.zeros((P, N_CONST + N_BAND), np.float32)
    i, j = np.arange(P)[:, None], np.arange(P)[None, :]
    c[:, C_ID:C_ID + P] = i == j
    c[:, C_TRI:C_TRI + P] = -(i >= j).astype(np.float32)
    c[:, C_ONES:C_ONES + P] = -1.0
    c[:, C_STRICT:C_STRICT + P] = i < j
    c[:, C_CAUS:C_CAUS + P] = np.where(j <= i, 0.0, NEG)
    c[:, C_WIN:C_WIN + P] = np.where(j > i, 0.0, NEG)
    for g, w in enumerate(WINDOWS):
        for part, (si, ti) in enumerate(((0, 0), (0, P), (P, P))):
            s, t = i + si, j + ti
            band = ((s <= t) & (s > t - w)) / np.minimum(t + 1, w) - (s == t)
            at = N_CONST + (3 * g + part) * P
            c[:, at:at + P] = band
    for k, v in ((K_INVD, 1 / D), (K_INVC, 1 / P), (K_INVD4, 4 / D), (K_EPS, EPS), (K_EPS4, 4 * EPS), (K_POW, -0.5)):
        c[:, C_SC + k] = v
    return c


def trunk(nc, a, out):
    with ExitStack() as ctx:
        sem = lambda n: ctx.enter_context(nc.semaphore(n))
        base = (nc.sbuf_base + 63) // 64 * 64
        place = {}

        def put(name, shape, dt, at=None):
            size = 4 * int(np.prod(shape))
            at = place.get("end", base) if at is None else at
            place["end"] = max(place.get("end", base), at + (size + 63) // 64 * 64)
            assert place["end"] <= nc.sbuf_usable_end, (name, place["end"])
            place[name] = at
            return nc.alloc_sbuf_tensor_at(name, [P, *shape], dt, offset=at)

        raw = put("raw", (RAW, 2048), F32)
        wh = put("wh", (SPL, 1024), F32R)
        wl = put("wl", (SPL, 1024), F32R)
        x = put("x", (NB, D), F32)
        xh = put("xh", (KC, TOK), F32R)
        xl = put("xl", (KC, TOK), F32R)
        ah = put("ah", (FC, TOK), F32R)
        al = put("al", (FC, TOK), F32R)
        A = place["ah"]
        brh = put("brh", (4, 2, TOK), F32R, A)
        brl = put("brl", (4, 2, TOK), F32R, A + 8192)
        at = A + 16384

        def mixer_tile(name, shape):
            nonlocal at
            t = put(name, shape, F32, at)
            at += 4 * int(np.prod(shape))
            assert at <= A + 2 * 4 * FC * TOK
            return t
        u_n = mixer_tile("u_n", (NB, BW))
        v_sb = mixer_tile("v_sb", (NB, BW))
        v_sw = mixer_tile("v_sw", (NB, P))
        v_ds = mixer_tile("v_ds", (NB, BW))
        dqT = mixer_tile("dqT", (2, TOK))
        iqT = mixer_tile("iqT", (2, TOK))
        ikT = mixer_tile("ikT", (TOK,))
        cT = mixer_tile("cT", (TOK,))
        dkT = mixer_tile("dkT", (2, TOK))
        sbqT = mixer_tile("sbqT", (2, TOK))
        sbkT = mixer_tile("sbkT", (2, TOK))
        swqT = mixer_tile("swqT", (2, TOK))
        swkT = mixer_tile("swkT", (2, TOK))
        poT = put("poT", (2, TOK), F32, place["sbqT"])
        memn = put("memn", (NB, D), F32, A + 16384)
        memh = put("memh", (KC, TOK), F32R, A + 24576)
        meml = put("meml", (KC, TOK), F32R, A + 32768)
        tmp = put("tmp", (NB, 512), F32, A + 40960)
        sc1 = put("sc1", (4, TOK), F32, A + 4096)
        pT1 = put("pT1", (4, 2, P), F32, A + 12288)
        yg = put("yg", (NB, D), F32)
        W = place["yg"]
        bands = put("bands", (N_BAND,), F32, W)
        merged = put("merged", (NB, D), F32, W)
        nat = put("nat", (2, NB, 512), F32)
        sg = put("sg", (2, NB, FG), F32, place["nat"])
        an = put("an", (2, NB, FG), F32, place["nat"] + 4096)
        gate = put("gate", (2, NB, 512), F32, place["nat"])
        sc = put("sc", (4, TOK), F32)
        S = place["sc"]
        junk = put("junk", (D,), F32, S)
        pT = put("pT", (4, 2, P), F32)
        gbc = put("gbc", (D,), F32)
        assert place["pT"] == S + 4096 and place["gbc"] == S + 8192
        cn = put("cn", (NB, P), F32, S + 4096)
        ikr = put("ikr", (NB, 4, 32), F32, S + 5120)
        swkr = put("swkr", (NB, 2, P), F32, S + 6144)
        relu = put("relu", (8, TOK), F32, S)
        sb_sp = put("sb_sp", (1536,), F32, S)
        sb_a = put("sb_a", (1536,), F32, S + 6144)
        score = put("score", (TOK,), F32)
        dmask = put("dmask", (NB, TOK), F32)
        xqT = put("xqT", (2, TOK), F32, place["score"])
        mkT = put("mkT", (2, TOK), F32)
        v_m = put("v_m", (NB, BW), F32)
        cst = put("cst", (N_CONST,), F32)
        gT = put("gT", (5, KC), F32)
        pw = put("pw", (2, 64), F32)
        psc = put("psc", (2,), F32)
        kvn = put("kvn", (1,), F32)
        uk = put("uk", (BW,), F32)
        uv = put("uv", (BW,), F32)
        snk = put("snk", (4,), F32)
        ssq = put("ssq", (NRQ,), F32)
        msq = put("msq", (NRQ,), F32)
        rms = put("rms", (NRQ,), F32)
        hrs = put("hrs", (NB,), F32)
        iw = put("iw", (NB, 8), F32)
        top8 = put("top8", (8,), F32)
        nmx = put("nmx", (2, 4), F32)
        den = put("den", (2, 4), F32)
        rcp = put("rcp", (2, 4), F32)
        carry = put("carry", (1,), F32)
        esk = put("esk", (4,), F32)

        ps = ctx.enter_context(nc.psum_tensor("ps", [P, 8, 512], F32))

        ident = cst[:, C_ID:C_ID + P]
        k_col = lambda k: cst[:, C_SC + k:C_SC + k + 1]

        raw_in = [sem(f"raw_in{r}") for r in range(RAW)]
        hi_done, split_done, half_done = sem("hi_done"), sem("split_done"), sem("half_done")
        params_in, const_in, x_in, gbc_in, mem_in, stored = (
            sem(n) for n in ("params_in", "const_in", "x_in", "gbc_in", "mem_in", "stored"))
        x_new, x_turned, x_hi, x_lo = sem("x_new"), sem("x_turned"), sem("x_hi"), sem("x_lo")
        squared, rms_ready, gained = sem("squared"), sem("rms_ready"), sem("gained")
        silu_done, act_done, act_turned, act_hi, act_lo = (
            sem(n) for n in ("silu_done", "act_done", "act_turned", "act_hi", "act_lo"))
        nat_done, turned, turned_out = sem("nat_done"), sem("turned"), sem("turned_out")
        mix_pe, mix_out, br_hi, br_lo = sem("mix_pe"), sem("mix_out"), sem("br_hi"), sem("br_lo")
        idx_pe, relu_done, sel_done = sem("idx_pe"), sem("relu_done"), sem("sel_done")
        sb_pe, sb_act, sb_dve = sem("sb_pe"), sem("sb_act"), sem("sb_dve")
        att_s, att_max, att_exp, att_p, att_t, att_tev, att_o = (
            sem(f"att_{n}") for n in ("s", "max", "exp", "p", "t", "tev", "o"))
        merge_done, m_turned, m_hi, m_lo = sem("merge_done"), sem("m_turned"), sem("m_hi"), sem("m_lo")
        mem_turned, mem_hi, mem_lo = sem("mem_turned"), sem("mem_hi"), sem("mem_lo")
        dve_link, act_link, pool_link = sem("dve_link"), sem("act_link"), sem("pool_link")
        half_rms, block0_done, gain_in, bands_in, masks_in = (
            sem(n) for n in ("half_rms", "block0_done", "gain_in", "bands_in", "masks_in"))

        N_PAR = 11
        N_NAT = 5 + 8 + 3
        N_MRG = 8
        N_BR = 8
        BR = {"pool": 0, "sb": 1, "swa0": 2, "swa1": 3, "dsa0": 4, "dsa1": 5, "x0": 6, "x1": 7}
        ATT = (("swa", 0), ("swa", 1), ("dsa", 0), ("dsa", 1), ("x", 0), ("x", 1))
        N_ATT = len(ATT)
        OUT_BANK = ((4, 6), (0, 2), (6, 2), (4, 6))
        S_BANK, T_BANK, O_BANK = (4, 4, 4, 4, 2, 6), (6, 6, 6, 6, 0, 2), (4, 4, 4, 4, 4, 5)
        scores, probsT = (sc, sc, sc, sc, sc, sc1), (pT, pT, pT, pT, pT, pT1)
        N_ALINK, N_VLINK = 3, 81

        up = {f: a[f"ffn{f}_w_up"].rearrange("l (c p) (t n) -> l p c t n", p=P, t=2) for f in (1, 2)}
        down = {f: a[f"ffn{f}_w_down"].rearrange("l (c p) n -> l p c n", p=P) for f in (1, 2)}
        w_in = a["w_in"].rearrange("l (c p) n -> l p c n", p=P)
        w_br = a["w_branch"].rearrange("l i (c p) n -> l i p c n", p=P)
        w_out = a["w_out"].rearrange("l (c p) n -> l p c n", p=P)
        w_q = a["xattn_w_q"].rearrange("l (c p) n -> l p c n", p=P)
        w_kv = a["xattn_w_kv"].rearrange("l (c p) n -> l p c n", p=P)
        w_o = a["xattn_w_o"].rearrange("l (c p) n -> l p c n", p=P)

        block = ctx.enter_context(nc.Block())

        @block.sync
        def _(sp):
            x_in_dram = a["x"].rearrange("o (b p) d -> p (o b) d", p=P)
            for blk in range(NB):
                sp.dma_start(x[:, blk], x_in_dram[:, blk]).then_inc(x_in, 16)
            sp.dma_start(cst[:, 0:N_FIRST], a["consts"][:, 0:N_FIRST]).then_inc(const_in, 16)

            def load(L, u, srcs, dims, it=0, by=0):
                c, n = dims
                dst = raw[:, u % RAW, 0:c * n].rearrange("p (c n) -> p c n", c=c)
                sp.wait_ge(split_done, L * NH + 2 * u + 2 + it * (2 * RAW))
                for i, src in enumerate(srcs):
                    part = dst[:, :, i * n // 2:(i + 1) * n // 2] if by else dst[:, i * c // 2:(i + 1) * c // 2, :]
                    sp.dma_start(part, src).then_inc(raw_in[u % RAW], 16)

            def chunks(w, k0, kn):
                return w[:, k0:k0 + kn // 2, :], w[:, k0 + kn // 2:k0 + kn, :]

            def load_gain(L, k, name):
                if k == 1:
                    sp.wait_ge(br_lo, L * N_BR + BR["sb"] + 1)
                if k == 2:
                    sp.wait_ge(gained, L * 8 + 2 * k)
                sp.dma_start(gbc[:], a[name][L].partition_broadcast(P)).then_inc(gbc_in, 16)

            def ffn(L, f, u0, k):
                def group(g, u, it=0):
                    for i in range(2):
                        load(L, u + i, [up[f][L, :, 4 * i:4 * i + 4, t, bass.ts(g, FG)] for t in range(2)], (4, 2 * FG),
                             it, by=1)
                group(0, u0)
                if f == 1:
                    params(L)
                else:
                    load_gain(L, 2, "xattn_post")
                with sp.Fori(0, (NG - 1) // 2) as it:
                    for j in range(2):
                        group(2 * it + 1 + j, u0 + 2 + 2 * j, it)
                load_gain(L, k, f"ffn{f}_post")
                for c in range(FC // 2):
                    load(L, u0 + 2 * NG + c, chunks(down[f][L], 2 * c, 2), (2, D))

            def params(L):
                def par(dst, src):
                    sp.dma_start(dst, src).then_inc(params_in, 16)
                with nc.allow_non_contiguous_dma("gains, a value per partition"):
                    for i, n in enumerate(("mix_pre", "xattn_pre", "mem_norm", "ffn2_pre")):
                        par(gT[:, i + 1, :], a[n][L].rearrange("(c p) -> p c", p=P))
                    par(psc[:], a["pool_scale"][L].rearrange("(c p) -> p c", p=P))
                    par(kvn[:], a["dsa_kv_norm"][L].rearrange("(c p) -> p c", p=P))
                for c in range(2):
                    par(pw[:, c, :], a["pool_w"][L, 2 * c:2 * c + 2].rearrange("g c d -> (g c) d"))
                par(uk[:], a["dsa_w_uk"][L].rearrange("r h d -> r (h d)"))
                par(uv[:], a["dsa_w_uv"][L].rearrange("r h d -> r (h d)"))
                par(snk[:], a["swa_sinks"][L].partition_broadcast(P))
                sp.dma_start(cst[:, N_FIRST:N_CONST], a["consts"][:, N_FIRST:N_CONST]).then_inc(masks_in, 16)

            with sp.Fori(0, DEPTH) as L:
                with nc.allow_non_contiguous_dma("gains, a value per partition"):
                    sp.dma_start(gT[:, 0, :], a["ffn1_pre"][L].rearrange("(c p) -> p c", p=P)).then_inc(gain_in, 16)
                ffn(L, 1, H_FFN1 // 2, 0)
                u = H_MIX // 2
                for g in range(5):
                    c0, n = MIX_COLS[g]
                    for i in range(2):
                        load(L, u, chunks(w_in[L, :, :, c0:c0 + n], 4 * i, 4), (4, n))
                        u += 1
                    if g == 1:
                        sp.wait_ge(x_new, L * 8 + 4)
                        sp.dma_start(bands[:], a["consts"][:, N_CONST:N_CONST + N_BAND]).then_inc(bands_in, 16)
                for n, b in enumerate(ORDER):
                    for hf in range(2):
                        c0 = MIX_COLS[5 + 2 * b + hf][0]
                        for i in range(2):
                            load(L, u, chunks(w_in[L, :, :, c0:c0 + 512], 4 * i, 4), (4, 512))
                            u += 1
                    if n == 3:
                        sp.wait_ge(br_lo, L * N_BR + BR["dsa1"] + 1)
                        sp.dma_start(memn[:], a["mem"].rearrange("o (b p) d -> p (o b) d", p=P)).then_inc(mem_in, 16)
                    load(L, u, [w_br[L, b, :, :, 512 * hf:512 * hf + 512] for hf in range(2)], (4, 512))
                    u += 1
                    if n == 1:
                        load_gain(L, 1, "mix_post")
                for i in range(4):
                    load(L, u, chunks(w_out[L], 2 * i, 2), (2, D))
                    u += 1
                load(L, u, chunks(w_kv[L, :, :, 0:BW], 0, KC), (KC, BW))
                load(L, u + 1, chunks(w_q[L], 0, KC), (KC, BW))
                load(L, u + 2, chunks(w_kv[L, :, :, BW:2 * BW], 0, KC), (KC, BW))
                u += 2
                load(L, u + 1, chunks(w_o[L], 0, 2), (2, D))
                ffn(L, 2, H_FFN2 // 2, 3)
            sp.wait_ge(x_new, 2 + 8 * DEPTH)
            sp.dma_start(out.rearrange("o (b p) d -> p (o b) d", p=P), x[:]).then_inc(stored, 16)
            sp.wait_ge(stored, 16)

        @block.gpsimd
        def _(pool):
            pool.wait_ge(const_in, 16)
            with pool.Fori(0, DEPTH) as L:
                for name, q in RQ.items():
                    half = name in ("post0_0", "post0_1", "post3_0", "post3_1")
                    inv = K_INVC if name[0] == "c" else K_INVD4 if half else K_INVD
                    pool.wait_ge(squared, L * NRQ + q + 1)
                    nc.gpsimd.tensor_tensor(msq[:, q:q + 1], ssq[:, q:q + 1], k_col(inv), ALU.mult).then_inc(pool_link, 1)
                    pool.wait_ge(pool_link, L * 2 * NRQ + 2 * q + 1)
                    nc.gpsimd.tensor_tensor(msq[:, q:q + 1], msq[:, q:q + 1], k_col(K_EPS4 if half else K_EPS),
                                            ALU.add).then_inc(pool_link, 1)
                    pool.wait_ge(pool_link, L * 2 * NRQ + 2 * q + 2)
                    nc.gpsimd.tensor_tensor(rms[:, q:q + 1], msq[:, q:q + 1], k_col(K_POW), ALU.pow).then_inc(rms_ready, 1)

        def rs(name):
            return rms[:, RQ[name]:RQ[name] + 1]

        def wide(bank, n=1024, at=0):
            return ps[:].rearrange("p b n -> p (b n)")[:, bank * 512 + at:bank * 512 + at + n]

        @block.tensor
        def _(pe):
            pe.sem_inc(half_done, SPL)
            pe.wait_ge(const_in, 16)
            mm = nc.tensor.matmul

            def turn(dst, src):
                return nc.tensor.transpose(dst, src, ident)

            def mm3(dst, sh, sl, mh, ml, start, stop):
                mm(dst, sh, mh, start=start, stop=False)
                mm(dst, sh, ml, start=False, stop=False)
                return mm(dst, sl, mh, start=False, stop=stop)

            def half(L, h, k0, kn, n, dst, sh, sl, K, it=0, blocks=(0, 1)):
                pe.wait_ge(split_done, L * NH + h + 1 + 2 * RAW + it * 8)
                q = h % SPL
                for b in blocks:
                    for k in range(kn):
                        tok = slice(b * P, b * P + P)
                        for c in range(0, n, 512):
                            w = min(512, n - c)
                            mv = slice(k * n + c, k * n + c + w)
                            last = mm3(dst(b, c, w), sh[:, k0 + k, tok], sl[:, k0 + k, tok],
                                       wh[:, q, mv], wl[:, q, mv], k0 + k == 0, k0 + k == K - 1)
                if 1 in blocks:
                    last.then_inc(half_done, 1)
                return last

            def turn_x(L, b, blk):
                pe.wait_ge(x_new, L * 8 + 2 * b + blk + 1)
                for hf in range(2):
                    for c in range(4):
                        k = 4 * hf + c
                        t = turn(ps[:, OUT_BANK[b - 1][blk] + hf, c * P:c * P + P], x[:, blk, k * P:k * P + P])
                    t.then_inc(x_turned, 1)

            def head(L, b, step):
                if b == 0:
                    turn_x(L, 0, 0)
                pe.wait_ge(x_lo, L * 16 + 4 * b + 2)
                for i in range(SKEW):
                    if i == SKEW - 1:
                        turn_x(L, b, 1)
                    step(i, (0,))
                pe.wait_ge(x_lo, L * 16 + 4 * b + 4)
                for i in range(SKEW):
                    step(i, (1,))

            def tail(L, b, step):
                for i in range(SKEW):
                    t = step(i, (0,))
                t.then_inc(block0_done, 1)
                for i in range(SKEW):
                    if i == SKEW - 1 and b < 3:
                        turn_x(L, b + 1, 0)
                    step(i, (1,))

            def ffn(L, f, h0, b):
                E = (L * 2 + f) * NG

                def act_turn(g, it, bank):
                    pe.wait_ge(act_done, E + g + 1 + it * 2)
                    for c in range(2):
                        for blk in range(NB):
                            t = turn(ps[:, bank, c * TOK + blk * P:c * TOK + blk * P + P],
                                     an[:, g % 2, blk, c * P:c * P + P])
                    t.then_inc(act_turned, 1)

                def up_half(g, i, it=0, blocks=(0, 1)):
                    return half(L, h0 + 4 * g + i, 2 * i, 2, 512, lambda blk, c, w: ps[:, 2 * (g % 2) + blk, :], xh, xl,
                                KC, it, blocks)

                def down_half(c, blocks=(0, 1)):
                    return half(L, h0 + 4 * NG + c, c, 1, D, lambda blk, cc, w: ps[:, 4 + 2 * blk + cc // 512, :], ah, al,
                                FC, 0, blocks)

                def group(g, it=0):
                    if g >= 2:
                        pe.wait_ge(act_done, E + g - 1 + it * 2)
                    for i in range(4):
                        up_half(g, i, it)
                        if i == 0:
                            if g > 2:
                                pe.wait_ge(act_lo, E + g - 2 + it * 2)
                            act_turn(g - 1, it, 4 + (g - 1) % 2)

                head(L, b, lambda i, blocks: up_half(0, i, 0, blocks))
                group(1)
                group(2)
                with pe.Fori(0, (NG - 3) // 2) as it:
                    group(3, it)
                    group(4, it)
                for c in range(FC - SKEW):
                    pe.wait_ge(act_lo, E + max(c // 2 + 1, NG - 1))
                    down_half(c)
                    if c == 0:
                        act_turn(NG - 1, 0, 2)
                pe.wait_ge(act_lo, E + NG)
                tail(L, b, lambda i, blocks: down_half(FC - SKEW + i, blocks))

            def mixer(L):
                h0 = H_MIX

                def t_wait(j):
                    pe.wait_ge(nat_done, L * N_NAT + (0, 1, 1, 1, 2, 2, 3, 4)[j] + 1)
                    if j == 3:
                        pe.wait_ge(act_link, L * N_ALINK + 1)
                    if j in (4, 5):
                        pe.wait_ge(relu_done, L * 2 + 1)
                        pe.wait_ge(mix_out, L * 2 + 2)
                    if j in (6, 7):
                        pe.wait_ge(relu_done, L * 2 + 2)

                def t_step(j):
                    src = (nat[:, 0, :, 256:512], nat[:, 1, :, 128:384], ikr, cn, nat[:, 0, :, 0:256],
                           nat[:, 0, :, 256:512], nat[:, 1, :, 256:512], swkr)[j]
                    bank = 4 + j % 2
                    if j >= 2:
                        pe.wait_ge(turned_out, L * 10 + j - 1)
                    for c in range(1 if j in (2, 3) else 2):
                        for blk in range(NB):
                            s = (ikr[:, blk].rearrange("p r d -> p (r d)") if j == 2 else cn[:, blk] if j == 3
                                 else swkr[:, blk, c] if j == 7 else src[:, blk, c * P:c * P + P])
                            t = turn(ps[:, bank, c * TOK + blk * P:c * TOK + blk * P + P], s)
                    t.then_inc(turned, 1)

                def pooled():
                    pe.wait_ge(bands_in, 16 * (L + 1))
                    for g in range(4):
                        o = ps[64 * (g % 2):64 * (g % 2) + 64, 6, (g // 2) * TOK:(g // 2) * TOK + TOK]
                        band = bands[:, 3 * g * P:3 * g * P + 3 * P]
                        mm(o, u_n[:, 0, 64 * g:64 * g + 64], band[:, 0:TOK], start=True, stop=False, skip_group_check=True)
                        t = mm(o[:, P:TOK], u_n[:, 1, 64 * g:64 * g + 64], band[:, TOK:3 * P], start=False, stop=True,
                               skip_group_check=True)
                    t.then_inc(mix_pe, 1)

                def pool_mix():
                    for g in range(4):
                        r = slice(64 * (g % 2), 64 * (g % 2) + 64)
                        t = mm(ps[r, 7, (g // 2) * TOK:(g // 2) * TOK + TOK], pw[r, g // 2, :], poT[r, g // 2, :],
                               start=True, stop=True, skip_group_check=True)
                    t.then_inc(mix_pe, 1)

                def dsa_kv():
                    pe.wait_ge(turned_out, L * 10 + 4)
                    for c in range(2):
                        mm(ps[:, 4, c * TOK:c * TOK + TOK], uk[:, c * P:c * P + P], cT[:], start=True, stop=True,
                           skip_group_check=True)
                    for blk in range(NB):
                        t = mm(ps[:, 5, blk * BW:blk * BW + BW], cT[:, blk * P:blk * P + P], uv[:], start=True, stop=True,
                               skip_group_check=True)
                    t.then_inc(mix_pe, 1)

                def index(b):
                    if b == 0:
                        pe.wait_ge(mix_out, L * 2 + 2)
                        pe.wait_ge(br_lo, L * N_BR + BR["pool"] + 1)
                    else:
                        pe.wait_ge(relu_done, L * 2 + 1)
                        pe.wait_ge(turned_out, L * 10 + 6)
                    W_ = P * (b + 1)
                    for h in range(8):
                        r = slice(32 * (h % 4), 32 * (h % 4) + 32)
                        t = mm(ps[:, 4 + h % 4, (h // 4) * TOK:(h // 4) * TOK + W_], iqT[r, h // 4, b * P:b * P + P],
                               ikT[r, 0:W_], start=True, stop=True, skip_group_check=True)
                    t.then_inc(idx_pe, 1)

                def sb_scores():
                    pe.wait_ge(turned_out, L * 10 + 8)
                    pe.wait_ge(relu_done, L * 2 + 2)
                    for h in range(4):
                        r, first = slice(64 * (h % 2), 64 * (h % 2) + 64), h < 2
                        mm(ps[:, 4 + h % 2, (h // 2) * TOK:(h // 2) * TOK + TOK], sbkT[r, h // 2, 0:P], sbqT[r, h // 2, :],
                           start=first, stop=False, skip_group_check=True)
                        t = mm(ps[:, 6 + h % 2, (h // 2) * P:(h // 2) * P + P], sbkT[r, h // 2, P:TOK],
                               sbqT[r, h // 2, P:TOK], start=first, stop=False, skip_group_check=True)
                    t.then_inc(sb_pe, 1)

                def sb_sums():
                    pe.wait_ge(sb_dve, L * 2 + 1)
                    tri, ones = cst[:, C_TRI:C_TRI + P], cst[:, C_ONES:C_ONES + P]
                    for e in range(2):
                        mm(ps[:, 4 + e, :], tri, sb_sp[:, e * 512:e * 512 + 512], start=False, stop=False, skip_group_check=True)
                        own = sb_sp[:, 1024 + e * TOK:1024 + e * TOK + TOK]
                        mm(ps[:, 4 + e, :].rearrange("p (h n) -> p h n", h=2)[:, :, P:TOK], ones,
                           own.rearrange("p (h n) -> p h n", h=2), start=False, stop=True, skip_group_check=True)
                        t = mm(ps[:, 6 + e, 0:TOK], tri, own, start=False, stop=True, skip_group_check=True)
                    t.then_inc(sb_pe, 1)

                def sb_values():
                    pe.wait_ge(sb_dve, L * 2 + 2)
                    for h in range(4):
                        o = ps[64 * (h % 2):64 * (h % 2) + 64, 4, (h // 2) * TOK:(h // 2) * TOK + TOK]
                        s = (h % 2) * 2 + h // 2
                        mm(o, v_sb[:, 0, 64 * h:64 * h + 64], sb_a[:, s * TOK:s * TOK + TOK], start=True, stop=False,
                           skip_group_check=True)
                        t = mm(o[:, P:TOK], v_sb[:, 1, 64 * h:64 * h + 64], sb_a[:, 1024 + s * P:1024 + s * P + P],
                               start=False, stop=True, skip_group_check=True)
                    t.then_inc(sb_pe, 1)

                def mem_turn():
                    pe.wait_ge(mem_in, 16 * (L + 1))
                    pe.wait_ge(br_lo, L * N_BR + BR["dsa1"] + 1)
                    for blk in range(NB):
                        for hf in range(2):
                            for c in range(4):
                                k = 4 * hf + c
                                t = turn(ps[:, 4 + 2 * blk + hf, c * P:c * P + P], memn[:, blk, k * P:k * P + P])
                            t.then_inc(mem_turned, 1)

                def w_in_half(m, blocks=(0, 1)):
                    g, i = m // 4, m % 4
                    n = MIX_COLS[g][1]
                    return half(L, h0 + m, 2 * i, 2, n, lambda blk, c, w: ps[:, 2 * (g % 2) + blk, 0:n], xh, xl, KC, 0, blocks)

                def branch_half(m):
                    n, r = (m - M_GATES) // 10, (m - M_GATES) % 10
                    hf = r // 4 if r < 8 else r - 8
                    dst = lambda blk, c, w: ps[:, 2 * hf + blk, :]
                    if r < 8:
                        if r % 4 == 0 and n == 0:
                            pe.wait_ge(nat_done, L * N_NAT + 4 + (1 - hf))
                        if r % 4 == 0 and n > 0:
                            pe.wait_ge(merge_done, L * N_MRG + 2 * (n - 1) + hf + 1)
                        half(L, h0 + m, 2 * (r % 4), 2, 512, dst, xh, xl, KC)
                    else:
                        b = ORDER[n]
                        pe.wait_ge(nat_done, L * N_NAT + 5 + 2 * n + hf + 1)
                        if hf == 0:
                            pe.wait_ge(br_lo, L * N_BR + BR[("pool", "dsa1", "sb", "swa1")[b]] + 1)
                        half(L, h0 + m, 0, 2, 512, dst, brh[:, b], brl[:, b], 2)

                def m_turn(hf):
                    pe.wait_ge(merge_done, L * N_MRG + N_MRG - 1 + hf)
                    for blk in range(NB):
                        for c in range(4):
                            k = 4 * hf + c
                            t = turn(ps[:, 4 + 2 * hf + blk, c * P:c * P + P], merged[:, blk, k * P:k * P + P])
                        t.then_inc(m_turned, 1)

                def out_half(k, blocks):
                    return half(L, h0 + M_OUT + k, k, 1, D, lambda blk, c, w: ps[:, 2 * blk + c // 512, :], xh, xl, KC, 0,
                                blocks)

                head(L, 1, w_in_half)
                for m in range(SKEW, M_OUT):
                    for j, at in AT_T.items():
                        if m == at:
                            t_wait(j)
                            t_step(j)
                    if m == AT_POOLED:
                        pooled()
                    if m == AT_POOLMIX:
                        pe.wait_ge(mix_out, L * 2 + 1)
                    if m == AT_DKV:
                        dsa_kv()
                    for b in range(NB):
                        if m == AT_IDX[b]:
                            index(b)
                    if m == AT_SB[0]:
                        sb_scores()
                    if m == AT_SB[1]:
                        sb_sums()
                    if m == AT_SB[2]:
                        sb_values()
                    for n, at in enumerate(AT_ATT):
                        if m == at:
                            att_scores(L, n)
                        if m == at + 2:
                            att_turn(L, n)
                        if m == at + 3:
                            att_values(L, n)
                    if m == AT_MEM:
                        mem_turn()
                    if m < M_GATES:
                        if m % 4 == 0 and m >= 8:
                            pe.wait_ge(nat_done, L * N_NAT + m // 4 - 1)
                        w_in_half(m)
                    else:
                        branch_half(m)
                    if m == AT_POOLMIX:
                        pool_mix()
                pe.wait_ge(mem_lo, L * 4 + 4)
                m_turn(0)
                pe.wait_ge(m_lo, L * 4 + 1)
                for k in range(SKEW):
                    if k == SKEW - 1:
                        m_turn(1)
                    out_half(k, (0,))
                pe.wait_ge(m_lo, L * 4 + 2)
                for k in range(SKEW):
                    out_half(k, (1,))
                pe.wait_ge(m_lo, L * 4 + 4)
                tail(L, 1, lambda i, blocks: out_half(SKEW + i, blocks))

            def att_scores(L, n):
                kind, b = ATT[n]
                if n == 0:
                    pe.wait_ge(br_lo, L * N_BR + BR["sb"] + 1)
                elif kind != "x":
                    pe.wait_ge(br_lo, L * N_BR + BR[kind + str(b)])
                W_ = TOK if kind == "x" else P * (b + 1)
                qT, kT = {"swa": (swqT, swkT), "dsa": (dqT, dkT), "x": (xqT, mkT)}[kind]
                for h in range(4):
                    r = slice(64 * (h % 2), 64 * (h % 2) + 64)
                    c = (0 if h % 2 == h // 2 else 1) if kind == "swa" else h // 2
                    t = mm(ps[:, S_BANK[n] + h % 2, (h // 2) * TOK:(h // 2) * TOK + W_], qT[r, h // 2, b * P:b * P + P],
                           kT[r, c, 0:W_], start=True, stop=True, skip_group_check=True)
                t.then_inc(att_s, 1)

            def att_turn(L, n):
                kind, b = ATT[n]
                pe.wait_ge(att_p, L * N_ATT + n + 1)
                for h in range(4):
                    for k in range(2 if kind == "x" else b + 1):
                        t = turn(ps[:, T_BANK[n] + h // 2, (h % 2) * TOK + k * P:(h % 2) * TOK + k * P + P],
                                 scores[n][:, h, k * P:k * P + P])
                t.then_inc(att_t, 1)

            def att_values(L, n):
                kind, b = ATT[n]
                v = {"swa": v_sw, "dsa": v_ds, "x": v_m}[kind]
                K = 2 if kind == "x" else b + 1
                pe.wait_ge(att_tev, L * N_ATT + n + 1)
                for h in range(4):
                    o = ps[64 * (h % 2):64 * (h % 2) + 64, O_BANK[n], (h // 2) * P:(h // 2) * P + P]
                    hv = h // 2 if kind == "swa" else h
                    for k in range(K):
                        t = mm(o, v[:, k, 64 * hv:64 * hv + 64], probsT[n][:, (h % 2) * 2 + h // 2, k, :], start=k == 0,
                               stop=k == K - 1, skip_group_check=True)
                t.then_inc(att_o, 1)

            def memory(L):
                h0 = H_X

                def mem_half(i, blocks=(0, 1)):
                    return half(L, h0 + i, 4 * (i % 2), 4, BW, lambda blk, c, w: ps[:, 4 + blk, 0:BW], memh, meml, KC, 0,
                                blocks)

                def query_half(i, blk):
                    half(L, h0 + 2 + i, 4 * i, 4, BW, lambda blk, c, w: ps[:, 6 + blk, 0:BW], xh, xl, KC, 0, (blk,))

                def nat_turn(j, bank):
                    for c in range(2):
                        for blk in range(NB):
                            t = turn(ps[:, bank, c * TOK + blk * P:c * TOK + blk * P + P], nat[:, j, blk, c * P:c * P + P])
                    t.then_inc(turned, 1)

                def out_half(k, blk):
                    return half(L, h0 + 6 + k, k, 1, D, lambda blk, c, w: ps[:, OUT_BANK[2][blk] + c // 512, :],
                                brh[:, 0], brl[:, 0], 2, 0, (blk,))

                mem_half(0)
                mem_half(1)
                turn_x(L, 2, 1)
                pe.wait_ge(x_lo, L * 16 + 10)
                query_half(0, 0)
                query_half(1, 0)
                pe.wait_ge(x_lo, L * 16 + 12)
                query_half(0, 1)
                query_half(1, 1)
                pe.wait_ge(nat_done, L * N_NAT + N_NAT - 2)
                nat_turn(0, 0)
                mem_half(4)
                pe.wait_ge(nat_done, L * N_NAT + N_NAT - 1)
                nat_turn(1, 1)
                mem_half(5, (0,))
                pe.wait_ge(turned_out, L * 10 + 10)
                att_scores(L, 4)
                att_scores(L, 5)
                mem_half(5, (1,))
                att_turn(L, 4)
                pe.wait_ge(nat_done, L * N_NAT + N_NAT)
                att_values(L, 4)
                att_turn(L, 5)
                pe.wait_ge(br_lo, L * N_BR + BR["x0"] + 1)
                out_half(0, 0)
                out_half(1, 0).then_inc(block0_done, 1)
                att_values(L, 5)
                pe.wait_ge(br_lo, L * N_BR + BR["x1"] + 1)
                out_half(0, 1)
                turn_x(L, 3, 0)
                out_half(1, 1)

            with pe.Fori(0, DEPTH) as L:
                ffn(L, 0, H_FFN1, 0)
                pe.wait_ge(params_in, 16 * N_PAR * (L + 1))
                pe.wait_ge(masks_in, 16 * (L + 1))
                mixer(L)
                memory(L)
                ffn(L, 1, H_FFN2, 3)

        @block.scalar
        def _(act):
            fn = nc.scalar.activation
            act.wait_ge(const_in, 16)

            def hi(L, h, it=0):
                if h >= NH:
                    return
                u, n = h // 2, HALF[h]
                if h % 2 == 0:
                    act.wait_ge(raw_in[u % RAW], 32 * (L * (NU // RAW) + u // RAW + 1 + it))
                act.wait_ge(half_done, L * NH + h + 1 + it * 8)
                fn(wh[:, h % SPL, 0:n], raw[:, u % RAW, (h % 2) * n:(h % 2) * n + n], ACT.Copy).then_inc(hi_done, 1)

            def group_done(L, h, it=0):
                act.wait_ge(half_done, L * NH + h + 1 + SPL + it * 8)

            def square(L, src, name, n=D):
                q = RQ[name]
                if q > 0:
                    act.wait_ge(squared, L * NRQ + q)
                fn(junk[:, 0:n], src, ACT.Square, accum_out=ssq[:, q:q + 1]).then_inc(squared, 1)

            def x_high(L, b, blk):
                gi = (0, 1, 2, 4)[b]
                for hf in range(2):
                    act.wait_ge(x_turned, L * 16 + b * 4 + 2 * blk + hf + 1)
                    for c in range(4):
                        k = 4 * hf + c
                        t = fn(xh[:, k, blk * P:blk * P + P], ps[:, OUT_BANK[b - 1][blk] + hf, c * P:c * P + P], ACT.Copy,
                               scale=gT[:, gi, k:k + 1])
                    t.then_inc(x_hi, 1)

            def pre_squares(L, b):
                for blk in range(NB):
                    square(L, x[:, blk], f"pre{b}_{blk}")

            def post_square(L, k, h_last, blk):
                if blk == 0:
                    act.wait_ge(block0_done, L * 4 + k + 1)
                else:
                    group_done(L, h_last)
                square(L, wide(OUT_BANK[k][blk]), f"post{k}_{blk}")

            def between(L, k, h0):
                hi(L, h0 + 3)
                post_square(L, k, h0 - 1, 0)
                for i in (4, 5, 6):
                    hi(L, h0 + i)
                x_high(L, k + 1, 0)
                post_square(L, k, h0 - 1, 1)
                hi(L, h0 + 7)
                x_high(L, k + 1, 1)
                pre_squares(L, k + 1)

            def ffn(L, f, h0, b):
                E = (L * 2 + f) * NG

                def silu(g, it=0):
                    group_done(L, h0 + 4 * g + 3, it)
                    if g == 0:
                        act.wait_ge(rms_ready, L * NRQ + RQ[f"pre{b}_1"] + 1)
                    if g >= 2 or not isinstance(it, int):
                        act.wait_ge(act_done, E + g - 1 + it * 2)
                    for blk in range(NB):
                        t = fn(sg[:, g % 2, blk], ps[:, 2 * (g % 2) + blk, 0:FG], ACT.Silu, scale=rs(f"pre{b}_{blk}"))
                    t.then_inc(silu_done, 1)

                def high(g, it=0):
                    bank = 2 if g == NG - 1 else 4 + g % 2
                    act.wait_ge(act_turned, E + g + 1 + it * 2)
                    k = 2 * g + 4 * it if not isinstance(it, int) else 2 * g
                    fn(ah[:, bass.ds(k, 2), :] if not isinstance(it, int) else ah[:, k:k + 2, :],
                       ps[:, bank, :].rearrange("p (c t) -> p c t", c=2), ACT.Copy).then_inc(act_hi, 1)

                for i in (8, 9, 10):
                    hi(L, h0 + i)

                def group(g, it=0):
                    silu(g - 1, it)
                    hi(L, h0 + 4 * g + AHEAD, it)
                    hi(L, h0 + 4 * g + 1 + AHEAD, it)
                    high(g - 1, it)
                    hi(L, h0 + 4 * g + 2 + AHEAD, it)
                    hi(L, h0 + 4 * g + 3 + AHEAD, it)
                group(1)
                group(2)
                with act.Fori(0, (NG - 3) // 2) as it:
                    group(3, it)
                    group(4, it)
                hd = h0 + 4 * NG
                silu(NG - 1)
                hi(L, hd + AHEAD)
                hi(L, hd + 1 + AHEAD)
                high(NG - 1)
                for c in range(2, FC - SKEW):
                    hi(L, hd + c + AHEAD)

            def branch_high(L, name, dst, src, scale=1.0):
                fn(dst, src, ACT.Copy, scale=scale).then_inc(br_hi, 1)

            def att_exp_step(L, n):
                kind, b = ATT[n]
                r = b if kind == "x" else 0
                W_ = TOK if kind == "x" else P * (b + 1)
                act.wait_ge(att_max, L * N_ATT + n + 1)
                for h in range(4):
                    if kind == "x":
                        src, scale = ps[:, S_BANK[n] + h // 2, (h % 2) * TOK:(h % 2) * TOK + TOK], 0.125
                    else:
                        src, scale = sc[:, h, 0:W_], 1.0
                    t = fn(scores[n][:, h, 0:W_], src, ACT.Exp, bias=nmx[:, r, h:h + 1], scale=scale,
                           accum_out=den[:, r, h:h + 1])
                if kind == "swa":
                    for h in range(4):
                        at = (h % 2) * 2 + h // 2
                        t = fn(esk[:, at:at + 1], snk[:, h:h + 1], ACT.Exp, bias=nmx[:, 0, at:at + 1])
                t.then_inc(att_exp, 1)

            def att_high(L, n):
                kind, b = ATT[n]
                i = {"swa": 3, "dsa": 1, "x": 0}[kind]
                act.wait_ge(att_o, L * N_ATT + n + 1)
                branch_high(L, kind + str(b), brh[:, i, :, b * P:b * P + P],
                            ps[:, O_BANK[n], 0:TOK].rearrange("p (c t) -> p c t", c=2))

            def mixer(L):
                h0 = H_MIX

                def natural(g):
                    group_done(L, h0 + 4 * g + 3)
                    bank = 2 * (g % 2)
                    if g == 0:
                        act.wait_ge(rms_ready, L * NRQ + RQ["pre1_1"] + 1)
                    if g == 2:
                        act.wait_ge(turned, L * 10 + 1)
                    if g == 3:
                        act.wait_ge(turned, L * 10 + 4)
                    if g == 4:
                        act.wait_ge(sel_done, L * 2 + 2)
                    for blk in range(NB):
                        src, r = ps[:, bank + blk, :], rs(f"pre1_{blk}")
                        if g == 0:
                            t = fn(u_n[:, blk], src[:, 0:256], ACT.Copy, scale=r)
                            t = fn(nat[:, 0, blk, 256:512], src[:, 256:512], ACT.Copy, scale=r)
                        elif g == 1:
                            t = fn(nat[:, 1, blk, 0:424], src[:, 0:424], ACT.Copy, scale=r)
                            for k in range(4):
                                t = fn(ikr[:, blk, k], src[:, 384:416], ACT.Copy, scale=r)
                        elif g == 2:
                            t = fn(nat[:, 0, blk], src, ACT.Copy, scale=r)
                        elif g == 3:
                            t = fn(v_sb[:, blk], src[:, 0:256], ACT.Copy, scale=r)
                            t = fn(nat[:, 1, blk, 256:512], src[:, 256:512], ACT.Copy, scale=r)
                        else:
                            fn(swkr[:, blk, 0], src[:, 0:128], ACT.Copy, scale=r)
                            fn(swkr[:, blk, 1, 0:64], src[:, 64:128], ACT.Copy, scale=r)
                            fn(swkr[:, blk, 1, 64:128], src[:, 0:64], ACT.Copy, scale=r)
                            t = fn(v_sw[:, blk], src[:, 128:256], ACT.Copy, scale=r)
                    t.then_inc(nat_done, 1)

                def gates(n, hf):
                    group_done(L, h0 + M_GATES + 10 * n + 4 * hf + 3)
                    if n == 0 and hf == 0:
                        act.wait_ge(half_rms, L + 1)
                    for blk in range(NB):
                        t = fn(gate[:, hf, blk], ps[:, 2 * hf + blk, :], ACT.Tanh, scale=hrs[:, blk:blk + 1])
                    t.then_inc(nat_done, 1)

                def c_square():
                    act.wait_ge(nat_done, L * N_NAT + 2)
                    for blk in range(NB):
                        square(L, nat[:, 1, blk, 0:P], f"c_{blk}", P)

                def c_norm():
                    act.wait_ge(rms_ready, L * NRQ + RQ["c_1"] + 1)
                    for blk in range(NB):
                        t = fn(cn[:, blk], nat[:, 1, blk, 0:P], ACT.Copy, scale=rs(f"c_{blk}"))
                    t.then_inc(act_link, 1)

                def relu_step(b):
                    W_ = P * (b + 1)
                    act.wait_ge(idx_pe, L * 2 + b + 1)
                    if b == 1:
                        act.wait_ge(sel_done, L * 2 + 1)
                    t = fn(relu[:, :, 0:W_], ps[:, 4:8, :].rearrange("p b (h n) -> p (b h) n", h=2)[:, :, 0:W_], ACT.Relu,
                           scale=32.0 ** -0.5)
                    t.then_inc(relu_done, 1)

                def sb_softplus():
                    parts = ((sb_sp[:, 0:1024], wide(4)),
                             (sb_sp[:, 1024:1536].rearrange("p (e n) -> p e n", e=2), ps[:, 6:8, 0:TOK]))
                    act.wait_ge(sb_pe, L * 3 + 1)
                    act.wait_ge(sel_done, L * 2 + 2)
                    for dst, z in parts:
                        t = fn(dst, z, ACT.Abs)
                    t.then_inc(act_link, 1)
                    act.wait_ge(act_link, L * N_ALINK + 2)
                    fn(sb_sp[:], sb_sp[:], ACT.Exp, scale=-1.0).then_inc(act_link, 1)
                    act.wait_ge(act_link, L * N_ALINK + 3)
                    fn(sb_sp[:], sb_sp[:], ACT.Ln, bias=1.0).then_inc(sb_act, 1)

                def sb_exp():
                    act.wait_ge(sb_pe, L * 3 + 2)
                    fn(sb_a[:, 0:1024], wide(4), ACT.Exp)
                    fn(sb_a[:, 1024:1536].rearrange("p (e n) -> p e n", e=2), ps[:, 6:8, 0:TOK], ACT.Exp).then_inc(sb_act, 1)

                def sb_high():
                    act.wait_ge(sb_pe, L * 3 + 3)
                    branch_high(L, "sb", brh[:, 2], ps[:, 4, :].rearrange("p (c t) -> p c t", c=2))

                def pool_high():
                    act.wait_ge(mix_pe, L * 3 + 2)
                    for c in range(2):
                        t = fn(brh[:, 0, c], ps[:, 7, c * TOK:c * TOK + TOK], ACT.Copy, scale=psc[:, c:c + 1])
                    t.then_inc(br_hi, 1)

                def memory_high(j):
                    act.wait_ge(mem_turned, L * 4 + j + 1)
                    for c in range(4):
                        k, blk = 4 * (j % 2) + c, j // 2
                        t = fn(memh[:, k, blk * P:blk * P + P], ps[:, 4 + j, c * P:c * P + P], ACT.Copy,
                               scale=gT[:, 3, k:k + 1])
                    t.then_inc(mem_hi, 1)

                def merged_high(j):
                    act.wait_ge(m_turned, L * 4 + j + 1)
                    k, blk = 4 * (j // 2), j % 2
                    fn(xh[:, k:k + 4, blk * P:blk * P + P], ps[:, 4 + j, :].rearrange("p (c t) -> p c t", c=4), ACT.Copy,
                       scale=0.5).then_inc(m_hi, 1)

                for m in range(1, M_OUT):
                    if m % 4 == 0 and 0 < m <= M_GATES:
                        natural(m // 4 - 1)
                        if m == 8:
                            c_square()
                    if m > M_GATES and (m - M_GATES) % 10 in (4, 8):
                        gates((m - M_GATES) // 10, (m - M_GATES) % 10 // 4 - 1)
                    hi(L, h0 + m + AHEAD)
                    if m == 9:
                        c_norm()
                    if m == AT_POOLMIX + 1:
                        pool_high()
                    for b in range(NB):
                        if m == AT_IDX[b]:
                            relu_step(b)
                    if m == AT_SB[0]:
                        sb_softplus()
                    if m == AT_SB[1]:
                        sb_exp()
                    if m == AT_SB[2]:
                        sb_high()
                    for n, at in enumerate(AT_ATT):
                        if m == at:
                            att_exp_step(L, n)
                        if m == at + 3:
                            att_high(L, n)
                    if AT_MEM <= m < AT_MEM + 4:
                        memory_high(m - AT_MEM)
                    if AT_MEM + 5 <= m < AT_MEM + 7:
                        blk = m - AT_MEM - 5
                        square(L, memn[:, blk], f"mem_{blk}")
                merged_high(0)
                merged_high(1)
                hi(L, h0 + M_OUT + AHEAD)
                merged_high(2)
                merged_high(3)
                for m in range(M_OUT + 1, M_OUT + SKEW):
                    hi(L, h0 + m + AHEAD)

            def memory(L):
                h0 = H_X

                def natural(h, dst, bank, name):
                    group_done(L, h)
                    act.wait_ge(rms_ready, L * NRQ + RQ[name + "_1"] + 1)
                    for blk in range(NB):
                        t = fn(dst[:, blk, 0:BW], ps[:, bank + blk, 0:BW], ACT.Copy, scale=rs(f"{name}_{blk}"))
                    t.then_inc(nat_done, 1)

                natural(h0 + 1, nat[:, 0], 4, "mem")
                hi(L, h0 + 8)
                hi(L, h0 + 9)
                natural(h0 + 3, nat[:, 1], 6, "pre2")
                hi(L, h0 + 10)
                hi(L, h0 + 11)
                hi(L, h0 + 12)
                att_exp_step(L, 4)
                natural(h0 + 5, v_m, 4, "mem")
                att_exp_step(L, 5)
                hi(L, h0 + 13)
                att_high(L, 4)
                h3 = H_FFN2
                post_square(L, 2, h3 - 1, 0)
                att_high(L, 5)
                hi(L, h3 + 6)
                x_high(L, 3, 0)
                post_square(L, 2, h3 - 1, 1)
                hi(L, h3 + 7)
                x_high(L, 3, 1)
                pre_squares(L, 3)

            with act.Fori(0, DEPTH) as L:
                act.wait_ge(gain_in, 16 * (L + 1))
                hi(L, 0)
                hi(L, 1)
                x_high(L, 0, 0)
                for h in range(2, AHEAD):
                    hi(L, h)
                x_high(L, 0, 1)
                hi(L, AHEAD)
                pre_squares(L, 0)
                ffn(L, 0, H_FFN1, 0)
                act.wait_ge(params_in, 16 * N_PAR * (L + 1))
                between(L, 0, H_MIX)
                mixer(L)
                between(L, 1, H_X)
                memory(L)
                ffn(L, 1, H_FFN2, 3)
                post_square(L, 3, NH - 1, 0)
                post_square(L, 3, NH - 1, 1)
                act.wait_ge(squared, L * NRQ + NRQ)
                act.wait_ge(x_in, 16 * NB)

        @block.vector
        def _(dve):
            v = nc.vector
            dve.sem_inc(split_done, 2 * RAW)
            dve.wait_ge(const_in, 16)
            dve.wait_ge(x_in, 16 * NB)
            dve.sem_inc(x_new, NB)
            links = [0]

            def link(L, ins):
                links[0] += 1
                ins.then_inc(dve_link, 1)
                dve.wait_ge(dve_link, L * N_VLINK + links[0])

            def lo(L, h, it=0):
                if h >= NH:
                    return
                u, n = h // 2, HALF[h]
                dve.wait_ge(hi_done, L * NH + h + 1 + it * 8)
                v.tensor_tensor(wl[:, h % SPL, 0:n], raw[:, u % RAW, (h % 2) * n:(h % 2) * n + n],
                                wh[:, h % SPL, 0:n].bitcast(F32), ALU.subtract).then_inc(split_done, 1)

            def x_low(L, b, blk):
                gi = (0, 1, 2, 4)[b]
                for hf in range(2):
                    dve.wait_ge(x_hi, L * 16 + b * 4 + 2 * blk + hf + 1)
                    for c in range(4):
                        k = 4 * hf + c
                        s = slice(blk * P, blk * P + P)
                        t = v.scalar_tensor_tensor(xl[:, k, s], ps[:, OUT_BANK[b - 1][blk] + hf, c * P:c * P + P],
                                                   gT[:, gi, k:k + 1], xh[:, k, s].bitcast(F32), ALU.mult, ALU.subtract)
                    t.then_inc(x_lo, 1)

            def post_gain(L, k, blk):
                if blk == 0:
                    dve.wait_ge(gbc_in, 16 * (L * 4 + k + 1))
                dve.wait_ge(squared, L * NRQ + RQ[f"post{k}_{blk}"] + 1)
                v.tensor_tensor(yg[:, blk], wide(OUT_BANK[k][blk]), gbc[:], ALU.mult).then_inc(gained, 1)

            def post_add(L, k, blk):
                dve.wait_ge(rms_ready, L * NRQ + RQ[f"post{k}_{blk}"] + 1)
                dve.wait_ge(gained, L * 8 + 2 * k + blk + 1)
                v.scalar_tensor_tensor(x[:, blk], yg[:, blk], rs(f"post{k}_{blk}"), x[:, blk], ALU.mult,
                                       ALU.add).then_inc(x_new, 1)

            def between(L, k, h0):
                lo(L, h0 + 3)
                post_gain(L, k, 0)
                post_add(L, k, 0)
                lo(L, h0 + 4)
                x_low(L, k + 1, 0)
                lo(L, h0 + 5)
                lo(L, h0 + 6)
                post_gain(L, k, 1)
                post_add(L, k, 1)
                lo(L, h0 + 7)
                x_low(L, k + 1, 1)

            def ffn(L, f, h0, b):
                E = (L * 2 + f) * NG

                def hidden(g, it=0):
                    dve.wait_ge(silu_done, E + g + 1 + it * 2)
                    if g >= 2 or not isinstance(it, int):
                        dve.wait_ge(act_turned, E + g - 1 + it * 2)
                    for blk in range(NB):
                        t = v.scalar_tensor_tensor(an[:, g % 2, blk], ps[:, 2 * (g % 2) + blk, FG:2 * FG],
                                                   rs(f"pre{b}_{blk}"), sg[:, g % 2, blk], ALU.mult, ALU.mult)
                    t.then_inc(act_done, 1)

                def low(g, it=0):
                    bank = 2 if g == NG - 1 else 4 + g % 2
                    dve.wait_ge(act_hi, E + g + 1 + it * 2)
                    k = 2 * g + 4 * it if not isinstance(it, int) else 2 * g
                    s = bass.ds(k, 2) if not isinstance(it, int) else slice(k, k + 2)
                    v.tensor_tensor(al[:, s, :], ps[:, bank, :].rearrange("p (c t) -> p c t", c=2),
                                    ah[:, s, :].bitcast(F32), ALU.subtract).then_inc(act_lo, 1)

                for i in (8, 9, 10):
                    lo(L, h0 + i)

                def group(g, it=0):
                    hidden(g - 1, it)
                    lo(L, h0 + 4 * g + AHEAD, it)
                    lo(L, h0 + 4 * g + 1 + AHEAD, it)
                    low(g - 1, it)
                    lo(L, h0 + 4 * g + 2 + AHEAD, it)
                    lo(L, h0 + 4 * g + 3 + AHEAD, it)
                group(1)
                group(2)
                with dve.Fori(0, (NG - 3) // 2) as it:
                    group(3, it)
                    group(4, it)
                hd = h0 + 4 * NG
                hidden(NG - 1)
                lo(L, hd + AHEAD)
                lo(L, hd + 1 + AHEAD)
                low(NG - 1)
                for c in range(2, FC - SKEW):
                    lo(L, hd + c + AHEAD)

            def turned_copy(L, j, dst, src):
                dve.wait_ge(turned, L * 10 + j + 1)
                if j == 3:
                    v.tensor_scalar(dst, src, kvn[:, 0:1], None, ALU.mult).then_inc(turned_out, 1)
                elif j == 4:
                    v.tensor_scalar(dst, src, 0.125, None, ALU.mult).then_inc(turned_out, 1)
                else:
                    v.tensor_copy(dst, src).then_inc(turned_out, 1)

            def att_mask(L, n):
                kind, b = ATT[n]
                W_ = P * (b + 1)
                dve.wait_ge(att_s, L * N_ATT + n + 1)
                if kind == "dsa":
                    dve.wait_ge(sel_done, L * 2 + 2)
                src = wide(S_BANK[n]).rearrange("p (h n) -> p h n", h=4)
                for k in range(b + 1):
                    s = slice(k * P, k * P + P)
                    if kind == "dsa":
                        m = dmask[:, b, s]
                    else:
                        m = cst[:, C_CAUS:C_CAUS + P] if k == b else cst[:, C_WIN:C_WIN + P]
                    t = v.scalar_tensor_tensor(sc[:, :, s], src[:, :, s], 0.125,
                                               m.unsqueeze(1).to_broadcast([P, 4, P]), ALU.mult, ALU.add)
                link(L, t)
                link(L, v.tensor_reduce(nmx[:, 0], sc[:, :, 0:W_], AX, ALU.max))
                if kind == "swa":
                    m = nmx[:, 0].rearrange("p (r c) -> p r c", r=2)
                    link(L, v.tensor_tensor(m, m, snk[:].rearrange("p (c r) -> p r c", r=2), ALU.max))
                v.tensor_scalar(nmx[:, 0], nmx[:, 0], -1.0, None, ALU.mult).then_inc(att_max, 1)

            def read_max(L, n):
                b = ATT[n][1]
                dve.wait_ge(att_s, L * N_ATT + n + 1)
                link(L, v.tensor_reduce(nmx[:, b], wide(S_BANK[n]).rearrange("p (h n) -> p h n", h=4), AX, ALU.max))
                v.tensor_scalar(nmx[:, b], nmx[:, b], -0.125, None, ALU.mult).then_inc(att_max, 1)

            def att_norm(L, n):
                kind, b = ATT[n]
                r = b if kind == "x" else 0
                W_ = TOK if kind == "x" else P * (b + 1)
                dve.wait_ge(att_exp, L * N_ATT + n + 1)
                if kind == "swa":
                    link(L, v.tensor_tensor(den[:, 0], den[:, 0], esk[:], ALU.add))
                link(L, v.reciprocal(rcp[:, r], den[:, r]))
                v.tensor_tensor(scores[n][:, :, 0:W_], scores[n][:, :, 0:W_],
                                rcp[:, r].unsqueeze(2).to_broadcast([P, 4, W_]), ALU.mult).then_inc(att_p, 1)

            def att_pT(L, n):
                kind, b = ATT[n]
                K = 2 if kind == "x" else b + 1
                dve.wait_ge(att_t, L * N_ATT + n + 1)
                v.tensor_copy(probsT[n][:, :, 0:K, :],
                              wide(T_BANK[n]).rearrange("p (h k n) -> p h k n", h=4, k=2)[:, :, 0:K, :]).then_inc(att_tev, 1)

            def att_low(L, n):
                kind, b = ATT[n]
                i = {"swa": 3, "dsa": 1, "x": 0}[kind]
                dve.wait_ge(br_hi, L * N_BR + BR[kind + str(b)] + 1)
                s = slice(b * P, b * P + P)
                v.tensor_tensor(brl[:, i, :, s], ps[:, O_BANK[n], 0:TOK].rearrange("p (c t) -> p c t", c=2),
                                brh[:, i, :, s].bitcast(F32), ALU.subtract).then_inc(br_lo, 1)

            def mixer(L):
                h0 = H_MIX

                def half_factors():
                    for blk in range(NB):
                        if blk == 0:
                            dve.wait_ge(rms_ready, L * NRQ + RQ["pre1_1"] + 1)
                        t = v.tensor_scalar(hrs[:, blk:blk + 1], rs(f"pre1_{blk}"), 0.5, None, ALU.mult)
                    t.then_inc(half_rms, 1)

                def index(b):
                    W_ = P * (b + 1)
                    dve.wait_ge(relu_done, L * 2 + b + 1)
                    link(L, v.tensor_scalar(score[:, 0:W_], relu[:, 0, 0:W_], iw[:, b, 0:1], None, ALU.mult))
                    for s in range(1, 8):
                        h = s // 2 + 4 * (s % 2)
                        link(L, v.scalar_tensor_tensor(score[:, 0:W_], relu[:, s, 0:W_], iw[:, b, h:h + 1],
                                                       score[:, 0:W_], ALU.mult, ALU.add))
                    link(L, v.tensor_tensor(score[:, b * P:b * P + P], score[:, b * P:b * P + P],
                                            cst[:, C_CAUS:C_CAUS + P], ALU.add))

                def rounds(b, n):
                    W_ = P * (b + 1)
                    for _ in range(n):
                        v.memset(carry[:], 0.0)
                        link(L, v.max(top8[:], score[:, 0:W_]))
                        v.memset(carry[:], 0.0)
                        link(L, v.match_replace(score[:, 0:W_], top8[:], score[:, 0:W_], TAKEN))

                def chosen(b):
                    W_ = P * (b + 1)
                    link(L, v.tensor_scalar(dmask[:, b, 0:W_], score[:, 0:W_], TAKEN / 2, NEG, ALU.is_gt, ALU.mult))
                    v.tensor_tensor(dmask[:, b, b * P:b * P + P], dmask[:, b, b * P:b * P + P],
                                    cst[:, C_CAUS:C_CAUS + P], ALU.add).then_inc(sel_done, 1)

                def strict_mask(t):
                    m = cst[:, C_STRICT:C_STRICT + P].unsqueeze(1).to_broadcast([P, 4, P])
                    d0 = t[:, 0:1024].rearrange("p (h n) -> p h n", h=4)[:, :, 0:P]
                    d1 = t[:, 1024:1536].rearrange("p (h n) -> p h n", h=4)
                    v.tensor_tensor(d0, d0, m, ALU.mult)
                    return v.tensor_tensor(d1, d1, m, ALU.mult)

                def merge(n, hf):
                    dve.wait_ge(half_done, L * NH + h0 + M_GATES + 10 * n + 8 + hf + 1 + SPL)
                    dve.wait_ge(nat_done, L * N_NAT + 5 + 2 * n + hf + 1)
                    if n > 0:
                        dve.wait_ge(merge_done, L * N_MRG + 2 * n + hf)
                    s = slice(hf * 512, hf * 512 + 512)
                    for blk in range(NB):
                        dst = merged[:, blk, s] if n == 0 else tmp[:, blk]
                        t = v.scalar_tensor_tensor(dst, gate[:, hf, blk], 1.0, ps[:, 2 * hf + blk, :], ALU.add, ALU.mult)
                    if n > 0:
                        link(L, t)
                        for blk in range(NB):
                            t = v.tensor_tensor(merged[:, blk, s], merged[:, blk, s], tmp[:, blk], ALU.add)
                    t.then_inc(merge_done, 1)

                def memory_low(j):
                    dve.wait_ge(mem_hi, L * 4 + j + 1)
                    for c in range(4):
                        k, blk = 4 * (j % 2) + c, j // 2
                        s = slice(blk * P, blk * P + P)
                        t = v.scalar_tensor_tensor(meml[:, k, s], ps[:, 4 + j, c * P:c * P + P], gT[:, 3, k:k + 1],
                                                   memh[:, k, s].bitcast(F32), ALU.mult, ALU.subtract)
                    t.then_inc(mem_lo, 1)

                def merged_low(j):
                    dve.wait_ge(m_hi, L * 4 + j + 1)
                    k, s = 4 * (j // 2), slice((j % 2) * P, (j % 2) * P + P)
                    v.scalar_tensor_tensor(xl[:, k:k + 4, s], ps[:, 4 + j, :].rearrange("p (c t) -> p c t", c=4), 0.5,
                                           xh[:, k:k + 4, s].bitcast(F32), ALU.mult, ALU.subtract).then_inc(m_lo, 1)

                half_factors()
                for m in range(1, M_OUT):
                    if m == 8:
                        dve.wait_ge(nat_done, L * N_NAT + 2)
                        for b in range(NB):
                            link(L, v.tensor_scalar(iw[:, b], nat[:, 1, b, 416:424], 8.0 ** -0.5, None, ALU.mult))
                    for j, at in AT_T.items():
                        if m == at:
                            dst = (dqT, iqT, ikT, cT, sbqT, sbkT, swqT, swkT)[j]
                            src = ps[:, 4 + j % 2, :]
                            if j in (2, 3):
                                turned_copy(L, j, dst[:], src[:, 0:TOK])
                            else:
                                turned_copy(L, j, dst[:], src.rearrange("p (c t) -> p c t", c=2))
                    if m == AT_POOLED:
                        dve.wait_ge(mix_pe, L * 3 + 1)
                        v.tensor_copy(poT[:], ps[:, 6, :].rearrange("p (c t) -> p c t", c=2)).then_inc(mix_out, 1)
                    if m == AT_POOLMIX + 1:
                        dve.wait_ge(br_hi, L * N_BR + BR["pool"] + 1)
                        for c in range(2):
                            t = v.scalar_tensor_tensor(brl[:, 0, c], ps[:, 7, c * TOK:c * TOK + TOK], psc[:, c:c + 1],
                                                       brh[:, 0, c].bitcast(F32), ALU.mult, ALU.subtract)
                        t.then_inc(br_lo, 1)
                    if m == AT_DKV:
                        dve.wait_ge(mix_pe, L * 3 + 3)
                        v.tensor_copy(dkT[:], ps[:, 4, :].rearrange("p (c t) -> p c t", c=2))
                        v.tensor_copy(v_ds[:], ps[:, 5, :].rearrange("p (c t) -> p c t", c=2)).then_inc(mix_out, 1)
                    for b in range(NB):
                        if m == AT_IDX[b]:
                            index(b)
                        if AT_IDX[b] < m <= AT_IDX[b] + 2:
                            rounds(b, 4)
                        if m == AT_IDX[b] + 2:
                            chosen(b)
                    if m == AT_SB[0] + 1:
                        dve.wait_ge(sb_act, L * 2 + 1)
                        v.scalar_tensor_tensor(sb_sp[:, 0:1024], wide(4), 0.0, sb_sp[:, 0:1024], ALU.max, ALU.add)
                        own = sb_sp[:, 1024:1536].rearrange("p (e n) -> p e n", e=2)
                        link(L, v.scalar_tensor_tensor(own, ps[:, 6:8, 0:TOK], 0.0, own, ALU.max, ALU.add))
                        strict_mask(sb_sp).then_inc(sb_dve, 1)
                    if m == AT_SB[1]:
                        dve.wait_ge(sb_act, L * 2 + 2)
                        strict_mask(sb_a).then_inc(sb_dve, 1)
                    if m == AT_SB[2]:
                        dve.wait_ge(br_hi, L * N_BR + BR["sb"] + 1)
                        v.tensor_tensor(brl[:, 2], ps[:, 4, :].rearrange("p (c t) -> p c t", c=2),
                                        brh[:, 2].bitcast(F32), ALU.subtract).then_inc(br_lo, 1)
                    if m > M_GATES and (m - M_GATES) % 10 in (0, 9):
                        merge((m - M_GATES - 9) // 10, 0 if (m - M_GATES) % 10 == 9 else 1)
                    for n, at in enumerate(AT_ATT):
                        if m == at:
                            att_mask(L, n)
                        if m == at + 2:
                            att_pT(L, n)
                        if m == at + 3:
                            att_low(L, n)
                    lo(L, h0 + m + AHEAD)
                    for n, at in enumerate(AT_ATT):
                        if m == at:
                            att_norm(L, n)
                    if AT_MEM <= m < AT_MEM + 4:
                        memory_low(m - AT_MEM)
                merged_low(0)
                merged_low(1)
                merge(3, 1)
                lo(L, h0 + M_OUT + AHEAD)
                merged_low(2)
                merged_low(3)
                for m in range(M_OUT + 1, M_OUT + SKEW):
                    lo(L, h0 + m + AHEAD)

            def memory(L):
                h0 = H_X
                lo(L, h0 + 8)
                lo(L, h0 + 9)
                turned_copy(L, 8, mkT[:], ps[:, 0, :].rearrange("p (c t) -> p c t", c=2))
                turned_copy(L, 9, xqT[:], ps[:, 1, :].rearrange("p (c t) -> p c t", c=2))
                lo(L, h0 + 10)
                lo(L, h0 + 11)
                read_max(L, 4)
                lo(L, h0 + 12)
                read_max(L, 5)
                att_norm(L, 4)
                att_pT(L, 4)
                att_norm(L, 5)
                lo(L, h0 + 13)
                att_low(L, 4)
                att_pT(L, 5)
                post_gain(L, 2, 0)
                att_low(L, 5)
                post_add(L, 2, 0)
                lo(L, h0 + 14)
                x_low(L, 3, 0)
                post_gain(L, 2, 1)
                post_add(L, 2, 1)
                lo(L, h0 + 15)
                x_low(L, 3, 1)

            with dve.Fori(0, DEPTH) as L:
                dve.wait_ge(gain_in, 16 * (L + 1))
                lo(L, 0)
                lo(L, 1)
                x_low(L, 0, 0)
                for h in range(2, AHEAD):
                    lo(L, h)
                x_low(L, 0, 1)
                lo(L, AHEAD)
                ffn(L, 0, H_FFN1, 0)
                dve.wait_ge(params_in, 16 * N_PAR * (L + 1))
                dve.wait_ge(masks_in, 16 * (L + 1))
                between(L, 0, H_MIX)
                mixer(L)
                between(L, 1, H_X)
                memory(L)
                ffn(L, 1, H_FFN2, 3)
                for blk in range(NB):
                    post_gain(L, 3, blk)
                    post_add(L, 3, blk)
            assert links[0] == N_VLINK, links[0]


_INS = ("x", "mem", "ffn1_pre", "ffn1_w_up", "ffn1_w_down", "ffn1_post", "mix_pre", "w_in", "pool_w", "pool_scale",
        "dsa_kv_norm", "dsa_w_uk", "dsa_w_uv", "swa_sinks", "w_branch", "w_out", "mix_post", "xattn_pre", "mem_norm",
        "xattn_w_q", "xattn_w_kv", "xattn_w_o", "xattn_post", "ffn2_pre", "ffn2_w_up", "ffn2_w_down", "ffn2_post")


def kernel(**inputs):
    import numpy as _np
    import concourse.bacc as _bacc
    from concourse import mybir as _mybir
    from concourse.bass_utils import run_bass_kernel_spmd as _run

    nc = _bacc.Bacc("TRN2", target_bir_lowering=False, num_devices=1)
    arrays, args = {}, {}
    for name in _INS + ("consts",):
        a = constants() if name == "consts" else _np.ascontiguousarray(inputs[name])
        arrays[f"in_{name}"] = a
        args[name] = nc.dram_tensor(f"in_{name}", a.shape, _mybir.dt.from_np(a.dtype), kind="ExternalInput").ap()
    out = nc.dram_tensor("out_x", (1, TOK, D), F32, kind="ExternalOutput").ap()
    trunk(nc, args, out)
    r = _run(nc, [arrays], core_ids=[0])
    return r.results[0]["out_x"]
```

```python
from contextlib import ExitStack

import concourse.bass as bass
from concourse import mybir
import numpy as np

P = 128
F32 = mybir.dt.float32
F32R = mybir.dt.float32r
ALU = mybir.AluOpType
ACT = mybir.ActivationFunctionType
AX = mybir.AxisListType.X

DEPTH = 2
TOK = 256
NB = TOK // P
D = 1024
KC = D // P
F = 2816
FG = 256
NG = F // FG
FC = F // P
BW = 256
EPS = 1e-6
NEG = -1e30
TAKEN = -3e38
TOPK = 64
WINDOWS = (2, 4, 8, 16)

H_FFN1 = 0
H_MIX = H_FFN1 + 4 * NG + FC
MIX_COLS = ((0, 512), (512, 424), (936, 512), (1448, 512), (1960, 256)) + tuple(
    (2216 + 512 * g, 512) for g in range(8))
NMG = len(MIX_COLS)
ORDER = (0, 2, 3, 1)
M_GATES = 20
M_OUT = M_GATES + 10 * len(ORDER)
H_X = H_MIX + M_OUT + 8
H_FFN2 = H_X + 8
NH = H_FFN2 + 4 * NG + FC
NU = NH // 2
RAW = 4
SPL = 8
AHEAD = SPL - 1
SKEW = 4
assert NU % RAW == 0 and NH % SPL == 0

HALF = [1024] * NH
for _g in range(5):
    for _i in range(4):
        HALF[H_MIX + 4 * _g + _i] = 2 * MIX_COLS[_g][1]

RQ = {n: i for i, n in enumerate([
    "pre0_0", "pre0_1", "post0_0", "post0_1", "pre1_0", "pre1_1", "c_0", "c_1", "mem_0", "mem_1",
    "post1_0", "post1_1", "pre2_0", "pre2_1", "post2_0", "post2_1", "pre3_0", "pre3_1", "post3_0", "post3_1"])}
NRQ = len(RQ)

AT_T = {0: 6, 1: 10, 2: 10, 3: 11, 4: 15, 5: 15, 6: 19, 7: 22}
AT_POOLED, AT_POOLMIX = 7, 8
AT_DKV = 12
AT_IDX = (13, 17)
ROUNDS = ({14: 2, 15: 3, 16: 3}, {24: 4, 27: 2, 31: 2})
AT_SB = (24, 28, 30)
AT_ATT = (32, 36, 41, 45)
AT_MEM = 53

C_ID, C_SC, C_TRI, C_ONES, C_STRICT, C_CAUS, C_WIN = 0, 128, 136, 264, 392, 520, 648
N_FIRST, N_CONST = C_TRI, 776
N_BAND = 12 * P
K_INVD, K_INVC, K_INVD4, K_EPS, K_EPS4, K_POW = range(6)


def constants():
    c = np.zeros((P, N_CONST + N_BAND), np.float32)
    i, j = np.arange(P)[:, None], np.arange(P)[None, :]
    c[:, C_ID:C_ID + P] = i == j
    c[:, C_TRI:C_TRI + P] = -(i >= j).astype(np.float32)
    c[:, C_ONES:C_ONES + P] = -1.0
    c[:, C_STRICT:C_STRICT + P] = i < j
    c[:, C_CAUS:C_CAUS + P] = np.where(j <= i, 0.0, NEG)
    c[:, C_WIN:C_WIN + P] = np.where(j > i, 0.0, NEG)
    for g, w in enumerate(WINDOWS):
        for part, (si, ti) in enumerate(((0, 0), (0, P), (P, P))):
            s, t = i + si, j + ti
            band = ((s <= t) & (s > t - w)) / np.minimum(t + 1, w) - (s == t)
            at = N_CONST + (3 * g + part) * P
            c[:, at:at + P] = band
    for k, v in ((K_INVD, 1 / D), (K_INVC, 1 / P), (K_INVD4, 4 / D), (K_EPS, EPS), (K_EPS4, 4 * EPS), (K_POW, -0.5)):
        c[:, C_SC + k] = v
    return c


def trunk(nc, a, out):
    with ExitStack() as ctx:
        sem = lambda n: ctx.enter_context(nc.semaphore(n))
        base = (nc.sbuf_base + 63) // 64 * 64
        place = {}

        def put(name, shape, dt, at=None):
            size = 4 * int(np.prod(shape))
            at = place.get("end", base) if at is None else at
            place["end"] = max(place.get("end", base), at + (size + 63) // 64 * 64)
            assert place["end"] <= nc.sbuf_usable_end, (name, place["end"])
            place[name] = at
            return nc.alloc_sbuf_tensor_at(name, [P, *shape], dt, offset=at)

        raw = put("raw", (RAW, 2048), F32)
        wh = put("wh", (SPL, 1024), F32R)
        wl = put("wl", (SPL, 1024), F32R)
        x = put("x", (NB, D), F32)
        xh = put("xh", (KC, TOK), F32R)
        xl = put("xl", (KC, TOK), F32R)
        ah = put("ah", (FC, TOK), F32R)
        al = put("al", (FC, TOK), F32R)
        A = place["ah"]
        brh = put("brh", (4, 2, TOK), F32R, A)
        brl = put("brl", (4, 2, TOK), F32R, A + 8192)
        at = A + 16384

        def mixer_tile(name, shape):
            nonlocal at
            t = put(name, shape, F32, at)
            at += 4 * int(np.prod(shape))
            assert at <= A + 2 * 4 * FC * TOK
            return t
        u_n = mixer_tile("u_n", (NB, BW))
        v_sb = mixer_tile("v_sb", (NB, BW))
        v_sw = mixer_tile("v_sw", (NB, P))
        v_ds = mixer_tile("v_ds", (NB, BW))
        dqT = mixer_tile("dqT", (2, TOK))
        iqT = mixer_tile("iqT", (2, TOK))
        ikT = mixer_tile("ikT", (TOK,))
        cT = mixer_tile("cT", (TOK,))
        dkT = mixer_tile("dkT", (2, TOK))
        sbqT = mixer_tile("sbqT", (2, TOK))
        sbkT = mixer_tile("sbkT", (2, TOK))
        swqT = mixer_tile("swqT", (2, TOK))
        swkT = mixer_tile("swkT", (2, TOK))
        poT = put("poT", (2, TOK), F32, place["sbqT"])
        memn = put("memn", (NB, D), F32, A + 16384)
        memh = put("memh", (KC, TOK), F32R, A + 24576)
        meml = put("meml", (KC, TOK), F32R, A + 32768)
        tmp = put("tmp", (NB, 512), F32, A + 40960)
        sc1 = put("sc1", (4, TOK), F32, A + 4096)
        pT1 = put("pT1", (4, 2, P), F32, A + 12288)
        yg = put("yg", (NB, D), F32)
        W = place["yg"]
        bands = put("bands", (N_BAND,), F32, W)
        merged = put("merged", (NB, D), F32, W)
        nat = put("nat", (2, NB, 512), F32)
        sg = put("sg", (2, NB, FG), F32, place["nat"])
        an = put("an", (2, NB, FG), F32, place["nat"] + 4096)
        gate = put("gate", (2, NB, 512), F32, place["nat"])
        sc = put("sc", (4, TOK), F32)
        S = place["sc"]
        junk = put("junk", (D,), F32, S)
        pT = put("pT", (4, 2, P), F32)
        gbc = put("gbc", (D,), F32)
        assert place["pT"] == S + 4096 and place["gbc"] == S + 8192
        cn = put("cn", (NB, P), F32, S + 4096)
        ikr = put("ikr", (NB, 4, 32), F32, S + 5120)
        swkr = put("swkr", (NB, 2, P), F32, place["tmp"])
        relu = put("relu", (8, TOK), F32, S)
        sb_sp = put("sb_sp", (1536,), F32, S)
        sb_a = put("sb_a", (1536,), F32, S + 6144)
        score = put("score", (TOK,), F32)
        dmask = put("dmask", (NB, TOK), F32)
        xqT = put("xqT", (2, TOK), F32, place["score"])
        mkT = put("mkT", (2, TOK), F32)
        v_m = put("v_m", (NB, BW), F32)
        cst = put("cst", (N_CONST,), F32)
        gT = put("gT", (5, KC), F32)
        pw = put("pw", (2, 64), F32)
        psc = put("psc", (2,), F32)
        kvn = put("kvn", (1,), F32)
        uk = put("uk", (BW,), F32)
        uv = put("uv", (BW,), F32)
        snk = put("snk", (4,), F32)
        ssq = put("ssq", (NRQ,), F32)
        msq = put("msq", (NRQ,), F32)
        rms = put("rms", (NRQ,), F32)
        hrs = put("hrs", (NB,), F32)
        iw = put("iw", (NB, 8), F32)
        top8 = put("top8", (8,), F32)
        nmx = put("nmx", (2, 4), F32)
        den = put("den", (2, 4), F32)
        rcp = put("rcp", (2, 4), F32)
        carry = put("carry", (1,), F32)
        table = put("table", (1,), F32)
        esk = put("esk", (4,), F32)

        ps = ctx.enter_context(nc.psum_tensor("ps", [P, 8, 512], F32))

        ident = cst[:, C_ID:C_ID + P]
        k_col = lambda k: cst[:, C_SC + k:C_SC + k + 1]

        x_in = [sem(f"x{blk}_in") for blk in range(NB)]
        raw_in = [sem(f"raw_in{r}") for r in range(RAW)]
        hi_done, split_done, half_done = sem("hi_done"), sem("split_done"), sem("half_done")
        params_in, const_in, gbc_in, mem_in, stored = (
            sem(n) for n in ("params_in", "const_in", "gbc_in", "mem_in", "stored"))
        x_new, x_turned, x_hi, x_lo = sem("x_new"), sem("x_turned"), sem("x_hi"), sem("x_lo")
        squared, rms_ready, gained = sem("squared"), sem("rms_ready"), sem("gained")
        silu_done, act_done, act_turned, act_hi, act_lo = (
            sem(n) for n in ("silu_done", "act_done", "act_turned", "act_hi", "act_lo"))
        nat_done, turned, turned_out = sem("nat_done"), sem("turned"), sem("turned_out")
        mix_pe, mix_out, br_hi, br_lo = sem("mix_pe"), sem("mix_out"), sem("br_hi"), sem("br_lo")
        idx_pe, relu_done, idx_sum, sel_done = sem("idx_pe"), sem("relu_done"), sem("idx_sum"), sem("sel_done")
        sb_pe, sb_act, sb_dve = sem("sb_pe"), sem("sb_act"), sem("sb_dve")
        att_s, att_max, att_exp, att_p, att_t, att_tev, att_o = (
            sem(f"att_{n}") for n in ("s", "max", "exp", "p", "t", "tev", "o"))
        y_out, merge_done, m_turned, m_hi, m_lo = sem("y_out"), sem("merge_done"), sem("m_turned"), sem("m_hi"), sem("m_lo")
        mem_turned, mem_hi, mem_lo = sem("mem_turned"), sem("mem_hi"), sem("mem_lo")
        dve_link, act_link, pool_link = sem("dve_link"), sem("act_link"), sem("pool_link")
        half_rms, block0_done, query0_done, gain_in, bands_in, masks_in = (
            sem(n) for n in ("half_rms", "block0_done", "query0_done", "gain_in", "bands_in", "masks_in"))

        N_PAR = 11
        N_NAT = 5 + 8 + 4
        N_TURN = 8 + 3
        N_MRG = 8
        N_BR = 8
        BR = {"pool": 0, "sb": 1, "swa0": 2, "swa1": 3, "dsa0": 4, "dsa1": 5, "x0": 6, "x1": 7}
        ATT = (("swa", 0), ("swa", 1), ("dsa", 0), ("dsa", 1), ("x", 0), ("x", 1))
        N_ATT = len(ATT)
        OUT_BANK = ((4, 6), (2, 0), (6, 2), (4, 6))
        G_BANK = (2, 0)
        S_BANK, T_BANK, O_BANK = (4, 4, 4, 4, 2, 2), (6, 6, 6, 6, 0, 0), (6, 6, 6, 6, 4, 5)
        scores, probsT = (sc, sc, sc, sc, sc, sc1), (pT, pT, pT, pT, pT, pT1)
        N_ALINK, N_VLINK = 3, 77

        up = {f: a[f"ffn{f}_w_up"].rearrange("l (c p) (t n) -> l p c t n", p=P, t=2) for f in (1, 2)}
        down = {f: a[f"ffn{f}_w_down"].rearrange("l (c p) n -> l p c n", p=P) for f in (1, 2)}
        w_in = a["w_in"].rearrange("l (c p) n -> l p c n", p=P)
        w_br = a["w_branch"].rearrange("l i (c p) n -> l i p c n", p=P)
        w_out = a["w_out"].rearrange("l (c p) n -> l p c n", p=P)
        w_q = a["xattn_w_q"].rearrange("l (c p) n -> l p c n", p=P)
        w_kv = a["xattn_w_kv"].rearrange("l (c p) n -> l p c n", p=P)
        w_o = a["xattn_w_o"].rearrange("l (c p) n -> l p c n", p=P)

        x_dram = a["x"].rearrange("o (b p) d -> p (o b) d", p=P)

        block = ctx.enter_context(nc.Block())

        @block.sync
        def _(sp):
            sp.dma_start(cst[:, 0:N_FIRST], a["consts"][:, 0:N_FIRST]).then_inc(const_in, 16)
            sp.dma_start(x[:, 0], x_dram[:, 0]).then_inc(x_in[0], 16)

            def load(L, u, srcs, dims, it=0, by=0):
                c, n = dims
                dst = raw[:, u % RAW, 0:c * n].rearrange("p (c n) -> p c n", c=c)
                sp.wait_ge(split_done, L * NH + 2 * u + 2 + it * (2 * RAW))
                for i, src in enumerate(srcs):
                    part = dst[:, :, i * n // 2:(i + 1) * n // 2] if by else dst[:, i * c // 2:(i + 1) * c // 2, :]
                    sp.dma_start(part, src).then_inc(raw_in[u % RAW], 16)

            def chunks(w, k0, kn):
                return w[:, k0:k0 + kn // 2, :], w[:, k0 + kn // 2:k0 + kn, :]

            def load_gain(L, k, name):
                if k == 1:
                    sp.wait_ge(br_lo, L * N_BR + BR["sb"] + 1)
                if k == 2:
                    sp.wait_ge(gained, L * 8 + 2 * k)
                sp.dma_start(gbc[:], a[name][L].partition_broadcast(P)).then_inc(gbc_in, 16)

            def ffn(L, f, u0, k):
                def group(g, u, it=0):
                    for i in range(2):
                        load(L, u + i, [up[f][L, :, 4 * i:4 * i + 4, t, bass.ts(g, FG)] for t in range(2)], (4, 2 * FG),
                             it, by=1)
                group(0, u0)
                if f == 2:
                    load_gain(L, 2, "xattn_post")
                with sp.Fori(0, (NG - 1) // 2) as it:
                    for j in range(2):
                        group(2 * it + 1 + j, u0 + 2 + 2 * j, it)
                if f == 1:
                    params(L)
                load_gain(L, k, f"ffn{f}_post")
                for c in range(FC // 2):
                    load(L, u0 + 2 * NG + c, chunks(down[f][L], 2 * c, 2), (2, D))

            def params(L):
                def par(dst, src):
                    sp.dma_start(dst, src).then_inc(params_in, 16)
                with nc.allow_non_contiguous_dma("gains, a value per partition"):
                    for i, n in enumerate(("mix_pre", "xattn_pre", "mem_norm", "ffn2_pre")):
                        par(gT[:, i + 1, :], a[n][L].rearrange("(c p) -> p c", p=P))
                    par(psc[:], a["pool_scale"][L].rearrange("(c p) -> p c", p=P))
                    par(kvn[:], a["dsa_kv_norm"][L].rearrange("(c p) -> p c", p=P))
                for c in range(2):
                    par(pw[:, c, :], a["pool_w"][L, 2 * c:2 * c + 2].rearrange("g c d -> (g c) d"))
                par(uk[:], a["dsa_w_uk"][L].rearrange("r h d -> r (h d)"))
                par(uv[:], a["dsa_w_uv"][L].rearrange("r h d -> r (h d)"))
                par(snk[:], a["swa_sinks"][L].partition_broadcast(P))
                sp.dma_start(cst[:, N_FIRST:N_CONST], a["consts"][:, N_FIRST:N_CONST]).then_inc(masks_in, 16)

            with sp.Fori(0, DEPTH) as L:
                with nc.allow_non_contiguous_dma("gains, a value per partition"):
                    sp.dma_start(gT[:, 0, :], a["ffn1_pre"][L].rearrange("(c p) -> p c", p=P)).then_inc(gain_in, 16)
                ffn(L, 1, H_FFN1 // 2, 0)
                u = H_MIX // 2
                for g in range(5):
                    c0, n = MIX_COLS[g]
                    for i in range(2):
                        load(L, u, chunks(w_in[L, :, :, c0:c0 + n], 4 * i, 4), (4, n))
                        u += 1
                    if g == 1:
                        sp.wait_ge(x_new, L * 8 + 4)
                        sp.dma_start(bands[:], a["consts"][:, N_CONST:N_CONST + N_BAND]).then_inc(bands_in, 16)
                for n, b in enumerate(ORDER):
                    for hf in range(2):
                        c0 = MIX_COLS[5 + 2 * b + hf][0]
                        for i in range(2):
                            load(L, u, chunks(w_in[L, :, :, c0:c0 + 512], 4 * i, 4), (4, 512))
                            u += 1
                    load(L, u, [w_br[L, b, :, :, 512 * hf:512 * hf + 512] for hf in range(2)], (4, 512))
                    if n == 3:
                        sp.wait_ge(br_lo, L * N_BR + BR["dsa1"] + 1)
                        sp.dma_start(memn[:], a["mem"].rearrange("o (b p) d -> p (o b) d", p=P)).then_inc(mem_in, 16)
                    u += 1
                    if n == 2:
                        load_gain(L, 1, "mix_post")
                for i in range(4):
                    load(L, u, chunks(w_out[L], 2 * i, 2), (2, D))
                    u += 1
                load(L, u, chunks(w_kv[L, :, :, 0:BW], 0, KC), (KC, BW))
                load(L, u + 1, chunks(w_q[L], 0, KC), (KC, BW))
                load(L, u + 2, chunks(w_kv[L, :, :, BW:2 * BW], 0, KC), (KC, BW))
                u += 2
                load(L, u + 1, chunks(w_o[L], 0, 2), (2, D))
                ffn(L, 2, H_FFN2 // 2, 3)
            for blk in range(NB):
                sp.wait_ge(x_new, 8 * DEPTH + blk + 1)
                sp.dma_start(out.rearrange("o (b p) d -> p (o b) d", p=P)[:, blk], x[:, blk]).then_inc(stored, 16)
            sp.wait_ge(stored, 16 * NB)

        @block.gpsimd
        def _(pool):
            pool.wait_ge(const_in, 16)
            for blk in range(NB):
                pool.wait_ge(x_in[blk], 16)
                pool.sem_inc(x_new, 1)

            def add_branch(L, n, hf):
                pool.wait_ge(y_out, L * 6 + 2 * n + hf + 1)
                s = slice(hf * 512, hf * 512 + 512)
                for blk in range(NB):
                    t = nc.gpsimd.tensor_tensor(merged[:, blk, s], merged[:, blk, s], tmp[:, blk], ALU.add)
                t.then_inc(merge_done, 1)

            with pool.Fori(0, DEPTH) as L:
                for name, q in RQ.items():
                    if name == "mem_0":
                        for n in (1, 2):
                            for hf in range(2):
                                add_branch(L, n, hf)
                    half = name in ("post0_0", "post0_1", "post3_0", "post3_1")
                    inv = K_INVC if name[0] == "c" else K_INVD4 if half else K_INVD
                    pool.wait_ge(squared, L * NRQ + q + 1)
                    nc.gpsimd.tensor_tensor(msq[:, q:q + 1], ssq[:, q:q + 1], k_col(inv), ALU.mult).then_inc(pool_link, 1)
                    pool.wait_ge(pool_link, L * 2 * NRQ + 2 * q + 1)
                    nc.gpsimd.tensor_tensor(msq[:, q:q + 1], msq[:, q:q + 1], k_col(K_EPS4 if half else K_EPS),
                                            ALU.add).then_inc(pool_link, 1)
                    pool.wait_ge(pool_link, L * 2 * NRQ + 2 * q + 2)
                    nc.gpsimd.tensor_tensor(rms[:, q:q + 1], msq[:, q:q + 1], k_col(K_POW), ALU.pow).then_inc(rms_ready, 1)

        def rs(name):
            return rms[:, RQ[name]:RQ[name] + 1]

        def wide(bank, n=1024, at=0):
            return ps[:].rearrange("p b n -> p (b n)")[:, bank * 512 + at:bank * 512 + at + n]

        @block.tensor
        def _(pe):
            pe.sem_inc(half_done, SPL)
            pe.wait_ge(const_in, 16)
            mm = nc.tensor.matmul

            def turn(dst, src):
                return nc.tensor.transpose(dst, src, ident)

            def half(L, h, k0, kn, n, dst, sh, sl, K, it=0, blocks=(0, 1), high=None, low=None):
                pe.wait_ge(split_done, L * NH + h + 1 + 2 * RAW + it * 8)
                if high:
                    pe.wait_ge(*high)
                q = h % SPL
                parts = [(k, c, min(512, n - c)) for k in range(kn) for c in range(0, n, 512)]
                for b in blocks:
                    tok = slice(b * P, b * P + P)
                    for k, c, w in parts:
                        mv = slice(k * n + c, k * n + c + w)
                        mm(dst(b, c, w), sh[:, k0 + k, tok], wh[:, q, mv], start=k0 + k == 0, stop=False)
                        mm(dst(b, c, w), sh[:, k0 + k, tok], wl[:, q, mv], start=False, stop=False)
                    if low and b == blocks[0]:
                        pe.wait_ge(*low)
                    for k, c, w in parts:
                        mv = slice(k * n + c, k * n + c + w)
                        last = mm(dst(b, c, w), sl[:, k0 + k, tok], wh[:, q, mv], start=False, stop=k0 + k == K - 1)
                if 1 in blocks:
                    last.then_inc(half_done, 1)
                return last

            def turn_x(L, b, blk):
                pe.wait_ge(x_new, L * 8 + 2 * b + blk + 1)
                for hf in range(2):
                    for c in range(4):
                        k = 4 * hf + c
                        t = turn(ps[:, OUT_BANK[b - 1][blk] + hf, c * P:c * P + P], x[:, blk, k * P:k * P + P])
                    t.then_inc(x_turned, 1)

            def head(L, b, step):
                if b == 0:
                    turn_x(L, 0, 0)
                for i in range(SKEW):
                    if i == SKEW - 1:
                        turn_x(L, b, 1)
                    step(i, (0,), *x_parts(L, b, 0, i // 2))
                for i in range(SKEW):
                    step(i, (1,), *x_parts(L, b, 1, i // 2))

            def x_parts(L, b, blk, hf):
                at = L * 16 + 4 * b + 2 * blk + hf + 1
                return (x_hi, at), (x_lo, at)

            def tail(L, b, step, n=SKEW):
                for i in range(n):
                    t = step(i, (0,))
                t.then_inc(block0_done, 1)
                for i in range(n):
                    if i == 3 and b < 3:
                        turn_x(L, b + 1, 0)
                    step(i, (1,))

            def ffn(L, f, h0, b):
                E = (L * 2 + f) * NG

                def act_turn(g, it, bank):
                    pe.wait_ge(act_done, E + g + 1 + it * 2)
                    for c in range(2):
                        for blk in range(NB):
                            t = turn(ps[:, bank, c * TOK + blk * P:c * TOK + blk * P + P],
                                     an[:, g % 2, blk, c * P:c * P + P])
                    t.then_inc(act_turned, 1)

                def up_half(g, i, it=0, blocks=(0, 1), high=None, low=None):
                    return half(L, h0 + 4 * g + i, 2 * i, 2, 512, lambda blk, c, w: ps[:, 2 * (g % 2) + blk, :], xh, xl,
                                KC, it, blocks, high, low)

                def down_half(c, blocks=(0, 1)):
                    return half(L, h0 + 4 * NG + c, c, 1, D, lambda blk, cc, w: ps[:, 4 + 2 * blk + cc // 512, :], ah, al,
                                FC, 0, blocks)

                def group(g, it=0):
                    if g >= 2:
                        pe.wait_ge(act_done, E + g - 1 + it * 2)
                    for i in range(4):
                        up_half(g, i, it)
                        if i == (2 if g == 1 else 0):
                            if g > 2:
                                pe.wait_ge(act_lo, E + g - 2 + it * 2)
                            act_turn(g - 1, it, 4 + (g - 1) % 2)

                head(L, b, lambda i, blocks, high, low: up_half(0, i, 0, blocks, high, low))
                group(1)
                group(2)
                with pe.Fori(0, (NG - 3) // 2) as it:
                    group(3, it)
                    group(4, it)
                for c in range(FC - SKEW - 1):
                    pe.wait_ge(act_lo, E + max(c // 2 + 1, NG - 1))
                    down_half(c)
                    if c == 0:
                        act_turn(NG - 1, 0, 2)
                pe.wait_ge(act_lo, E + NG)
                tail(L, b, lambda i, blocks: down_half(FC - SKEW - 1 + i, blocks), SKEW + 1)

            def mixer(L):
                h0 = H_MIX

                def t_wait(j):
                    pe.wait_ge(nat_done, L * N_NAT + (0, 1, 1, 1, 2, 2, 3, 4)[j] + 1)
                    if j == 3:
                        pe.wait_ge(act_link, L * N_ALINK + 1)
                    if j in (4, 5):
                        pe.wait_ge(relu_done, L * 2 + 1)
                        pe.wait_ge(mix_out, L * 2 + 2)
                    if j in (6, 7):
                        pe.wait_ge(relu_done, L * 2 + 2)

                def t_step(j):
                    src = (nat[:, 0, :, 256:512], nat[:, 1, :, 128:384], ikr, cn, nat[:, 0, :, 0:256],
                           nat[:, 0, :, 256:512], nat[:, 1, :, 256:512], swkr)[j]
                    bank = 4 + j % 2
                    if j >= 2:
                        pe.wait_ge(turned_out, L * N_TURN + j - 1)
                    for c in range(1 if j in (2, 3) else 2):
                        for blk in range(NB):
                            s = (ikr[:, blk].rearrange("p r d -> p (r d)") if j == 2 else cn[:, blk] if j == 3
                                 else swkr[:, blk, c] if j == 7 else src[:, blk, c * P:c * P + P])
                            t = turn(ps[:, bank, c * TOK + blk * P:c * TOK + blk * P + P], s)
                    t.then_inc(turned, 1)

                def pooled():
                    pe.wait_ge(bands_in, 16 * (L + 1))
                    for g in range(4):
                        o = ps[64 * (g % 2):64 * (g % 2) + 64, 6, (g // 2) * TOK:(g // 2) * TOK + TOK]
                        band = bands[:, 3 * g * P:3 * g * P + 3 * P]
                        mm(o, u_n[:, 0, 64 * g:64 * g + 64], band[:, 0:TOK], start=True, stop=False, skip_group_check=True)
                        t = mm(o[:, P:TOK], u_n[:, 1, 64 * g:64 * g + 64], band[:, TOK:3 * P], start=False, stop=True,
                               skip_group_check=True)
                    t.then_inc(mix_pe, 1)

                def pool_mix():
                    for g in range(4):
                        r = slice(64 * (g % 2), 64 * (g % 2) + 64)
                        t = mm(ps[r, 7, (g // 2) * TOK:(g // 2) * TOK + TOK], pw[r, g // 2, :], poT[r, g // 2, :],
                               start=True, stop=True, skip_group_check=True)
                    t.then_inc(mix_pe, 1)

                def dsa_kv():
                    pe.wait_ge(turned_out, L * N_TURN + 4)
                    for c in range(2):
                        mm(ps[:, 4, c * TOK:c * TOK + TOK], uk[:, c * P:c * P + P], cT[:], start=True, stop=True,
                           skip_group_check=True)
                    for blk in range(NB):
                        t = mm(ps[:, 5, blk * BW:blk * BW + BW], cT[:, blk * P:blk * P + P], uv[:], start=True, stop=True,
                               skip_group_check=True)
                    t.then_inc(mix_pe, 1)

                def index(b):
                    if b == 0:
                        pe.wait_ge(mix_out, L * 2 + 2)
                        pe.wait_ge(br_lo, L * N_BR + BR["pool"] + 1)
                    else:
                        pe.wait_ge(relu_done, L * 2 + 1)
                        pe.wait_ge(turned_out, L * N_TURN + 6)
                    W_ = P * (b + 1)
                    for h in range(8):
                        r = slice(32 * (h % 4), 32 * (h % 4) + 32)
                        t = mm(ps[:, 4 + h % 4, (h // 4) * TOK:(h // 4) * TOK + W_], iqT[r, h // 4, b * P:b * P + P],
                               ikT[r, 0:W_], start=True, stop=True, skip_group_check=True)
                    t.then_inc(idx_pe, 1)

                def sb_scores():
                    pe.wait_ge(turned_out, L * N_TURN + 8)
                    pe.wait_ge(relu_done, L * 2 + 2)
                    for h in range(4):
                        r, first = slice(64 * (h % 2), 64 * (h % 2) + 64), h < 2
                        mm(ps[:, 4 + h % 2, (h // 2) * TOK:(h // 2) * TOK + TOK], sbkT[r, h // 2, 0:P], sbqT[r, h // 2, :],
                           start=first, stop=False, skip_group_check=True)
                        t = mm(ps[:, 6 + h % 2, (h // 2) * P:(h // 2) * P + P], sbkT[r, h // 2, P:TOK],
                               sbqT[r, h // 2, P:TOK], start=first, stop=False, skip_group_check=True)
                    t.then_inc(sb_pe, 1)

                def sb_sums():
                    pe.wait_ge(sb_dve, L * 2 + 1)
                    tri, ones = cst[:, C_TRI:C_TRI + P], cst[:, C_ONES:C_ONES + P]
                    for e in range(2):
                        mm(ps[:, 4 + e, :], tri, sb_sp[:, e * 512:e * 512 + 512], start=False, stop=False, skip_group_check=True)
                        own = sb_sp[:, 1024 + e * TOK:1024 + e * TOK + TOK]
                        mm(ps[:, 4 + e, :].rearrange("p (h n) -> p h n", h=2)[:, :, P:TOK], ones,
                           own.rearrange("p (h n) -> p h n", h=2), start=False, stop=True, skip_group_check=True)
                        t = mm(ps[:, 6 + e, 0:TOK], tri, own, start=False, stop=True, skip_group_check=True)
                    t.then_inc(sb_pe, 1)

                def sb_values():
                    pe.wait_ge(sb_dve, L * 2 + 2)
                    for h in range(4):
                        o = ps[64 * (h % 2):64 * (h % 2) + 64, 4, (h // 2) * TOK:(h // 2) * TOK + TOK]
                        s = (h % 2) * 2 + h // 2
                        mm(o, v_sb[:, 0, 64 * h:64 * h + 64], sb_a[:, s * TOK:s * TOK + TOK], start=True, stop=False,
                           skip_group_check=True)
                        t = mm(o[:, P:TOK], v_sb[:, 1, 64 * h:64 * h + 64], sb_a[:, 1024 + s * P:1024 + s * P + P],
                               start=False, stop=True, skip_group_check=True)
                    t.then_inc(sb_pe, 1)

                def mem_turn():
                    pe.wait_ge(mem_in, 16 * (L + 1))
                    pe.wait_ge(br_lo, L * N_BR + BR["dsa1"] + 1)
                    for blk in range(NB):
                        for hf in range(2):
                            for c in range(4):
                                k = 4 * hf + c
                                t = turn(ps[:, 4 + 2 * blk + hf, c * P:c * P + P], memn[:, blk, k * P:k * P + P])
                            t.then_inc(mem_turned, 1)

                def w_in_half(m, blocks=(0, 1), high=None, low=None):
                    g, i = m // 4, m % 4
                    n = MIX_COLS[g][1]
                    return half(L, h0 + m, 2 * i, 2, n, lambda blk, c, w: ps[:, 2 * (g % 2) + blk, 0:n], xh, xl, KC, 0, blocks,
                                high, low)

                def branch_half(m, blocks=(0, 1)):
                    n, r = (m - M_GATES) // 10, (m - M_GATES) % 10
                    hf = r // 4 if r < 8 else r - 8
                    dst = lambda blk, c, w: ps[:, G_BANK[hf] + blk, :]
                    if r < 8:
                        if r % 4 == 0 and n == 0:
                            pe.wait_ge(nat_done, L * N_NAT + 4 + hf)
                        if r % 4 == 0 and n > 0:
                            pe.wait_ge(y_out, L * 6 + 2 * (n - 1) + hf + 1)
                        half(L, h0 + m, 2 * (r % 4), 2, 512, dst, xh, xl, KC)
                    else:
                        b = ORDER[n]
                        pe.wait_ge(nat_done, L * N_NAT + 5 + 2 * n + hf + 1)
                        if hf == 0:
                            pe.wait_ge(br_lo, L * N_BR + BR[("pool", "dsa1", "sb", "swa1")[b]] + 1)
                        half(L, h0 + m, 0, 2, 512, dst, brh[:, b], brl[:, b], 2, 0, blocks)

                def m_turn(hf, blk):
                    pe.wait_ge(merge_done, L * N_MRG + 4 + 2 * hf + blk + 1)
                    for c in range(4):
                        k = 4 * hf + c
                        t = turn(ps[:, 4 + 2 * hf + blk, c * P:c * P + P], merged[:, blk, k * P:k * P + P])
                    t.then_inc(m_turned, 1)

                def out_half(k, blocks, high=None, low=None):
                    return half(L, h0 + M_OUT + k, k, 1, D, lambda blk, c, w: ps[:, OUT_BANK[1][blk] + c // 512, :], xh, xl, KC,
                                0, blocks, high, low)

                head(L, 1, w_in_half)
                for m in range(SKEW, M_OUT - 1):
                    for j, at in AT_T.items():
                        if m == at:
                            t_wait(j)
                            t_step(j)
                    if m == AT_POOLED:
                        pooled()
                    if m == AT_POOLMIX:
                        pe.wait_ge(mix_out, L * 2 + 1)
                    if m == AT_DKV:
                        dsa_kv()
                    for b in range(NB):
                        if m == AT_IDX[b]:
                            index(b)
                    if m == AT_SB[0]:
                        sb_scores()
                    if m == AT_SB[1]:
                        sb_sums()
                    if m == AT_SB[2]:
                        sb_values()
                    for n, at in enumerate(AT_ATT):
                        if m == at + 4:
                            att_values(L, n)
                        if m == at:
                            att_scores(L, n)
                        if m == at + 3:
                            att_turn(L, n)
                    if m == AT_MEM:
                        mem_turn()
                    if m < M_GATES:
                        if m % 4 == 0 and m >= 8:
                            pe.wait_ge(nat_done, L * N_NAT + m // 4 - 1)
                        w_in_half(m)
                    else:
                        branch_half(m)
                    if m == AT_POOLMIX:
                        pool_mix()
                branch_half(M_OUT - 1, (0,))
                pe.wait_ge(mem_lo, L * 4 + 4)
                m_turn(0, 0)
                branch_half(M_OUT - 1, (1,))
                pe.wait_ge(merge_done, L * N_MRG + 6)
                m_parts = lambda j: ((m_hi, L * 4 + j + 1), (m_lo, L * 4 + j + 1))
                for k in range(SKEW):
                    if k == 1:
                        m_turn(0, 1)
                    if k == SKEW - 1:
                        m_turn(1, 0)
                        m_turn(1, 1)
                    out_half(k, (0,), *m_parts(0))
                for k in range(SKEW):
                    out_half(k, (1,), *m_parts(1))
                pe.wait_ge(m_lo, L * 4 + 4)
                tail(L, 1, lambda i, blocks: out_half(SKEW + i, blocks))

            def att_scores(L, n):
                kind, b = ATT[n]
                if n == 0:
                    pe.wait_ge(br_lo, L * N_BR + BR["sb"] + 1)
                W_ = TOK if kind == "x" else P * (b + 1)
                qT, kT = {"swa": (swqT, swkT), "dsa": (dqT, dkT), "x": (xqT, mkT)}[kind]
                for h in range(4):
                    r = slice(64 * (h % 2), 64 * (h % 2) + 64)
                    c = (0 if h % 2 == h // 2 else 1) if kind == "swa" else h // 2
                    t = mm(ps[:, S_BANK[n] + h % 2, (h // 2) * TOK:(h // 2) * TOK + W_], qT[r, h // 2, b * P:b * P + P],
                           kT[r, c, 0:W_], start=True, stop=True, skip_group_check=True)
                t.then_inc(att_s, 1)

            def att_turn(L, n):
                kind, b = ATT[n]
                if 0 < n < 4:
                    pe.wait_ge(br_lo, L * N_BR + BR[kind + str(b)])
                pe.wait_ge(att_p, L * N_ATT + n + 1)
                for h in range(4):
                    for k in range(2 if kind == "x" else b + 1):
                        t = turn(ps[:, T_BANK[n] + h // 2, (h % 2) * TOK + k * P:(h % 2) * TOK + k * P + P],
                                 scores[n][:, h, k * P:k * P + P])
                t.then_inc(att_t, 1)

            def att_values(L, n):
                kind, b = ATT[n]
                v = {"swa": v_sw, "dsa": v_ds, "x": v_m}[kind]
                K = 2 if kind == "x" else b + 1
                pe.wait_ge(att_tev, L * N_ATT + n + 1)
                for h in range(4):
                    o = ps[64 * (h % 2):64 * (h % 2) + 64, O_BANK[n], (h // 2) * P:(h // 2) * P + P]
                    hv = h // 2 if kind == "swa" else h
                    for k in range(K):
                        t = mm(o, v[:, k, 64 * hv:64 * hv + 64], probsT[n][:, (h % 2) * 2 + h // 2, k, :], start=k == 0,
                               stop=k == K - 1, skip_group_check=True)
                t.then_inc(att_o, 1)

            def memory(L):
                h0 = H_X

                def mem_half(i, blocks=(0, 1)):
                    return half(L, h0 + i, 4 * (i % 2), 4, BW, lambda blk, c, w: ps[:, 4 + blk, 0:BW], memh, meml, KC, 0,
                                blocks)

                def query_half(i, blk):
                    return half(L, h0 + 2 + i, 4 * i, 4, BW, lambda blk, c, w: ps[:, 6 + blk, 0:BW], xh, xl, KC, 0, (blk,),
                                *x_parts(L, 2, blk, i))

                def nat_turn(j, blk, dst):
                    for c in range(2):
                        t = turn(dst[:, c * TOK:c * TOK + P], nat[:, j, blk, c * P:c * P + P])
                    return t

                def out_half(k, blk):
                    at = L * N_BR + BR["x0"] + blk + 1
                    return half(L, h0 + 6 + k, k, 1, D, lambda blk, c, w: ps[:, OUT_BANK[2][blk] + c // 512, :],
                                brh[:, 0], brl[:, 0], 2, 0, (blk,), *((br_hi, at), (br_lo, at)))

                mem_half(0)
                mem_half(1)
                turn_x(L, 2, 1)
                for blk in range(NB):
                    for i in range(2):
                        t = query_half(i, blk)
                    if blk == 0:
                        t.then_inc(query0_done, 1)
                pe.wait_ge(nat_done, L * N_NAT + N_NAT - 3)
                nat_turn(0, 0, ps[:, 0, :])
                nat_turn(0, 1, ps[:, 0, P:]).then_inc(turned, 1)
                pe.wait_ge(nat_done, L * N_NAT + N_NAT - 2)
                nat_turn(1, 0, ps[:, 1, :]).then_inc(turned, 1)
                mem_half(4, (0,))
                pe.wait_ge(turned_out, L * N_TURN + 10)
                att_scores(L, 4)
                mem_half(4, (1,))
                pe.wait_ge(nat_done, L * N_NAT + N_NAT - 1)
                nat_turn(1, 1, ps[:, 1, P:]).then_inc(turned, 1)
                mem_half(5)
                att_turn(L, 4)
                pe.wait_ge(turned_out, L * N_TURN + 11)
                att_scores(L, 5)
                pe.wait_ge(nat_done, L * N_NAT + N_NAT)
                att_values(L, 4)
                out_half(0, 0)
                out_half(1, 0).then_inc(block0_done, 1)
                att_turn(L, 5)
                att_values(L, 5)
                out_half(0, 1)
                turn_x(L, 3, 0)
                out_half(1, 1)

            with pe.Fori(0, DEPTH) as L:
                ffn(L, 0, H_FFN1, 0)
                pe.wait_ge(params_in, 16 * N_PAR * (L + 1))
                pe.wait_ge(masks_in, 16 * (L + 1))
                mixer(L)
                memory(L)
                ffn(L, 1, H_FFN2, 3)

        @block.scalar
        def _(act):
            fn = nc.scalar.activation
            act.wait_ge(const_in, 16)
            nc.scalar.dma_start(x[:, 1], x_dram[:, 1]).then_inc(x_in[1], 16)

            def hi(L, h, it=0):
                if h >= NH:
                    return
                u, n = h // 2, HALF[h]
                if h % 2 == 0:
                    act.wait_ge(raw_in[u % RAW], 32 * (L * (NU // RAW) + u // RAW + 1 + it))
                act.wait_ge(half_done, L * NH + h + 1 + it * 8)
                fn(wh[:, h % SPL, 0:n], raw[:, u % RAW, (h % 2) * n:(h % 2) * n + n], ACT.Copy).then_inc(hi_done, 1)

            def group_done(L, h, it=0):
                act.wait_ge(half_done, L * NH + h + 1 + SPL + it * 8)

            def square(L, src, name, n=D):
                q = RQ[name]
                if q > 0:
                    act.wait_ge(squared, L * NRQ + q)
                fn(junk[:, 0:n], src, ACT.Square, accum_out=ssq[:, q:q + 1]).then_inc(squared, 1)

            def x_high(L, b, blk, parts=(0, 1)):
                gi = (0, 1, 2, 4)[b]
                for hf in parts:
                    act.wait_ge(x_turned, L * 16 + b * 4 + 2 * blk + hf + 1)
                    for c in range(4):
                        k = 4 * hf + c
                        t = fn(xh[:, k, blk * P:blk * P + P], ps[:, OUT_BANK[b - 1][blk] + hf, c * P:c * P + P], ACT.Copy,
                               scale=gT[:, gi, k:k + 1])
                    t.then_inc(x_hi, 1)

            def pre_square(L, b, blk):
                square(L, x[:, blk], f"pre{b}_{blk}")

            def post_square(L, k, h_last, blk):
                if blk == 0:
                    act.wait_ge(block0_done, L * 4 + k + 1)
                else:
                    group_done(L, h_last)
                square(L, wide(OUT_BANK[k][blk]), f"post{k}_{blk}")

            def between(L, k, h0):
                post_square(L, k, h0 - 1, 0)
                hi(L, h0 + 3)
                hi(L, h0 + 4)
                hi(L, h0 + 5)
                x_high(L, k + 1, 0)
                post_square(L, k, h0 - 1, 1)
                pre_square(L, k + 1, 0)
                hi(L, h0 + 6)
                if k == 1:
                    return
                x_high(L, k + 1, 1)
                pre_square(L, k + 1, 1)
                hi(L, h0 + 7)

            def ffn(L, f, h0, b):
                E = (L * 2 + f) * NG

                def silu(g, it=0):
                    group_done(L, h0 + 4 * g + 3, it)
                    if g == 0:
                        act.wait_ge(rms_ready, L * NRQ + RQ[f"pre{b}_1"] + 1)
                    if g >= 2 or not isinstance(it, int):
                        act.wait_ge(act_done, E + g - 1 + it * 2)
                    for blk in range(NB):
                        t = fn(sg[:, g % 2, blk], ps[:, 2 * (g % 2) + blk, 0:FG], ACT.Silu, scale=rs(f"pre{b}_{blk}"))
                    t.then_inc(silu_done, 1)

                def high(g, it=0):
                    bank = 2 if g == NG - 1 else 4 + g % 2
                    act.wait_ge(act_turned, E + g + 1 + it * 2)
                    k = 2 * g + 4 * it if not isinstance(it, int) else 2 * g
                    fn(ah[:, bass.ds(k, 2), :] if not isinstance(it, int) else ah[:, k:k + 2, :],
                       ps[:, bank, :].rearrange("p (c t) -> p c t", c=2), ACT.Copy).then_inc(act_hi, 1)

                for i in (8, 9, 10):
                    hi(L, h0 + i)

                def group(g, it=0):
                    silu(g - 1, it)
                    hi(L, h0 + 4 * g + AHEAD, it)
                    hi(L, h0 + 4 * g + 1 + AHEAD, it)
                    high(g - 1, it)
                    hi(L, h0 + 4 * g + 2 + AHEAD, it)
                    hi(L, h0 + 4 * g + 3 + AHEAD, it)
                group(1)
                group(2)
                with act.Fori(0, (NG - 3) // 2) as it:
                    group(3, it)
                    group(4, it)
                hd = h0 + 4 * NG
                silu(NG - 1)
                hi(L, hd + AHEAD)
                hi(L, hd + 1 + AHEAD)
                high(NG - 1)
                for c in range(2, FC - SKEW):
                    hi(L, hd + c + AHEAD)

            def branch_high(L, name, dst, src, scale=1.0):
                fn(dst, src, ACT.Copy, scale=scale).then_inc(br_hi, 1)

            def att_exp_step(L, n):
                kind, b = ATT[n]
                r = b if kind == "x" else 0
                W_ = TOK if kind == "x" else P * (b + 1)
                act.wait_ge(att_max, L * N_ATT + n + 1)
                for h in range(4):
                    if kind == "x":
                        src, scale = ps[:, S_BANK[n] + h // 2, (h % 2) * TOK:(h % 2) * TOK + TOK], 0.125
                    else:
                        src, scale = sc[:, h, 0:W_], 1.0
                    t = fn(scores[n][:, h, 0:W_], src, ACT.Exp, bias=nmx[:, r, h:h + 1], scale=scale,
                           accum_out=den[:, r, h:h + 1])
                if kind == "swa":
                    for h in range(4):
                        at = (h % 2) * 2 + h // 2
                        t = fn(esk[:, at:at + 1], snk[:, h:h + 1], ACT.Exp, bias=nmx[:, 0, at:at + 1])
                t.then_inc(att_exp, 1)

            def att_pT(L, n):
                K = ATT[n][1] + 1
                act.wait_ge(att_t, L * N_ATT + n + 1)
                fn(pT[:, :, 0:K, :], wide(T_BANK[n]).rearrange("p (h k n) -> p h k n", h=4, k=2)[:, :, 0:K, :],
                   ACT.Copy).then_inc(att_tev, 1)

            def att_high(L, n):
                kind, b = ATT[n]
                i = {"swa": 3, "dsa": 1, "x": 0}[kind]
                act.wait_ge(att_o, L * N_ATT + n + 1)
                branch_high(L, kind + str(b), brh[:, i, :, b * P:b * P + P],
                            ps[:, O_BANK[n], 0:TOK].rearrange("p (c t) -> p c t", c=2))

            def mixer(L):
                h0 = H_MIX

                def natural(g):
                    group_done(L, h0 + 4 * g + 3)
                    bank = 2 * (g % 2)
                    if g == 0:
                        act.wait_ge(rms_ready, L * NRQ + RQ["pre1_1"] + 1)
                    if g == 2:
                        act.wait_ge(turned, L * N_TURN + 1)
                    if g == 3:
                        act.wait_ge(turned, L * N_TURN + 4)
                    for blk in range(NB):
                        src, r = ps[:, bank + blk, :], rs(f"pre1_{blk}")
                        if g == 0:
                            t = fn(u_n[:, blk], src[:, 0:256], ACT.Copy, scale=r)
                            t = fn(nat[:, 0, blk, 256:512], src[:, 256:512], ACT.Copy, scale=r)
                        elif g == 1:
                            t = fn(nat[:, 1, blk, 0:424], src[:, 0:424], ACT.Copy, scale=r)
                            for k in range(4):
                                t = fn(ikr[:, blk, k], src[:, 384:416], ACT.Copy, scale=r)
                        elif g == 2:
                            t = fn(nat[:, 0, blk], src, ACT.Copy, scale=r)
                        elif g == 3:
                            t = fn(v_sb[:, blk], src[:, 0:256], ACT.Copy, scale=r)
                            t = fn(nat[:, 1, blk, 256:512], src[:, 256:512], ACT.Copy, scale=r)
                        else:
                            fn(swkr[:, blk, 0], src[:, 0:128], ACT.Copy, scale=r)
                            fn(swkr[:, blk, 1, 0:64], src[:, 64:128], ACT.Copy, scale=r)
                            fn(swkr[:, blk, 1, 64:128], src[:, 0:64], ACT.Copy, scale=r)
                            t = fn(v_sw[:, blk], src[:, 128:256], ACT.Copy, scale=r)
                    t.then_inc(nat_done, 1)

                def gates(n, hf):
                    group_done(L, h0 + M_GATES + 10 * n + 4 * hf + 3)
                    if n == 0 and hf == 0:
                        act.wait_ge(half_rms, L + 1)
                    for blk in range(NB):
                        t = fn(gate[:, hf, blk], ps[:, G_BANK[hf] + blk, :], ACT.Tanh, scale=hrs[:, blk:blk + 1])
                    t.then_inc(nat_done, 1)

                def c_square():
                    act.wait_ge(nat_done, L * N_NAT + 2)
                    for blk in range(NB):
                        square(L, nat[:, 1, blk, 0:P], f"c_{blk}", P)

                def c_norm():
                    act.wait_ge(rms_ready, L * NRQ + RQ["c_1"] + 1)
                    for blk in range(NB):
                        t = fn(cn[:, blk], nat[:, 1, blk, 0:P], ACT.Copy, scale=rs(f"c_{blk}"))
                    t.then_inc(act_link, 1)

                def relu_step(b):
                    W_ = P * (b + 1)
                    act.wait_ge(idx_pe, L * 2 + b + 1)
                    if b == 1:
                        act.wait_ge(idx_sum, L * 2 + 1)
                    t = fn(relu[:, :, 0:W_], ps[:, 4:8, :].rearrange("p b (h n) -> p (b h) n", h=2)[:, :, 0:W_], ACT.Relu,
                           scale=32.0 ** -0.5)
                    t.then_inc(relu_done, 1)

                def sb_softplus():
                    parts = ((sb_sp[:, 0:1024], wide(4)),
                             (sb_sp[:, 1024:1536].rearrange("p (e n) -> p e n", e=2), ps[:, 6:8, 0:TOK]))
                    act.wait_ge(sb_pe, L * 3 + 1)
                    act.wait_ge(idx_sum, L * 2 + 2)
                    for dst, z in parts:
                        t = fn(dst, z, ACT.Abs)
                    t.then_inc(act_link, 1)
                    act.wait_ge(act_link, L * N_ALINK + 2)
                    fn(sb_sp[:], sb_sp[:], ACT.Exp, scale=-1.0).then_inc(act_link, 1)
                    act.wait_ge(act_link, L * N_ALINK + 3)
                    fn(sb_sp[:], sb_sp[:], ACT.Ln, bias=1.0).then_inc(sb_act, 1)

                def sb_exp():
                    act.wait_ge(sb_pe, L * 3 + 2)
                    fn(sb_a[:, 0:1024], wide(4), ACT.Exp)
                    fn(sb_a[:, 1024:1536].rearrange("p (e n) -> p e n", e=2), ps[:, 6:8, 0:TOK], ACT.Exp).then_inc(sb_act, 1)

                def sb_high():
                    act.wait_ge(sb_pe, L * 3 + 3)
                    branch_high(L, "sb", brh[:, 2], ps[:, 4, :].rearrange("p (c t) -> p c t", c=2))

                def pool_high():
                    act.wait_ge(mix_pe, L * 3 + 2)
                    for c in range(2):
                        t = fn(brh[:, 0, c], ps[:, 7, c * TOK:c * TOK + TOK], ACT.Copy, scale=psc[:, c:c + 1])
                    t.then_inc(br_hi, 1)

                def memory_high(j):
                    act.wait_ge(mem_turned, L * 4 + j + 1)
                    for c in range(4):
                        k, blk = 4 * (j % 2) + c, j // 2
                        t = fn(memh[:, k, blk * P:blk * P + P], ps[:, 4 + j, c * P:c * P + P], ACT.Copy,
                               scale=gT[:, 3, k:k + 1])
                    t.then_inc(mem_hi, 1)

                def merged_high(j):
                    act.wait_ge(m_turned, L * 4 + j + 1)
                    k, blk = 4 * (j // 2), j % 2
                    fn(xh[:, k:k + 4, blk * P:blk * P + P], ps[:, 4 + j, :].rearrange("p (c t) -> p c t", c=4), ACT.Copy,
                       scale=0.5).then_inc(m_hi, 1)

                for m in range(1, M_OUT):
                    if m % 4 == 0 and 0 < m <= M_GATES:
                        natural(m // 4 - 1)
                        if m == 8:
                            c_square()
                    if m > M_GATES and (m - M_GATES) % 10 in (4, 8):
                        gates((m - M_GATES) // 10, (m - M_GATES) % 10 // 4 - 1)
                    for j, at in AT_T.items():
                        if m == at and j >= 4:
                            act.wait_ge(turned, L * N_TURN + j + 1)
                            fn((sbqT, sbkT, swqT, swkT)[j - 4][:], ps[:, 4 + j % 2, :].rearrange("p (c t) -> p c t", c=2),
                               ACT.Copy, scale=0.125 if j == 4 else 1.0).then_inc(turned_out, 1)
                    hi(L, h0 + m + AHEAD)
                    if m == 9:
                        c_norm()
                    if m == AT_POOLMIX + 1:
                        pool_high()
                    for b in range(NB):
                        if m == AT_IDX[b]:
                            relu_step(b)
                    if m == AT_SB[0]:
                        sb_softplus()
                    if m == AT_SB[1]:
                        sb_exp()
                    if m == AT_SB[2]:
                        sb_high()
                    for n, at in enumerate(AT_ATT):
                        if m == at + 4:
                            att_high(L, n)
                        if m == at + 1:
                            att_exp_step(L, n)
                        if m == at + 3:
                            att_pT(L, n)
                    if AT_MEM <= m < AT_MEM + 4:
                        memory_high(m - AT_MEM)
                    if AT_MEM + 4 <= m < AT_MEM + 6:
                        square(L, memn[:, m - AT_MEM - 4], f"mem_{m - AT_MEM - 4}")
                merged_high(0)
                merged_high(1)
                hi(L, h0 + M_OUT + AHEAD)
                merged_high(2)
                merged_high(3)
                for m in range(M_OUT + 1, M_OUT + SKEW):
                    hi(L, h0 + m + AHEAD)

            def memory(L):
                h0 = H_X

                def natural(dst, bank, name, blocks=(0, 1)):
                    act.wait_ge(rms_ready, L * NRQ + RQ[f"{name}_{blocks[-1]}"] + 1)
                    for blk in blocks:
                        t = fn(dst[:, blk, 0:BW], ps[:, bank + blk, 0:BW], ACT.Copy, scale=rs(f"{name}_{blk}"))
                    t.then_inc(nat_done, 1)

                group_done(L, h0 + 1)
                natural(nat[:, 0], 4, "mem")
                x_high(L, 2, 1)
                act.wait_ge(query0_done, L + 1)
                natural(nat[:, 1], 6, "pre2", (0,))
                pre_square(L, 2, 1)
                hi(L, h0 + 7)
                group_done(L, h0 + 3)
                natural(nat[:, 1], 6, "pre2", (1,))
                hi(L, h0 + 8)
                hi(L, h0 + 9)
                att_exp_step(L, 4)
                hi(L, h0 + 10)
                hi(L, h0 + 11)
                group_done(L, h0 + 5)
                natural(v_m, 4, "mem")
                att_high(L, 4)
                att_exp_step(L, 5)
                hi(L, h0 + 12)
                hi(L, h0 + 13)
                h3 = H_FFN2
                post_square(L, 2, h3 - 1, 0)
                att_high(L, 5)
                x_high(L, 3, 0)
                post_square(L, 2, h3 - 1, 1)
                pre_square(L, 3, 0)
                hi(L, h3 + 6)
                x_high(L, 3, 1)
                pre_square(L, 3, 1)
                hi(L, h3 + 7)

            with act.Fori(0, DEPTH) as L:
                fn(table[:], k_col(K_EPS), ACT.Copy)
                act.wait_ge(gain_in, 16 * (L + 1))
                for hf in range(2):
                    hi(L, hf)
                    x_high(L, 0, 0, (hf,))
                for h in range(2, SKEW):
                    hi(L, h)
                x_high(L, 0, 1)
                for h in range(SKEW, AHEAD):
                    hi(L, h)
                hi(L, AHEAD)
                for blk in range(NB):
                    pre_square(L, 0, blk)
                ffn(L, 0, H_FFN1, 0)
                act.wait_ge(params_in, 16 * N_PAR * (L + 1))
                between(L, 0, H_MIX)
                mixer(L)
                between(L, 1, H_X)
                memory(L)
                ffn(L, 1, H_FFN2, 3)
                post_square(L, 3, NH - 1, 0)
                post_square(L, 3, NH - 1, 1)
                act.wait_ge(squared, L * NRQ + NRQ)
                act.wait_ge(x_in[1], 16)

        @block.vector
        def _(dve):
            v = nc.vector
            dve.sem_inc(split_done, 2 * RAW)
            dve.wait_ge(const_in, 16)
            links = [0]

            def link(L, ins):
                links[0] += 1
                ins.then_inc(dve_link, 1)
                dve.wait_ge(dve_link, L * N_VLINK + links[0])

            def lo(L, h, it=0):
                if h >= NH:
                    return
                u, n = h // 2, HALF[h]
                dve.wait_ge(hi_done, L * NH + h + 1 + it * 8)
                v.tensor_tensor(wl[:, h % SPL, 0:n], raw[:, u % RAW, (h % 2) * n:(h % 2) * n + n],
                                wh[:, h % SPL, 0:n].bitcast(F32), ALU.subtract).then_inc(split_done, 1)

            def x_low(L, b, blk, parts=(0, 1)):
                gi = (0, 1, 2, 4)[b]
                for hf in parts:
                    dve.wait_ge(x_hi, L * 16 + b * 4 + 2 * blk + hf + 1)
                    for c in range(4):
                        k = 4 * hf + c
                        s = slice(blk * P, blk * P + P)
                        t = v.scalar_tensor_tensor(xl[:, k, s], ps[:, OUT_BANK[b - 1][blk] + hf, c * P:c * P + P],
                                                   gT[:, gi, k:k + 1], xh[:, k, s].bitcast(F32), ALU.mult, ALU.subtract)
                    t.then_inc(x_lo, 1)

            def post_gain(L, k, blk):
                if blk == 0:
                    dve.wait_ge(gbc_in, 16 * (L * 4 + k + 1))
                dve.wait_ge(squared, L * NRQ + RQ[f"post{k}_{blk}"] + 1)
                v.tensor_tensor(yg[:, blk], wide(OUT_BANK[k][blk]), gbc[:], ALU.mult).then_inc(gained, 1)

            def post_add(L, k, blk):
                dve.wait_ge(rms_ready, L * NRQ + RQ[f"post{k}_{blk}"] + 1)
                dve.wait_ge(gained, L * 8 + 2 * k + blk + 1)
                v.scalar_tensor_tensor(x[:, blk], yg[:, blk], rs(f"post{k}_{blk}"), x[:, blk], ALU.mult,
                                       ALU.add).then_inc(x_new, 1)

            def between(L, k, h0):
                post_gain(L, k, 0)
                post_add(L, k, 0)
                lo(L, h0 + 3)
                lo(L, h0 + 4)
                x_low(L, k + 1, 0)
                post_gain(L, k, 1)
                post_add(L, k, 1)
                lo(L, h0 + 5)
                lo(L, h0 + 6)
                x_low(L, k + 1, 1)
                if k == 1:
                    return
                lo(L, h0 + 7)

            def ffn(L, f, h0, b):
                E = (L * 2 + f) * NG

                def hidden(g, it=0):
                    dve.wait_ge(silu_done, E + g + 1 + it * 2)
                    if g >= 2 or not isinstance(it, int):
                        dve.wait_ge(act_turned, E + g - 1 + it * 2)
                    for blk in range(NB):
                        t = v.scalar_tensor_tensor(an[:, g % 2, blk], ps[:, 2 * (g % 2) + blk, FG:2 * FG],
                                                   rs(f"pre{b}_{blk}"), sg[:, g % 2, blk], ALU.mult, ALU.mult)
                    t.then_inc(act_done, 1)

                def low(g, it=0):
                    bank = 2 if g == NG - 1 else 4 + g % 2
                    dve.wait_ge(act_hi, E + g + 1 + it * 2)
                    k = 2 * g + 4 * it if not isinstance(it, int) else 2 * g
                    s = bass.ds(k, 2) if not isinstance(it, int) else slice(k, k + 2)
                    v.tensor_tensor(al[:, s, :], ps[:, bank, :].rearrange("p (c t) -> p c t", c=2),
                                    ah[:, s, :].bitcast(F32), ALU.subtract).then_inc(act_lo, 1)

                for i in (8, 9, 10):
                    lo(L, h0 + i)

                def group(g, it=0):
                    hidden(g - 1, it)
                    lo(L, h0 + 4 * g + AHEAD, it)
                    lo(L, h0 + 4 * g + 1 + AHEAD, it)
                    low(g - 1, it)
                    lo(L, h0 + 4 * g + 2 + AHEAD, it)
                    lo(L, h0 + 4 * g + 3 + AHEAD, it)
                group(1)
                group(2)
                with dve.Fori(0, (NG - 3) // 2) as it:
                    group(3, it)
                    group(4, it)
                hd = h0 + 4 * NG
                hidden(NG - 1)
                lo(L, hd + AHEAD)
                lo(L, hd + 1 + AHEAD)
                low(NG - 1)
                for c in range(2, FC - SKEW):
                    lo(L, hd + c + AHEAD)

            def turned_copy(L, j, dst, src):
                dve.wait_ge(turned, L * N_TURN + j + 1)
                if j == 3:
                    v.tensor_scalar(dst, src, kvn[:, 0:1], None, ALU.mult).then_inc(turned_out, 1)
                else:
                    v.tensor_copy(dst, src).then_inc(turned_out, 1)

            def att_mask(L, n):
                kind, b = ATT[n]
                W_ = P * (b + 1)
                dve.wait_ge(att_s, L * N_ATT + n + 1)
                if kind == "dsa":
                    dve.wait_ge(sel_done, L * 2 + 2)
                src = wide(S_BANK[n]).rearrange("p (h n) -> p h n", h=4)
                for k in range(b + 1):
                    s = slice(k * P, k * P + P)
                    if kind == "dsa":
                        m = dmask[:, b, s]
                    else:
                        m = cst[:, C_CAUS:C_CAUS + P] if k == b else cst[:, C_WIN:C_WIN + P]
                    t = v.scalar_tensor_tensor(sc[:, :, s], src[:, :, s], 0.125,
                                               m.unsqueeze(1).to_broadcast([P, 4, P]), ALU.mult, ALU.add)
                link(L, t)
                link(L, v.tensor_reduce(nmx[:, 0], sc[:, :, 0:W_], AX, ALU.max))
                if kind == "swa":
                    m = nmx[:, 0].rearrange("p (r c) -> p r c", r=2)
                    link(L, v.tensor_tensor(m, m, snk[:].rearrange("p (c r) -> p r c", r=2), ALU.max))
                v.tensor_scalar(nmx[:, 0], nmx[:, 0], -1.0, None, ALU.mult).then_inc(att_max, 1)

            def read_max(L, n):
                b = ATT[n][1]
                dve.wait_ge(att_s, L * N_ATT + n + 1)
                link(L, v.tensor_reduce(nmx[:, b], wide(S_BANK[n]).rearrange("p (h n) -> p h n", h=4), AX, ALU.max))
                v.tensor_scalar(nmx[:, b], nmx[:, b], -0.125, None, ALU.mult).then_inc(att_max, 1)

            def att_norm(L, n):
                kind, b = ATT[n]
                r = b if kind == "x" else 0
                W_ = TOK if kind == "x" else P * (b + 1)
                dve.wait_ge(att_exp, L * N_ATT + n + 1)
                if kind == "swa":
                    link(L, v.tensor_tensor(den[:, 0], den[:, 0], esk[:], ALU.add))
                link(L, v.reciprocal(rcp[:, r], den[:, r]))
                v.tensor_tensor(scores[n][:, :, 0:W_], scores[n][:, :, 0:W_],
                                rcp[:, r].unsqueeze(2).to_broadcast([P, 4, W_]), ALU.mult).then_inc(att_p, 1)

            def att_pT(L, n):
                dve.wait_ge(att_t, L * N_ATT + n + 1)
                v.tensor_copy(probsT[n][:], wide(T_BANK[n]).rearrange("p (h k n) -> p h k n", h=4, k=2)).then_inc(att_tev, 1)

            def att_low(L, n):
                kind, b = ATT[n]
                i = {"swa": 3, "dsa": 1, "x": 0}[kind]
                dve.wait_ge(br_hi, L * N_BR + BR[kind + str(b)] + 1)
                s = slice(b * P, b * P + P)
                v.tensor_tensor(brl[:, i, :, s], ps[:, O_BANK[n], 0:TOK].rearrange("p (c t) -> p c t", c=2),
                                brh[:, i, :, s].bitcast(F32), ALU.subtract).then_inc(br_lo, 1)

            def mixer(L):
                h0 = H_MIX

                def half_factors():
                    for blk in range(NB):
                        if blk == 0:
                            dve.wait_ge(rms_ready, L * NRQ + RQ["pre1_1"] + 1)
                        t = v.tensor_scalar(hrs[:, blk:blk + 1], rs(f"pre1_{blk}"), 0.5, None, ALU.mult)
                    t.then_inc(half_rms, 1)

                def index(b):
                    W_ = P * (b + 1)
                    dve.wait_ge(relu_done, L * 2 + b + 1)
                    if b == 1:
                        dve.wait_ge(sel_done, L * 2 + 1)
                    link(L, v.tensor_scalar(score[:, 0:W_], relu[:, 0, 0:W_], iw[:, b, 0:1], None, ALU.mult))
                    for s in range(1, 8):
                        h = s // 2 + 4 * (s % 2)
                        t = v.scalar_tensor_tensor(score[:, 0:W_], relu[:, s, 0:W_], iw[:, b, h:h + 1],
                                                   score[:, 0:W_], ALU.mult, ALU.add)
                        if s < 7:
                            link(L, t)
                    t.then_inc(idx_sum, 1)
                    dve.wait_ge(idx_sum, L * 2 + b + 1)
                    link(L, v.tensor_tensor(score[:, b * P:b * P + P], score[:, b * P:b * P + P],
                                            cst[:, C_CAUS:C_CAUS + P], ALU.add))

                def rounds(b, n):
                    W_ = P * (b + 1)
                    for _ in range(n):
                        v.memset(carry[:], 0.0)
                        link(L, v.max(top8[:], score[:, 0:W_]))
                        v.memset(carry[:], 0.0)
                        link(L, v.match_replace(score[:, 0:W_], top8[:], score[:, 0:W_], TAKEN))

                def chosen(b):
                    W_ = P * (b + 1)
                    link(L, v.tensor_scalar(dmask[:, b, 0:W_], score[:, 0:W_], TAKEN / 2, NEG, ALU.is_gt, ALU.mult))
                    v.tensor_tensor(dmask[:, b, b * P:b * P + P], dmask[:, b, b * P:b * P + P],
                                    cst[:, C_CAUS:C_CAUS + P], ALU.add).then_inc(sel_done, 1)

                def strict_mask(t):
                    m = cst[:, C_STRICT:C_STRICT + P].unsqueeze(1).to_broadcast([P, 4, P])
                    d0 = t[:, 0:1024].rearrange("p (h n) -> p h n", h=4)[:, :, 0:P]
                    d1 = t[:, 1024:1536].rearrange("p (h n) -> p h n", h=4)
                    v.tensor_tensor(d0, d0, m, ALU.mult)
                    return v.tensor_tensor(d1, d1, m, ALU.mult)

                def merge(n, hf):
                    dve.wait_ge(half_done, L * NH + h0 + M_GATES + 10 * n + 8 + hf + 1 + SPL)
                    dve.wait_ge(nat_done, L * N_NAT + 5 + 2 * n + hf + 1)
                    if 2 * (n - 1) + hf > 0:
                        dve.wait_ge(merge_done, L * N_MRG + (2 * (n - 1) + hf if n < 3 else 4 + 2 * hf))
                    s = slice(hf * 512, hf * 512 + 512)
                    for blk in range(NB):
                        dst = merged[:, blk, s] if n == 0 else tmp[:, blk]
                        t = v.scalar_tensor_tensor(dst, gate[:, hf, blk], 1.0, ps[:, G_BANK[hf] + blk, :], ALU.add,
                                                   ALU.mult)
                        if n == 3:
                            link(L, t)
                            v.tensor_tensor(merged[:, blk, s], merged[:, blk, s], tmp[:, blk], ALU.add)\
                                .then_inc(merge_done, 1)
                    if n < 3:
                        t.then_inc(y_out, 1)

                def memory_low(j):
                    dve.wait_ge(mem_hi, L * 4 + j + 1)
                    for c in range(4):
                        k, blk = 4 * (j % 2) + c, j // 2
                        s = slice(blk * P, blk * P + P)
                        t = v.scalar_tensor_tensor(meml[:, k, s], ps[:, 4 + j, c * P:c * P + P], gT[:, 3, k:k + 1],
                                                   memh[:, k, s].bitcast(F32), ALU.mult, ALU.subtract)
                    t.then_inc(mem_lo, 1)

                def merged_low(j):
                    dve.wait_ge(m_hi, L * 4 + j + 1)
                    k, s = 4 * (j // 2), slice((j % 2) * P, (j % 2) * P + P)
                    v.scalar_tensor_tensor(xl[:, k:k + 4, s], ps[:, 4 + j, :].rearrange("p (c t) -> p c t", c=4), 0.5,
                                           xh[:, k:k + 4, s].bitcast(F32), ALU.mult, ALU.subtract).then_inc(m_lo, 1)

                half_factors()
                for m in range(1, M_OUT):
                    if m > M_GATES and (m - M_GATES) % 10 in (0, 9):
                        merge((m - M_GATES - 9) // 10, 0 if (m - M_GATES) % 10 == 9 else 1)
                    if m == 10:
                        dve.wait_ge(nat_done, L * N_NAT + 2)
                        for b in range(NB):
                            link(L, v.tensor_scalar(iw[:, b], nat[:, 1, b, 416:424], 8.0 ** -0.5, None, ALU.mult))
                    for j, at in AT_T.items():
                        if m == at and j < 4:
                            dst = (dqT, iqT, ikT, cT)[j]
                            src = ps[:, 4 + j % 2, :]
                            if j in (2, 3):
                                turned_copy(L, j, dst[:], src[:, 0:TOK])
                            else:
                                turned_copy(L, j, dst[:], src.rearrange("p (c t) -> p c t", c=2))
                    if m == AT_POOLED:
                        dve.wait_ge(mix_pe, L * 3 + 1)
                        v.tensor_copy(poT[:], ps[:, 6, :].rearrange("p (c t) -> p c t", c=2)).then_inc(mix_out, 1)
                    if m == AT_POOLMIX + 1:
                        dve.wait_ge(br_hi, L * N_BR + BR["pool"] + 1)
                        for c in range(2):
                            t = v.scalar_tensor_tensor(brl[:, 0, c], ps[:, 7, c * TOK:c * TOK + TOK], psc[:, c:c + 1],
                                                       brh[:, 0, c].bitcast(F32), ALU.mult, ALU.subtract)
                        t.then_inc(br_lo, 1)
                    if m == AT_DKV:
                        dve.wait_ge(mix_pe, L * 3 + 3)
                        v.tensor_copy(dkT[:], ps[:, 4, :].rearrange("p (c t) -> p c t", c=2))
                        v.tensor_copy(v_ds[:], ps[:, 5, :].rearrange("p (c t) -> p c t", c=2)).then_inc(mix_out, 1)
                    for b in range(NB):
                        if m == AT_IDX[b]:
                            index(b)
                    if m == AT_SB[0] + 1:
                        dve.wait_ge(sb_act, L * 2 + 1)
                        v.scalar_tensor_tensor(sb_sp[:, 0:1024], wide(4), 0.0, sb_sp[:, 0:1024], ALU.max, ALU.add)
                        own = sb_sp[:, 1024:1536].rearrange("p (e n) -> p e n", e=2)
                        link(L, v.scalar_tensor_tensor(own, ps[:, 6:8, 0:TOK], 0.0, own, ALU.max, ALU.add))
                        strict_mask(sb_sp).then_inc(sb_dve, 1)
                    if m == AT_SB[1]:
                        dve.wait_ge(sb_act, L * 2 + 2)
                        strict_mask(sb_a).then_inc(sb_dve, 1)
                    if m == AT_SB[2]:
                        dve.wait_ge(br_hi, L * N_BR + BR["sb"] + 1)
                        v.tensor_tensor(brl[:, 2], ps[:, 4, :].rearrange("p (c t) -> p c t", c=2),
                                        brh[:, 2].bitcast(F32), ALU.subtract).then_inc(br_lo, 1)
                    for n, at in enumerate(AT_ATT):
                        if m == at + 4:
                            att_low(L, n)
                        if m == at:
                            att_mask(L, n)
                        if m == at + 2:
                            att_norm(L, n)
                    if m < M_OUT - 2:
                        lo(L, h0 + m + AHEAD)
                    for b in range(NB):
                        if m in ROUNDS[b]:
                            rounds(b, ROUNDS[b][m])
                        if m == max(ROUNDS[b]):
                            chosen(b)
                    if AT_MEM <= m < AT_MEM + 4:
                        memory_low(m - AT_MEM)
                merged_low(0)
                merge(3, 1)
                merged_low(1)
                lo(L, h0 + M_OUT - 2 + AHEAD)
                lo(L, h0 + M_OUT - 1 + AHEAD)
                lo(L, h0 + M_OUT + AHEAD)
                merged_low(2)
                merged_low(3)
                for m in range(M_OUT + 1, M_OUT + SKEW):
                    lo(L, h0 + m + AHEAD)

            def memory(L):
                h0 = H_X
                turned_copy(L, 8, mkT[:], ps[:, 0, :].rearrange("p (c t) -> p c t", c=2))
                turned_copy(L, 9, xqT[:, :, 0:P], ps[:, 1, :].rearrange("p (c t) -> p c t", c=2)[:, :, 0:P])
                lo(L, h0 + 7)
                lo(L, h0 + 8)
                read_max(L, 4)
                turned_copy(L, 10, xqT[:, :, P:TOK], ps[:, 1, :].rearrange("p (c t) -> p c t", c=2)[:, :, P:TOK])
                lo(L, h0 + 9)
                att_norm(L, 4)
                att_pT(L, 4)
                read_max(L, 5)
                att_low(L, 4)
                lo(L, h0 + 10)
                att_norm(L, 5)
                att_pT(L, 5)
                post_gain(L, 2, 0)
                att_low(L, 5)
                post_add(L, 2, 0)
                lo(L, h0 + 11)
                lo(L, h0 + 12)
                x_low(L, 3, 0)
                post_gain(L, 2, 1)
                post_add(L, 2, 1)
                lo(L, h0 + 13)
                x_low(L, 3, 1)
                lo(L, h0 + 14)
                lo(L, h0 + 15)

            with dve.Fori(0, DEPTH) as L:
                dve.wait_ge(gain_in, 16 * (L + 1))
                for hf in range(2):
                    lo(L, hf)
                    x_low(L, 0, 0, (hf,))
                for h in range(2, SKEW):
                    lo(L, h)
                x_low(L, 0, 1)
                for h in range(SKEW, AHEAD):
                    lo(L, h)
                lo(L, AHEAD)
                ffn(L, 0, H_FFN1, 0)
                dve.wait_ge(params_in, 16 * N_PAR * (L + 1))
                dve.wait_ge(masks_in, 16 * (L + 1))
                between(L, 0, H_MIX)
                mixer(L)
                between(L, 1, H_X)
                memory(L)
                ffn(L, 1, H_FFN2, 3)
                for blk in range(NB):
                    post_gain(L, 3, blk)
                    post_add(L, 3, blk)
            assert links[0] == N_VLINK, links[0]


_INS = ("x", "mem", "ffn1_pre", "ffn1_w_up", "ffn1_w_down", "ffn1_post", "mix_pre", "w_in", "pool_w", "pool_scale",
        "dsa_kv_norm", "dsa_w_uk", "dsa_w_uv", "swa_sinks", "w_branch", "w_out", "mix_post", "xattn_pre", "mem_norm",
        "xattn_w_q", "xattn_w_kv", "xattn_w_o", "xattn_post", "ffn2_pre", "ffn2_w_up", "ffn2_w_down", "ffn2_post")


def kernel(**inputs):
    import numpy as _np
    import concourse.bacc as _bacc
    from concourse import mybir as _mybir
    from concourse.bass_utils import run_bass_kernel_spmd as _run

    nc = _bacc.Bacc("TRN2", target_bir_lowering=False, num_devices=1)
    arrays, args = {}, {}
    for name in _INS + ("consts",):
        a = constants() if name == "consts" else _np.ascontiguousarray(inputs[name])
        arrays[f"in_{name}"] = a
        args[name] = nc.dram_tensor(f"in_{name}", a.shape, _mybir.dt.from_np(a.dtype), kind="ExternalInput").ap()
    out = nc.dram_tensor("out_x", (1, TOK, D), F32, kind="ExternalOutput").ap()
    trunk(nc, args, out)
    r = _run(nc, [arrays], core_ids=[0])
    return r.results[0]["out_x"]
```
